# Optimizing a Trainium2 kernel written in Bass

```python
import jax, jax.numpy as jnp
from jax import lax
import numpy as np

D_MODEL = 1024
BATCH = 1
SEQ = 512
DEPTH = 1

HEAD_DIM = 64
DSA_HEADS = 8
DSA_LATENT = 128
IDX_HEADS = 8
IDX_DIM = 32
DSA_TOPK_MAX = 256
NSA_HEADS = 8
NSA_KV_HEADS = 2
NSA_GROUP = NSA_HEADS // NSA_KV_HEADS
CMP_LEN = 32
CMP_STRIDE = 16
CMP_HIDDEN = 128
SLC_LEN = 64
SLC_TOPN = 16
WINDOW = 512
FORCE_BONUS = 1e6
Q_BLOCK = 128
D_FF = 4 * D_MODEL
RMS_EPS = 1e-6
NEG_INF = -1e30

WIDTH_A = DSA_HEADS * HEAD_DIM
WIDTH_B = NSA_HEADS * HEAD_DIM
NSA_KV_W = NSA_KV_HEADS * HEAD_DIM
COL_SIZES = (WIDTH_A, DSA_LATENT, IDX_HEADS * IDX_DIM, IDX_DIM, IDX_HEADS,
             WIDTH_B, 6 * NSA_KV_W, 3 * NSA_HEADS, 2 * D_MODEL)
D_IN = WIDTH_A + DSA_LATENT + IDX_HEADS * IDX_DIM + IDX_DIM + IDX_HEADS + WIDTH_B + 6 * NSA_KV_W + 3 * NSA_HEADS + 2 * D_MODEL

kernel_name = "hybrid_dsa_nsa_gated_block"

def rms_norm(x, g):
    xf = x.astype(jnp.float32)
    y = xf * lax.rsqrt(jnp.mean(xf * xf, axis=-1, keepdims=True) + RMS_EPS)
    return (y * g.astype(jnp.float32)).astype(x.dtype)

def alibi_slopes(n_heads):
    return jnp.asarray(2.0 ** (-8.0 * np.arange(1, n_heads + 1) / n_heads), dtype=jnp.float32)

def masked_softmax(s, valid):
    p = jax.nn.softmax(jnp.where(valid, s, NEG_INF), axis=-1)
    return jnp.where(valid, p, 0.0)

def split_cols(a, sizes):
    out, start = [], 0
    for n in sizes:
        out.append(a[..., start:start + n])
        start += n
    return out

def to_blocks(a, nb):
    return a.reshape((a.shape[0], nb, Q_BLOCK) + a.shape[2:]).swapaxes(0, 1)

def from_blocks(a):
    a = a.swapaxes(0, 1)
    return a.reshape((a.shape[0], a.shape[1] * a.shape[2]) + a.shape[3:])

def dsa_mixer(q, c_kv, q_idx, k_idx, w_idx, g_q, g_k, g_lat, w_uk, w_uv):
    B, S = q.shape[0], q.shape[1]
    nb = S // Q_BLOCK
    topk = min(DSA_TOPK_MAX, S // 4)
    c = rms_norm(c_kv, g_lat)
    k = rms_norm(c @ w_uk, g_k)
    v = c @ w_uv
    q = rms_norm(q, g_q)
    w_idx = w_idx * (IDX_HEADS ** -0.5 * IDX_DIM ** -0.5)
    slopes = alibi_slopes(DSA_HEADS)
    bi = jnp.arange(B)[:, None, None]
    s_pos = jnp.arange(S)

    def block(args):
        qb, qib, wb, start = args
        t = start + jnp.arange(Q_BLOCK)
        logits = jnp.einsum('bthd,bsd->bths', qib, k_idx).astype(jnp.float32)
        score = jnp.einsum('bths,bth->bts', jax.nn.relu(logits), wb.astype(jnp.float32))
        score = jnp.where((s_pos[None, :] <= t[:, None])[None], score, -jnp.inf)
        _, idx = lax.top_k(score, topk)
        ks = k[bi, idx]
        vs = v[bi, idx]
        dist = (t[None, :, None] - idx).astype(jnp.float32)
        s = jnp.einsum('bthd,btkd->bthk', qb, ks).astype(jnp.float32) * (HEAD_DIM ** -0.5)
        s = s - slopes[None, None, :, None] * dist[:, :, None, :]
        p = masked_softmax(s, (dist >= 0)[:, :, None, :])
        return jnp.einsum('bthk,btkd->bthd', p.astype(vs.dtype), vs)

    starts = jnp.arange(nb, dtype=jnp.int32) * Q_BLOCK
    out = lax.map(block, (to_blocks(q, nb), to_blocks(q_idx, nb), to_blocks(w_idx, nb), starts))
    return from_blocks(out).reshape(B, S, WIDTH_A)

def nsa_mixer(q, kv, gates, g_q, g_kc, g_ks, g_kw, pe_cmp, phi_k1, phi_k2, phi_v1, phi_v2):
    B, S = q.shape[0], q.shape[1]
    KH, G, dh = NSA_KV_HEADS, NSA_GROUP, HEAD_DIM
    nb = S // Q_BLOCK
    scale = dh ** -0.5
    q = rms_norm(q.reshape(B, S, KH, G, dh), g_q)
    k_c, v_c, k_s, v_s, k_w, v_w = [a.reshape(B, S, KH, dh) for a in split_cols(kv, (NSA_KV_W,) * 6)]
    k_s = rms_norm(k_s, g_ks)
    k_w = rms_norm(k_w, g_kw)
    slopes = alibi_slopes(NSA_HEADS).reshape(KH, G)
    pos = jnp.arange(S)

    n_cmp = (S - CMP_LEN) // CMP_STRIDE + 1
    cmp_start = jnp.arange(n_cmp) * CMP_STRIDE
    blk_pos = cmp_start[:, None] + jnp.arange(CMP_LEN)[None, :]

    def compress(a, w1, w2):
        blocks = a[:, blk_pos] + pe_cmp[None, None, :, None, :]
        blocks = blocks.transpose(0, 1, 3, 2, 4).reshape(B, n_cmp, KH, CMP_LEN * dh)
        return jax.nn.gelu(blocks @ w1) @ w2

    kc = rms_norm(compress(k_c, phi_k1, phi_k2), g_kc)
    vc = compress(v_c, phi_v1, phi_v2)
    valid_c = (cmp_start + CMP_LEN - 1)[None, :] <= pos[:, None]
    s_c = jnp.einsum('bsgqd,bcgd->bsgqc', q, kc).astype(jnp.float32) * scale
    p_c = masked_softmax(s_c, valid_c[None, :, None, None, :])
    o_cmp = jnp.einsum('bsgqc,bcgd->bsgqd', p_c.astype(vc.dtype), vc)

    n_slc = S // SLC_LEN
    slc_start = jnp.arange(n_slc) * SLC_LEN
    overlap = ((cmp_start[:, None] < slc_start[None, :] + SLC_LEN)
               & (cmp_start[:, None] + CMP_LEN > slc_start[None, :])).astype(jnp.float32)
    imp = jnp.einsum('bsgqc,cj->bsgj', p_c, overlap)
    cur = pos // SLC_LEN
    blk = jnp.arange(n_slc)
    future = blk[None, :] > cur[:, None]
    forced = (blk[None, :] == 0) | (blk[None, :] == cur[:, None]) | (blk[None, :] == cur[:, None] - 1)
    imp = jnp.where(future[None, :, None, :], -jnp.inf,
                    imp + jnp.where(forced, FORCE_BONUS, 0.0)[None, :, None, :])
    n_top = min(SLC_TOPN, n_slc)
    _, sel = lax.top_k(imp, n_top)

    kb = k_s.reshape(B, n_slc, SLC_LEN, KH, dh).transpose(0, 3, 1, 2, 4)
    vb = v_s.reshape(B, n_slc, SLC_LEN, KH, dh).transpose(0, 3, 1, 2, 4)
    kw_pad = jnp.pad(k_w, ((0, 0), (WINDOW, 0), (0, 0), (0, 0)))
    vw_pad = jnp.pad(v_w, ((0, 0), (WINDOW, 0), (0, 0), (0, 0)))
    bi = jnp.arange(B)[:, None, None, None]
    gi = jnp.arange(KH)[None, None, :, None]
    win_len = WINDOW + Q_BLOCK

    def block(args):
        qb, selb, start = args
        t = start + jnp.arange(Q_BLOCK)
        ks = kb[bi, gi, selb]
        vs = vb[bi, gi, selb]
        kpos = selb[..., None] * SLC_LEN + jnp.arange(SLC_LEN)
        dist = (t[None, :, None, None, None] - kpos).astype(jnp.float32)
        s = jnp.einsum('btgqd,btgnld->btgqnl', qb, ks).astype(jnp.float32) * scale
        s = s - slopes[None, None, :, :, None, None] * dist[:, :, :, None]
        s = s.reshape(B, Q_BLOCK, KH, G, n_top * SLC_LEN)
        valid = (dist >= 0).reshape(B, Q_BLOCK, KH, 1, n_top * SLC_LEN)
        p = masked_softmax(s, valid).reshape(B, Q_BLOCK, KH, G, n_top, SLC_LEN)
        o_slc = jnp.einsum('btgqnl,btgnld->btgqd', p.astype(vs.dtype), vs)
        kw = lax.dynamic_slice_in_dim(kw_pad, start, win_len, axis=1)
        vw = lax.dynamic_slice_in_dim(vw_pad, start, win_len, axis=1)
        wpos = start - WINDOW + jnp.arange(win_len)
        wd = t[:, None] - wpos[None, :]
        wvalid = (wd >= 0) & (wd < WINDOW) & (wpos[None, :] >= 0)
        s_w = jnp.einsum('btgqd,bsgd->btgqs', qb, kw).astype(jnp.float32) * scale
        s_w = s_w - slopes[None, None, :, :, None] * wd.astype(jnp.float32)[None, :, None, None, :]
        p_w = masked_softmax(s_w, wvalid[None, :, None, None, :])
        o_win = jnp.einsum('btgqs,bsgd->btgqd', p_w.astype(vw.dtype), vw)
        return o_slc, o_win

    starts = jnp.arange(nb, dtype=jnp.int32) * Q_BLOCK
    o_slc, o_win = lax.map(block, (to_blocks(q, nb), to_blocks(sel, nb), starts))
    o_slc = from_blocks(o_slc)
    o_win = from_blocks(o_win)
    g = jax.nn.sigmoid(gates.reshape(B, S, KH, G, 3))
    o = g[..., 0:1] * o_cmp + g[..., 1:2] * o_slc + g[..., 2:3] * o_win
    return o.reshape(B, S, WIDTH_B)

def setup_inputs(seed: int = 0) -> dict:
    key = jax.random.key(seed)
    ks = jax.random.split(key, 24)
    f32 = jnp.float32
    L, dh = DEPTH, HEAD_DIM

    def nrm(k, shape, scale):
        return jax.random.normal(k, shape, f32) * scale

    def gain(k, n):
        return 1.0 + 0.05 * jax.random.normal(k, (DEPTH, n), f32)

    return {
        "x": nrm(ks[0], (BATCH, SEQ, D_MODEL), 1.0),
        "g_mix": gain(ks[1], D_MODEL),
        "w_in": nrm(ks[2], (L, D_MODEL, D_IN), D_MODEL ** -0.5),
        "g_q_a": gain(ks[3], dh),
        "g_k_a": gain(ks[4], dh),
        "g_lat_a": gain(ks[5], DSA_LATENT),
        "w_uk_a": nrm(ks[6], (L, DSA_LATENT, dh), DSA_LATENT ** -0.5),
        "w_uv_a": nrm(ks[7], (L, DSA_LATENT, dh), DSA_LATENT ** -0.5),
        "g_q_b": gain(ks[8], dh),
        "g_kc_b": gain(ks[9], dh),
        "g_ks_b": gain(ks[10], dh),
        "g_kw_b": gain(ks[11], dh),
        "pe_cmp_b": nrm(ks[12], (L, CMP_LEN, dh), 0.1),
        "phi_k1_b": nrm(ks[13], (L, CMP_LEN * dh, CMP_HIDDEN), (CMP_LEN * dh) ** -0.5),
        "phi_k2_b": nrm(ks[14], (L, CMP_HIDDEN, dh), CMP_HIDDEN ** -0.5),
        "phi_v1_b": nrm(ks[15], (L, CMP_LEN * dh, CMP_HIDDEN), (CMP_LEN * dh) ** -0.5),
        "phi_v2_b": nrm(ks[16], (L, CMP_HIDDEN, dh), CMP_HIDDEN ** -0.5),
        "w_up_a": nrm(ks[17], (L, WIDTH_A, D_MODEL), WIDTH_A ** -0.5),
        "w_up_b": nrm(ks[18], (L, WIDTH_B, D_MODEL), WIDTH_B ** -0.5),
        "w_out": nrm(ks[19], (L, D_MODEL, D_MODEL), D_MODEL ** -0.5),
        "g_mlp": gain(ks[20], D_MODEL),
        "w_ff1": nrm(ks[21], (L, D_MODEL, D_FF), D_MODEL ** -0.5),
        "w_ff2": nrm(ks[22], (L, D_FF, D_MODEL), D_FF ** -0.5),
    }

def reference(x, g_mix, w_in, g_q_a, g_k_a, g_lat_a, w_uk_a, w_uv_a, g_q_b, g_kc_b, g_ks_b, g_kw_b,
              pe_cmp_b, phi_k1_b, phi_k2_b, phi_v1_b, phi_v2_b, w_up_a, w_up_b, w_out, g_mlp, w_ff1, w_ff2):
    B, S = x.shape[0], x.shape[1]
    for l in range(DEPTH):
        h = rms_norm(x, g_mix[l])
        proj = h @ w_in[l]
        q_a, c_a, qi_a, ki_a, wi_a, q_b, kv_b, gate_b, gate_m = split_cols(proj, COL_SIZES)
        o_a = dsa_mixer(q_a.reshape(B, S, DSA_HEADS, HEAD_DIM), c_a,
                        qi_a.reshape(B, S, IDX_HEADS, IDX_DIM), ki_a, wi_a,
                        g_q_a[l], g_k_a[l], g_lat_a[l], w_uk_a[l], w_uv_a[l])
        o_b = nsa_mixer(q_b, kv_b, gate_b, g_q_b[l], g_kc_b[l], g_ks_b[l], g_kw_b[l],
                        pe_cmp_b[l], phi_k1_b[l], phi_k2_b[l], phi_v1_b[l], phi_v2_b[l])
        gate_a_m, gate_b_m = split_cols(gate_m, (D_MODEL, D_MODEL))
        merged = jax.nn.sigmoid(gate_a_m) * (o_a @ w_up_a[l]) + jax.nn.sigmoid(gate_b_m) * (o_b @ w_up_b[l])
        x = x + merged @ w_out[l]
        h2 = rms_norm(x, g_mlp[l])
        x = x + jnp.square(jax.nn.relu(h2 @ w_ff1[l])) @ w_ff2[l]
    return x


_drawn_inputs = setup_inputs


def setup_inputs(seed=0):
    import zlib

    import numpy as np

    out = dict(_drawn_inputs(seed))
    spreads = {}
    factors = {'g_q_a': 5.941,
     'g_k_a': 7.701,
     'g_lat_a': 3.301,
     'g_q_b': 8.0,
     'g_kc_b': 23.464,
     'g_ks_b': 8.0,
     'g_kw_b': 8.0,
     'pe_cmp_b': 3.113}
    for name, (base, spread) in spreads.items():
        noise = np.random.default_rng([zlib.crc32(name.encode()), seed]).standard_normal(out[name].shape)
        drawn = base * np.exp(spread * noise) if base else spread * noise
        out[name] = __import__('jax').numpy.asarray(drawn.astype(out[name].dtype))
    for name, factor in factors.items():
        out[name] = (out[name] * factor).astype(out[name].dtype)
    return out
```

```python
from contextlib import ExitStack

import concourse.bass as bass
from concourse import mybir

F32 = mybir.dt.float32
F32R = mybir.dt.float32r
ALU = mybir.AluOpType
ACT = mybir.ActivationFunctionType
AX = mybir.AxisListType

P = 128
BANK = 512
SLC_LEN, SLC_TOPN, WINDOW, TOPK_MAX = 64, 16, 512, 256
CMP_LEN, CMP_STRIDE = 32, 16
EPS = 1e-6
MASKED = 1e33
FUTURE = -3.0e38
TAKEN = -3.4e38
GELU_IN, GELU_CUBE = 0.7978845608028654, 0.044715


class Banks:

    def __init__(self):
        self.uses = [0] * 8
        self.at = {}

    def use(self, key, bank):
        self.uses[bank] += 1
        self.at[key] = (bank, self.uses[bank])

    def __getitem__(self, key):
        return self.at[key]


def hybrid_layer(nc, x, g_mix, w_in, g_q_a, g_k_a, g_lat_a, w_uk_a, w_uv_a, g_q_b, g_kc_b, g_ks_b, g_kw_b,
                 pe_cmp_b, phi_k1_b, phi_k2_b, phi_v1_b, phi_v2_b, w_up_a, w_up_b, w_out, g_mlp, w_ff1, w_ff2,
                 out):
    _, S, D = x.shape
    DH = g_q_a.shape[1]
    LAT = g_lat_a.shape[1]
    WA, WB = w_up_a.shape[1], w_up_b.shape[1]
    H = WA // DH
    KH = 2
    G = H // KH
    IH, ID = 8, 32
    FF = w_ff1.shape[2]
    HID = phi_k1_b.shape[2]
    TT = S // P
    KT = D // P
    NCMP = (S - CMP_LEN) // CMP_STRIDE + 1
    CP = NCMP + 1
    TOPK = min(TOPK_MAX, S // 4)
    assert S == BANK and KT == 8 and TT == 4 and H == 8 and DH == 64 and LAT == P and HID == P and CP == 32
    assert min(SLC_TOPN, S // SLC_LEN) == S // SLC_LEN and WINDOW >= S and TOPK == P and WA == WB == 4 * P
    KVW = KH * DH

    Q_A = 0
    IDX = WA
    Q_B = IDX + LAT + IH * ID + ID + IH
    KV = Q_B + WB
    GATE_M = KV + 6 * KVW + 3 * H
    C_IDX, C_KV1, C_KV2, C_QB, C_QA = range(5)
    PROJ = [(IDX, Q_B - IDX), (KV, 3 * KVW), (KV + 3 * KVW, 3 * KVW + 3 * H), (Q_B, WB), (Q_A, WA)]

    def ktiles(w, n=None):
        return w.rearrange("(k p) n -> p k n", p=P)

    w_in_k, w_ff1_k, w_ff2_k = ktiles(w_in[0]), ktiles(w_ff1[0]), ktiles(w_ff2[0])
    w_out_k, up_k = ktiles(w_out[0]), [ktiles(w_up_a[0]), ktiles(w_up_b[0])]

    panels = []
    for c0, n in PROJ:
        panels += [(w_in_k[:, 4 * hf:4 * hf + 4, c0:c0 + n], 4, n) for hf in range(2)]
    GATE0 = len(panels)
    for n in range(2):
        for m in range(2):
            c0 = GATE_M + m * D + n * BANK
            panels += [(w_in_k[:, 4 * hf:4 * hf + 4, c0:c0 + BANK], 4, BANK) for hf in range(2)]
            panels += [(up_k[m][:, :, n * BANK:(n + 1) * BANK], 4, BANK)]
    OUT0 = len(panels)
    for n in range(2):
        panels += [(w_out_k[:, 4 * hf:4 * hf + 4, n * BANK:(n + 1) * BANK], 4, BANK) for hf in range(2)]
    FF1 = len(panels)
    NFF1 = 2 * FF // BANK
    FF2 = FF1 + NFF1
    NFF2 = FF // P // 2
    assert FF1 % 2 == 0 and NFF1 % 4 == 0 and NFF2 % 2 == 0

    SLC, WIN, DSA = range(3)
    units = [(br, tt, h) for br in (SLC, WIN, DSA) for tt in range(TT) for h in range(H)]
    NU = len(units)
    T_LAG, PV_LAG = 2, 4
    STEPS = NU + PV_LAG + 2
    CMP_STEP = H * TT + PV_LAG + 1
    NSA_DONE = 2 * H * TT - 1 + PV_LAG

    bank = Banks()
    bank.use("gains", 0)
    for tt in range(TT):
        for hf in range(2):
            bank.use(("hT", tt, hf), 2 * tt + hf)

    def use_set(prefix, s, count=4):
        for i in range(count):
            bank.use((*prefix, i), 4 * s + i % 4)

    use_set(("proj", C_IDX), 0)
    use_set(("proj", C_KV1), 1)
    use_set(("T_idx",), 0)
    use_set(("proj", C_KV2), 0)
    INDEX_UNITS = [(tt, h) for tt in range(1, TT) for h in range(IH)]
    use_set(("kv_a",), 1, 1)
    for i in range(4):
        bank.use(("cmpT", i), 4 + (1 + i) % 4)
    for g in range(KH):
        bank.use(("ksT", g), 4 + (5 + g) % 4)
    for u in range(len(INDEX_UNITS)):
        bank.use(("index", u), 4 + (7 + u) % 4)
    use_set(("proj", C_QB), 1)
    bank.use("kaT", 0)
    for g in range(KH):
        bank.use(("kwT", g), 1 + g)
    for t in range(2):
        bank.use(("hidden", t), (3 + t) % 4)
    use_set(("proj", C_QA), 0)
    for i in range(4):
        bank.use(("qbT", i), 4 + i)
    bank.use("kc", 4)
    bank.use("vc", 5)
    bank.use("kcT", 6)
    for i in range(4):
        bank.use(("qaT", i), i)
    for i in range(4):
        bank.use(("cmpS", i), 4 + i)
    score_ring, pt_ring = (2, 3, 4), (5, 6, 7)
    ring_at = 0

    def use_ring(key):
        nonlocal ring_at
        bank.use(key, score_ring[ring_at % 3])
        ring_at += 1

    for s in range(STEPS):
        if s < NU:
            use_ring(("S", s))
        if s == CMP_STEP:
            for g in range(KH):
                use_ring(("cmpPT", g))
            for tt in range(TT):
                use_ring(("cmpO", tt))
        if T_LAG <= s < NU + T_LAG:
            bank.use(("PT", s - T_LAG), pt_ring[(s - T_LAG) % 3])
        if PV_LAG <= s < NU + PV_LAG and (s - PV_LAG) % H == 0:
            bank.use(("O", (s - PV_LAG) // H), (s - PV_LAG) // H % 2)
        if s == NSA_DONE + 2:
            for tt in range(TT):
                use_ring(("oT", 1, tt))
    for tt in range(TT):
        use_ring(("oT", 0, tt))
    for n in range(2):
        for m in range(2):
            use_set(("gate", n, m), 0)
            use_set(("up", n, m), 1)
    for n in range(2):
        use_set(("out", n), n)
    for tt in range(TT):
        for hf in range(2):
            bank.use(("h2T", tt, hf), 2 * (tt % 2) + hf)
    ff1_first = []
    for b in range(8):
        bank.use(("ff1", b), b)
        ff1_first.append(bank[("ff1", b)][1])
        for _ in range(FF // P // 8 - 1):
            bank.use(("ff1 later", b), b)
    for b in range(8):
        bank.use(("y", b), b)

    released = {}
    halves = 0
    for c in range(5):
        halves += 1
        released[2 * c], released[2 * c + 1] = ("half", halves), ("full", ("proj", c, 3))
    for n in range(2):
        for m in range(2):
            p = GATE0 + 3 * (2 * n + m)
            halves += 1
            released[p], released[p + 1] = ("half", halves), ("full", ("gate", n, m, 3))
            released[p + 2] = ("full", ("up", n, m, 3))
    for n in range(2):
        halves += 1
        released[OUT0 + 2 * n], released[OUT0 + 2 * n + 1] = ("half", halves), ("full", ("out", n, 3))
    HALVES_FF1 = halves

    with ExitStack() as ctx:
        def sem(name):
            return ctx.enter_context(nc.semaphore(name))

        psum = ctx.enter_context(nc.psum_tensor("psum", [P, 8, BANK], F32))
        base = (nc.sbuf_base + 511) // 512 * 512
        names = set()

        def place(name, shape, at, dt=F32):
            assert name not in names
            names.add(name)
            return nc.alloc_sbuf_tensor_at(name, shape, dt, offset=base + at)

        K = 1024
        stage = place("stage", [P, 2, 2048], 0)
        w_hi = place("w_hi", [P, 2, 2048], 16 * K, F32R)
        w_lo = place("w_lo", [P, 2, 2048], 32 * K, F32R)
        hT_hi = place("hT_hi", [P, KT, S], 48 * K, F32R)
        hT_lo = place("hT_lo", [P, KT, S], 64 * K, F32R)
        small = 80 * K

        def place_small(name, shape):
            nonlocal small
            n = 4
            for d in shape[1:]:
                n *= d
            t = place(name, shape, small)
            small += (n + 31) // 32 * 32
            return t

        R_GMIX, R_GMLP, R_LAT = 0, KT, 2 * KT
        R_QA, R_KA, R_QB, R_KS, R_KW, R_KC = range(2 * KT + 1, 2 * KT + 7)
        R_PE = 2 * KT + 7
        NG = R_PE + CMP_LEN // 2
        ident = place_small("ident", [P, P])
        gain_rows = place_small("gain_rows", [NG, P])
        gains = place_small("gains", [P, NG])
        dist = place_small("dist", [P, S])
        q_scale = place_small("q_scale", [P, H])
        cmp_scale = place_small("cmp_scale", [P, H * CP])
        cmp_valid = place_small("cmp_valid", [P, TT, CP])
        cmp_mask = place_small("cmp_mask", [P, TT, CP])
        neg_half = place_small("neg_half", [P, H * TT])
        xss = place_small("xss", [P, 2 * TT])
        xvar = place_small("xvar", [P, 2 * TT])
        xrstd = place_small("xrstd", [P, 2 * TT])
        NORMS = {}
        at = 0
        for name, n in (("c", TT), ("ks", TT * KH), ("ka", TT), ("kw", TT * KH), ("qb", TT * H), ("kc", 1),
                        ("qa", TT * H)):
            NORMS[name] = (len(NORMS) + 1, slice(at, at + n))
            at += n
        nss = place_small("nss", [P, at])
        nvar = place_small("nvar", [P, at])
        nrstd = place_small("nrstd", [P, at])
        wi = place_small("wi", [P, TT, IH])
        top8 = place_small("top8", [P, 8])
        neg_max = place_small("neg_max", [P, 4])
        row_sum = place_small("row_sum", [P, 3 * TT * H])
        row_inv = place_small("row_inv", [P, 3 * TT * H])
        gate_b = place_small("gate_b", [P, TT, 3 * H])
        cmp_max = place_small("cmp_max", [P, TT * H])
        cmp_sum = place_small("cmp_sum", [P, TT * H])
        kc = place_small("kc", [CP * KH, DH])
        kcT = place_small("kcT", [P, KH * CP])
        hid = place_small("hid", [P, 2, KH, NCMP])
        gel = place_small("gel", [P, 2, KH, NCMP])
        gel_k = place_small("gel_k", [P, KH, CP])
        phi2 = place_small("phi2", [P, 2, DH])
        w_ukv = place_small("w_ukv", [P, 2, DH])
        small = (small + 511) // 512 * 512
        hf = place("hf", [P, 2, BANK], small)
        Z = small + 4 * K
        xs = place("xs", [P, TT, D], Z + 76 * K)
        xt = place("xt", [P, TT, D], Z + 92 * K)
        p_idx = place("p_idx", [P, TT, PROJ[C_IDX][1]], Z)
        p_kv1 = place("p_kv1", [P, TT, PROJ[C_KV1][1]], Z + 7 * K)
        cmp_in = place("cmp_in", [P, 2, 2, KH, S // 2], Z + 16 * K)
        qbT = place("qbT", [P, H // 2, S], Z + 24 * K)
        p_kv2 = place("p_kv2", [P, TT, PROJ[C_KV2][1]], Z + 32 * K)
        p_q = place("p_q", [P, TT, H * DH], Z + 39 * K)
        cmp_dup = place("cmp_dup", [P, 2, TT, KH, 2, DH], Z + 47 * K)
        ks_dup = place("ks_dup", [P, TT, KH, 2, DH], Z + 55 * K)
        kw_dup = place("kw_dup", [P, TT, KH, 2, DH], Z + 59 * K)
        ka_dup = place("ka_dup", [P, TT, 2, DH], Z + 63 * K)
        ki_dup = place("ki_dup", [P, TT, G, ID], Z + 65 * K)
        qaT = place("qaT", [P, H // 2, S], Z + 67 * K)
        kaT = place("kaT", [P, S], Z + 75 * K)
        ksT = place("ksT", [P, KH, S], Z + 77 * K)
        kwT = place("kwT", [P, KH, S], Z + 81 * K)
        kv_a = place("kv_a", [P, TT, 2 * DH], Z + 85 * K)
        o_b = place("o_b", [P, TT, H * DH], Z + 87 * K)
        cT = place("cT", [P, S], Z + 89 * K)
        score_at = [None, 0, 2 * P, 5 * P]
        score = place("score", [P, 9 * P], Z + 95 * K)
        prob = place("prob", [P, 3, S], Z + 100 * K)
        probT = place("probT", [P, 3, S], Z + 106 * K)
        square = place("square", [P, TT * H * DH], Z + 100 * K)
        relu = place("relu", [P, 2, S], Z + 108 * K)
        o_a = place("o_a", [P, TT, H * DH], Z + 39 * K)
        cmp_e = place("cmp_e", [P, TT, H, CP], Z + 47 * K)
        cmp_pT = place("cmp_pT", [P, KH, S], Z + 51 * K)
        phi1 = [place(f"phi1_{i}", [P, CMP_LEN // 2, HID], Z + at * K) for i, at in ((0, 67), (1, 39))]
        qiT = place("qiT", [P, 2, S], Z + 91 * K)
        kiT = place("kiT", [P, S], Z + 87 * K)
        vc_diag = place("vc_diag", [P, KH, G, DH], Z + 13 * K)
        gel_v = place("gel_v", [P, KH, G, CP], Z + 15 * K)
        kc_dup = place("kc_dup", [CP * KH, 2, DH], Z + 38 * K + 512)
        oT_hi = [place(f"oT_hi{m}", [P, 4, S], Z + (16 - 16 * m) * K, F32R) for m in range(2)]
        oT_lo = [place(f"oT_lo{m}", [P, 4, S], Z + (24 - 16 * m) * K, F32R) for m in range(2)]
        mT_hi = place("mT_hi", [P, KT, S], Z + 32 * K, F32R)
        mT_lo = place("mT_lo", [P, KT, S], Z + 48 * K, F32R)
        sg = place("sg", [P, 4, S], Z + 64 * K)
        mg = place("mg", [P, 4, S], Z + 72 * K)
        act = place("act", [P, FF // P, S], Z)
        a_hi = place("a_hi", [P, 2, 2 * S], Z + 64 * K, F32R)
        a_lo = place("a_lo", [P, 2, 2 * S], Z + 72 * K, F32R)
        assert base + Z + 112 * K <= nc.sbuf_usable_end

        bank_full = [sem(f"bank_full{b}") for b in range(8)]
        bank_drained = [sem(f"bank_drained{b}") for b in range(8)]
        stage_loaded = [sem(f"stage_loaded{i}") for i in range(2)]
        hi_done = sem("hi_done")
        split_done = sem("split_done")
        half_used = sem("half_used")
        ff2_used = sem("ff2_used")
        x_loaded = [sem(f"x_loaded{tt}") for tt in range(TT)]
        x_reloaded = sem("x_reloaded")
        gains_loaded = sem("gains_loaded")
        small_loaded = sem("small_loaded")
        phi1_loaded = sem("phi1_loaded")
        stored = sem("stored")
        consts = sem("consts")
        x_squared = sem("x_squared")
        x_var = sem("x_var")
        x_rstd = sem("x_rstd")
        x_scaled = sem("x_scaled")
        h_hi_done = sem("h_hi_done")
        h_lo_done = sem("h_lo_done")
        norm_squared = sem("norm_squared")
        norm_summed = sem("norm_summed")
        norm_rstd = sem("norm_rstd")
        ev_names = ["cn", "ki_dup", "cmp_dup", "ks_dup", "ka_dup", "kw_dup", "qb_n", "qa_n", "kc_dup", "gelu_in",
                    "tanh", "gelu", "cmp_soft_in", "cmp_exp", "cmp_p", "gate_exp", "gate_b"]
        ev = {n: sem("ev_" + n) for n in ev_names}
        index_added = sem("index_added")
        score_masked = sem("score_masked")
        exp_done = sem("exp_done")
        pv_done = sem("pv_done")
        oT_hi_done = sem("oT_hi_done")
        sg_done = sem("sg_done")
        mixed = sem("mixed")
        m_hi_done = sem("m_hi_done")
        m_lo_done = sem("m_lo_done")
        relu_done = sem("relu_done")
        act_done = sem("act_done")
        a_hi_done = sem("a_hi_done")
        a_lo_done = sem("a_lo_done")
        y_done = sem("y_done")
        dve_chain = sem("dve_chain")
        pool_chain = sem("pool_chain")
        act_chain = sem("act_chain")

        def chained(eng, semaphore):
            count = [0]

            def link(ins):
                count[0] += 1
                ins.then_inc(semaphore, 1)
                eng.wait_ge(semaphore, count[0])
            return link

        def wait_full(eng, key):
            b, n = bank[key]
            eng.wait_ge(bank_full[b], n)
            return psum[:, b, :]

        def wait_drained(eng, key):
            b, n = bank[key]
            eng.wait_ge(bank_drained[b], n)

        def drained(ins, key):
            ins.then_inc(bank_drained[bank[key][0]], 1)

        def wait_released(eng, p):
            kind, what = released[p]
            if kind == "half":
                eng.wait_ge(half_used, what)
            else:
                wait_full(eng, what)

        def wait_pv(eng, u):
            if u % H == H - 1:
                wait_full(eng, ("O", u // H))
            else:
                eng.wait_ge(pv_done, u + 1 - u // H)

        SPLIT_SIZE = [k * n for _, k, n in panels] + [2048, 2048]

        def drains_probT(u):
            return "vector" if units[u][0] == DSA and u % 2 else "scalar"

        def round_oT(se, copy, m, tt):
            ps = wait_full(se, ("oT", m, tt))
            copy(oT_hi[m][:, :, tt * P:(tt + 1) * P], ps.rearrange("p (k t) -> p k t", k=4)).then_inc(oT_hi_done, 1)

        def weigh(ve, link, tt, ps, factor, key):
            o3 = ps.rearrange("p (h d) -> p h d", d=DH)
            link(nc.vector.tensor_tensor(o3, o3, factor[:, :, None].to_broadcast([P, H, DH]), ALU.mult))
            drained(nc.vector.tensor_tensor(o_b[:, tt, :], o_b[:, tt, :], ps, ALU.add), key)
            wait_drained(ve, key)

        def split_oT(ve, tt_op, m, tt):
            i = tt if m else TT + tt
            ps = wait_full(ve, ("oT", m, tt))
            ve.wait_ge(oT_hi_done, i + 1)
            tok = slice(tt * P, (tt + 1) * P)
            drained(tt_op(oT_lo[m][:, :, tok], ps.rearrange("p (k t) -> p k t", k=4),
                          oT_hi[m][:, :, tok].bitcast(F32), ALU.subtract), ("oT", m, tt))

        block = ctx.enter_context(nc.Block())

        @block.sync
        def _(sp):
            xv = x[0].rearrange("(t p) d -> p t d", p=P)
            for tt in range(TT):
                sp.dma_start(xt[:, tt, :], xv[:, tt, :]).then_inc(x_loaded[tt], 16)
                if tt == 0:
                    rows = [(R_GMIX, g_mix[0].rearrange("(k p) -> k p", p=P)),
                            (R_GMLP, g_mlp[0].rearrange("(k p) -> k p", p=P)), (R_LAT, g_lat_a)]
                    for r, g in ((R_QA, g_q_a), (R_KA, g_k_a), (R_QB, g_q_b), (R_KS, g_ks_b), (R_KW, g_kw_b),
                                 (R_KC, g_kc_b)):
                        rows += [(r, g), (r, g)]
                    rows += [(R_PE, pe_cmp_b[0].rearrange("(j a) d -> j (a d)", a=2))]
                    seen = set()
                    for r, src in rows:
                        n = src.shape[0]
                        width = src.shape[1]
                        c0 = width if r in seen else 0
                        seen.add(r)
                        sp.dma_start(gain_rows[r:r + n, c0:c0 + width], src).then_inc(gains_loaded, 16)

            def load_panel(p):
                src, k, n = panels[p]
                if p >= 2:
                    sp.wait_ge(split_done, p - 1)
                sp.dma_start(stage[:, p % 2, 0:k * n].rearrange("p (k n) -> p k n", k=k), src)\
                  .then_inc(stage_loaded[p % 2], 16)

            load_panel(0)
            load_panel(1)
            sp.dma_start(w_ukv[:, 0, :], w_uk_a[0]).then_inc(small_loaded, 16)
            sp.dma_start(w_ukv[:, 1, :], w_uv_a[0]).then_inc(small_loaded, 16)
            sp.dma_start(phi2[:, 0, :], phi_k2_b[0]).then_inc(small_loaded, 16)
            sp.dma_start(phi2[:, 1, :], phi_v2_b[0]).then_inc(small_loaded, 16)
            for p in range(2, 4):
                load_panel(p)
            for i, w in enumerate((phi_k1_b, phi_v1_b)):
                sp.dma_start(phi1[i][:, :, :], w[0].rearrange("(j p) h -> p j h", p=P)).then_inc(phi1_loaded, 16)
            for p in range(4, GATE0 + 2):
                load_panel(p)
            for tt in range(TT):
                wait_drained(sp, ("oT", 0, tt))
            sp.dma_start(xt[:, :, :], xv).then_inc(x_reloaded, 16)
            for p in range(GATE0 + 2, FF1):
                load_panel(p)

            def load_ff1(p, q_half, col, settled):
                sp.wait_ge(split_done, settled)
                sp.dma_start(stage[:, q_half, :].rearrange("p (k n) -> p k n", k=4),
                             w_ff1_k[:, 4 * q_half:4 * q_half + 4, col]).then_inc(stage_loaded[q_half], 16)

            for q in range(2):
                load_ff1(FF1 + q, q, slice(0, BANK), FF1 + q - 1)
            with sp.Fori(0, NFF1 // 2 - 1) as i:
                for hfl in range(2):
                    load_ff1(None, hfl, bass.ds(i * BANK + BANK, BANK), 2 * i + (FF1 + 1 + hfl))
            with sp.Fori(0, NFF2 // 2) as i:
                for k in range(2):
                    sp.wait_ge(split_done, 2 * i + (FF2 + k - 1))
                    sp.dma_start(stage[:, k, :].rearrange("p (k n) -> p k n", k=2),
                                 w_ff2_k[:, bass.ds(4 * i + 2 * k, 2), :]).then_inc(stage_loaded[k], 16)
            ov = out[0].rearrange("(t p) d -> p t d", p=P)
            for tt in range(TT):
                sp.wait_ge(y_done, 2 * (tt + 1))
                sp.dma_start(ov[:, tt, :], xt[:, tt, :]).then_inc(stored, 16)
            sp.wait_ge(stored, 16 * TT)

        @block.gpsimd
        def _(pool):
            link = chained(pool, pool_chain)
            link(nc.gpsimd.memset(ident[:, :], 0.0))
            nc.gpsimd.affine_select(out=ident[:, :], in_=ident[:, :], compare_op=ALU.not_equal, fill=1.0, base=0,
                                    pattern=[[-1, P]], channel_multiplier=1).then_inc(consts, 1)
            nc.gpsimd.memset(neg_half[:, :], -0.5).then_inc(consts, 1)
            pool.wait_ge(consts, 2)

            def rstd_of_x(i):
                pool.wait_ge(x_var, i + 1)
                nc.gpsimd.tensor_tensor(xrstd[:, i:i + 1], xvar[:, i:i + 1], neg_half[:, 0:1], ALU.pow)\
                    .then_inc(x_rstd, 1)

            for tt in range(TT):
                rstd_of_x(tt)
            link(nc.gpsimd.iota(dist[:, :], pattern=[[-1, S]], base=S - P, channel_multiplier=1,
                                allow_small_or_imprecise_dtypes=True))
            nc.gpsimd.affine_select(out=dist[:, S - P:S], in_=dist[:, S - P:S], compare_op=ALU.is_ge, fill=MASKED,
                                    base=0, pattern=[[-1, P]], channel_multiplier=1).then_inc(consts, 1)
            for h in range(H):
                nc.gpsimd.memset(q_scale[:, h:h + 1], -float(2 ** (h + 1)) * DH ** -0.5).then_inc(consts, 1)
                nc.gpsimd.memset(cmp_scale[:, h * CP:(h + 1) * CP], -float(2.0 ** -(h + 1))).then_inc(consts, 1)
            for t in (gel_k[:, :, :], gel_v[:, :, :, :], vc_diag[:, :, :, :]):
                nc.gpsimd.memset(t, 0.0).then_inc(consts, 1)
            link(nc.gpsimd.memset(cmp_valid[:, :, :], 1.0))
            link(nc.gpsimd.affine_select(out=cmp_valid[:, :, :], in_=cmp_valid[:, :, :], compare_op=ALU.is_ge,
                                         fill=0.0, base=1 - CMP_LEN, pattern=[[P, TT], [-CMP_STRIDE, CP]],
                                         channel_multiplier=1))
            nc.gpsimd.tensor_scalar(cmp_mask[:, :, :], cmp_valid[:, :, :], -1.0, 1e30, ALU.add, ALU.mult)\
                .then_inc(consts, 1)

            def rstd(name):
                i, cols = NORMS[name]
                rows = CP * KH if name == "kc" else P
                n = cols.stop - cols.start
                pool.wait_ge(norm_summed, i)
                nc.gpsimd.tensor_tensor(nrstd[0:rows, cols], nvar[0:rows, cols], neg_half[0:rows, 0:n], ALU.pow)\
                    .then_inc(norm_rstd, 1)

            rstd("c")
            for tt in range(TT):
                wait_drained(pool, ("proj", C_KV1, tt))
            for t in range(2):
                for d in range(2):
                    nc.gpsimd.tensor_copy(cmp_dup[:, t, :, :, d, :],
                                          p_kv1[:, :, t * KVW:(t + 1) * KVW]
                                          .rearrange("p t (g d) -> p t g d", g=KH)).then_inc(ev["cmp_dup"], 1)
            rstd("ks")
            rstd("ka")
            for tt in range(1, TT):
                pool.wait_ge(index_added, IH * tt)
                diag = score[:, score_at[tt] + tt * P:score_at[tt] + (tt + 1) * P]
                nc.gpsimd.affine_select(out=diag, in_=diag, compare_op=ALU.is_ge, fill=FUTURE, base=0,
                                        pattern=[[-1, P]], channel_multiplier=1).then_inc(score_masked, 1)
            for name in ("kw", "qb", "kc", "qa"):
                rstd(name)
            for tt in range(TT):
                rstd_of_x(TT + tt)

        CONSTS_ALL = 2 + 1 + 2 * H + 3 + 1

        @block.scalar
        def _(se):
            link = chained(se, act_chain)

            def copy(dst, src, scale=1.0):
                return nc.scalar.activation(dst, src, ACT.Copy, scale=scale)

            def round_panel(p):
                se.wait_ge(stage_loaded[p % 2], 16 * (p // 2 + 1))
                if p >= 2:
                    wait_released(se, p - 2)
                n = SPLIT_SIZE[p]
                copy(w_hi[:, p % 2, 0:n], stage[:, p % 2, 0:n]).then_inc(hi_done, 1)

            def round_h(key, tt, hfl):
                i = 2 * tt + hfl
                wait_drained(se, (key, tt, hfl))
                copy(hT_hi[:, 4 * hfl:4 * hfl + 4, tt * P:(tt + 1) * P],
                     hf[:, i % 2, :].rearrange("p (k t) -> p k t", k=4)).then_inc(h_hi_done, 1)

            def squares(name, src, dst):
                i, _ = NORMS[name]
                if i >= 2:
                    se.wait_ge(norm_summed, i - 1)
                nc.scalar.activation(dst, src, ACT.Square).then_inc(norm_squared, 1)

            def drain_proj(c, dst):
                for tt in range(TT):
                    ps = wait_full(se, ("proj", c, tt))
                    drained(copy(dst[:, tt, :], ps[:, 0:PROJ[c][1]]), ("proj", c, tt))

            def drain_T(key, dst, gain=None):
                ps = wait_full(se, key)
                scale = 1.0 if gain is None else gains[:, gain:gain + 1]
                drained(copy(dst, ps[:, 0:dst.shape[1]], scale), key)

            for tt in range(TT):
                se.wait_ge(x_loaded[tt], 16)
                nc.scalar.activation(xs[:, tt, :], xt[:, tt, :], ACT.Square, accum_out=xss[:, tt:tt + 1])\
                    .then_inc(x_squared, 1)
            for hfl in range(2):
                round_h("hT", 0, hfl)
            round_panel(0)
            for i in range(2, 2 * TT):
                round_h("hT", i // 2, i % 2)
            round_panel(1)
            round_panel(2)
            drain_proj(C_IDX, p_idx)
            for tt in range(TT):
                wait_drained(se, ("proj", C_IDX, tt))
            squares("c", p_idx[:, :, 0:LAT], square[:, 0:TT * LAT].rearrange("p (t n) -> p t n", t=TT))
            ki = p_idx[:, :, LAT + IH * ID:LAT + IH * ID + ID]
            copy(ki_dup[:, :, :, :], ki[:, :, None, :].to_broadcast([P, TT, G, ID])).then_inc(ev["ki_dup"], 1)
            round_panel(3)
            round_panel(4)
            se.wait_ge(gains_loaded, 16 * 16)
            se.wait_ge(bank_drained[0], 1)
            drain_T(("T_idx", 0), cT[:, :], R_LAT)
            drain_T(("T_idx", 1), qiT[:, 0, :])
            drain_T(("T_idx", 2), qiT[:, 1, :])
            drain_T(("T_idx", 3), kiT[:, :])
            round_panel(5)
            drain_proj(C_KV1, p_kv1)
            for tt in range(TT):
                wait_drained(se, ("proj", C_KV1, tt))
            squares("ks", p_kv1[:, :, 2 * KVW:3 * KVW], square[:, 0:TT * KVW].rearrange("p (t n) -> p t n", t=TT))
            round_panel(6)
            wait_drained(se, ("kv_a", 0))
            squares("ka", kv_a[:, :, 0:DH], square[:, 0:TT * DH].rearrange("p (t n) -> p t n", t=TT))
            def relu_unit(u):
                tt, h = INDEX_UNITS[u]
                w = (tt + 1) * P
                ps = wait_full(se, ("index", u))
                if u >= 2:
                    se.wait_ge(index_added, u - 1)
                drained(nc.scalar.activation(relu[:, u % 2, 0:w], ps[:, 0:w], ACT.Relu), ("index", u))

            for u in range(len(INDEX_UNITS)):
                if u == 0:
                    for g in range(KH):
                        drain_T(("ksT", g), ksT[:, g, :], R_KS)
                relu_unit(u)
            round_panel(7)
            drain_proj(C_KV2, p_kv2)
            for tt in range(TT):
                wait_drained(se, ("proj", C_KV2, tt))
            squares("kw", p_kv2[:, :, KVW:2 * KVW], square[:, 0:TT * KVW].rearrange("p (t n) -> p t n", t=TT))
            nc.scalar.activation(gate_b[:, :, :], p_kv2[:, :, 3 * KVW:], ACT.Exp, scale=-1.0)\
                .then_inc(ev["gate_exp"], 1)
            round_panel(8)
            drain_T("kaT", kaT[:, :], R_KA)
            for g in range(KH):
                drain_T(("kwT", g), kwT[:, g, :], R_KW)
            se.wait_ge(ev["gelu_in"], 1)
            nc.scalar.activation(gel[:, :, :, :], gel[:, :, :, :], ACT.Tanh, scale=GELU_IN).then_inc(ev["tanh"], 1)
            round_panel(9)
            drain_proj(C_QB, p_q)
            for tt in range(TT):
                wait_drained(se, ("proj", C_QB, tt))
            pq = p_q[:, :, :].rearrange("p t n -> p (t n)")
            squares("qb", pq, square[:, :])
            round_panel(10)
            for i in range(4):
                drain_T(("qbT", i), qbT[:, i, :], R_QB)
            wait_drained(se, "kc")
            squares("kc", kc[:, :], square[0:CP * KH, 0:DH])
            round_panel(11)
            drain_proj(C_QA, p_q)
            for tt in range(TT):
                wait_drained(se, ("proj", C_QA, tt))
            squares("qa", pq, square[:, :])
            drain_T("kcT", kcT[:, :], R_KC)
            for i in range(4):
                drain_T(("qaT", i), qaT[:, i, :], R_QA)
            se.wait_ge(ev["cmp_soft_in"], 1)
            nc.scalar.activation(cmp_e[:, :, :, :], cmp_e[:, :, :, :], ACT.Exp).then_inc(ev["cmp_exp"], 1)

            for s in range(STEPS):
                if s < NU:
                    br, tt, h = units[s]
                    w = (tt + 1) * P
                    wait_drained(se, ("S", s))
                    nc.scalar.activation(prob[:, s % 3, 0:w], prob[:, s % 3, 0:w], ACT.Exp, scale=-1.0,
                                         bias=neg_max[:, s % 4:s % 4 + 1],
                                         accum_out=row_sum[:, s:s + 1]).then_inc(exp_done, 1)
                if s == CMP_STEP:
                    for g in range(KH):
                        drain_T(("cmpPT", g), cmp_pT[:, g, :])
                u = s - T_LAG
                if 0 <= u < NU and drains_probT(u) == "scalar":
                    w = (units[u][1] + 1) * P
                    ps = wait_full(se, ("PT", u))
                    if u >= 3:
                        wait_pv(se, u - 3)
                    drained(copy(probT[:, u % 3, 0:w], ps[:, 0:w]), ("PT", u))
                if s == NSA_DONE + 2:
                    for tt2 in range(TT):
                        round_oT(se, copy, 1, tt2)
            for tt in range(TT):
                round_oT(se, copy, 0, tt)

            for p in range(GATE0, OUT0):
                n, m, j = (p - GATE0) // 6, (p - GATE0) // 3 % 2, (p - GATE0) % 3
                round_panel(p + 2)
                if j == 1:
                    for i in range(4):
                        ps = wait_full(se, ("gate", n, m, i))
                        if m:
                            wait_drained(se, ("up", n, 0, i))
                        elif n:
                            se.wait_ge(mixed, 4 * n)
                        drained(nc.scalar.activation(sg[:, i, :], ps, ACT.Sigmoid), ("gate", n, m, i))
                if j == 2 and m == 1:
                    for i in range(4):
                        se.wait_ge(mixed, 4 * n + i + 1)
                        copy(mT_hi[:, 4 * n + i, :], mg[:, i, :]).then_inc(m_hi_done, 1)
            for p in range(OUT0, FF1 - 1):
                round_panel(p + 2)
            for tt in range(TT):
                wait_drained(se, ("out", 1, tt))
                nc.scalar.activation(xs[:, tt, :], xt[:, tt, :], ACT.Square,
                                     accum_out=xss[:, TT + tt:TT + tt + 1]).then_inc(x_squared, 1)
                if tt >= 1:
                    for hfl in range(2):
                        round_h("h2T", tt - 1, hfl)
            for hfl in range(2):
                round_h("h2T", TT - 1, hfl)
            round_panel(FF1 + 1)

            with se.Fori(0, NFF1 // 4) as i:
                for k in range(4):
                    b0 = 4 * (k // 2)
                    if k % 2 == 0:
                        se.wait_ge(half_used, 2 * i + (HALVES_FF1 + 1 + k // 2))
                    else:
                        se.wait_ge(bank_full[b0 + 3], i + ff1_first[b0 + 3])
                    se.wait_ge(stage_loaded[k % 2], 32 * i + 16 * ((FF1 + 2 + k) // 2 + 1))
                    copy(w_hi[:, k % 2, :], stage[:, k % 2, :]).then_inc(hi_done, 1)
                    if k % 2:
                        for j in range(4):
                            nc.scalar.activation(act[:, bass.ds(8 * i + (b0 + j), 1), :].rearrange("p a t -> p (a t)"),
                                                 psum[:, b0 + j, :], ACT.Relu).then_inc(bank_drained[b0 + j], 1)

            def round_act(q, pair, count):
                se.wait_ge(act_done, count)
                copy(a_hi[:, q % 2, :], act[:, pair, :].rearrange("p a t -> p (a t)")).then_inc(a_hi_done, 1)

            for q in range(2):
                round_act(q, slice(2 * q, 2 * q + 2), FF // P)
            with se.Fori(0, NFF2 // 2 - 1) as i:
                for k in range(2):
                    se.wait_ge(ff2_used, 2 * i + (k + 1))
                    se.wait_ge(stage_loaded[k], 16 * i + 16 * ((FF2 + 2 + k) // 2 + 1))
                    copy(w_hi[:, k, :], stage[:, k, :]).then_inc(hi_done, 1)
                    copy(a_hi[:, k, :], act[:, bass.ds(4 * i + (4 + 2 * k), 2), :].rearrange("p a t -> p (a t)"))\
                        .then_inc(a_hi_done, 1)

        @block.vector
        def _(ve):
            link = chained(ve, dve_chain)
            tt_op = nc.vector.tensor_tensor

            def split_panel(p):
                n = SPLIT_SIZE[p]
                ve.wait_ge(hi_done, p + 1)
                tt_op(w_lo[:, p % 2, 0:n], stage[:, p % 2, 0:n], w_hi[:, p % 2, 0:n].bitcast(F32), ALU.subtract)\
                    .then_inc(split_done, 1)

            def scale_x(i, tt):
                ve.wait_ge(x_squared, i + 1)
                nc.vector.tensor_scalar(xvar[:, i:i + 1], xss[:, i:i + 1], 1.0 / D, EPS, ALU.mult, ALU.add)\
                    .then_inc(x_var, 1)
                ve.wait_ge(x_rstd, i + 1)
                nc.vector.tensor_scalar(xs[:, tt, :], xt[:, tt, :], xrstd[:, i:i + 1], None, ALU.mult)\
                    .then_inc(x_scaled, 1)

            def drain_h(i, tt, key, row):
                for hfl in range(2):
                    j = i + hfl
                    ps = wait_full(ve, (key, tt, hfl))
                    g = gains[:, row + 4 * hfl:row + 4 * hfl + 4]
                    if j >= 2:
                        ve.wait_ge(h_lo_done, j - 1)
                    drained(tt_op(hf[:, j % 2, :].rearrange("p (k t) -> p k t", k=4), ps.rearrange("p (k t) -> p k t", k=4),
                                  g[:, :, None].to_broadcast([P, 4, P]), ALU.mult), (key, tt, hfl))
                for hfl in range(2):
                    j = i + hfl
                    ve.wait_ge(h_hi_done, j + 1)
                    tok = slice(tt * P, (tt + 1) * P)
                    tt_op(hT_lo[:, 4 * hfl:4 * hfl + 4, tok],
                          hf[:, j % 2, :].rearrange("p (k t) -> p k t", k=4),
                          hT_hi[:, 4 * hfl:4 * hfl + 4, tok].bitcast(F32), ALU.subtract).then_inc(h_lo_done, 1)

            def norm(name, n, count, src=None):
                i, cols = NORMS[name]
                rows = CP * KH if name == "kc" else P
                ve.wait_ge(norm_squared, i)
                link(nc.vector.tensor_reduce(nss[0:rows, cols],
                                             square[0:rows, 0:count * n].rearrange("p (a n) -> p a n", n=n),
                                             AX.X, ALU.add))
                nc.vector.tensor_scalar(nvar[0:rows, cols], nss[0:rows, cols], 1.0 / n, EPS, ALU.mult, ALU.add)\
                    .then_inc(norm_summed, 1)
                ve.wait_ge(norm_rstd, i)
                return nrstd[0:rows, cols]

            ve.wait_ge(consts, 2)
            b, _ = bank["gains"]
            ps = wait_full(ve, "gains")
            drained(nc.vector.tensor_copy(gains[:, :], ps[:, 0:NG]), "gains")
            ve.wait_ge(bank_drained[b], 1)
            for tt in range(TT):
                scale_x(tt, tt)
                if tt >= 1:
                    drain_h(2 * (tt - 1), tt - 1, "hT", R_GMIX)
                if tt == 1:
                    split_panel(0)
            drain_h(2 * TT - 2, TT - 1, "hT", R_GMIX)
            split_panel(1)
            split_panel(2)
            r = norm("c", LAT, TT)
            c = p_idx[:, :, 0:LAT]
            tt_op(c, c, r[:, :, None].to_broadcast([P, TT, LAT]), ALU.mult).then_inc(ev["cn"], 1)
            link(nc.vector.tensor_scalar(wi[:, :, :], p_idx[:, :, LAT + IH * ID + ID:],
                                         float(IH ** -0.5 * ID ** -0.5), None, ALU.mult))
            split_panel(3)
            split_panel(4)
            split_panel(5)

            def scale_dup(name, dst, src):
                r = norm(name, DH, TT * KH)
                r = r.rearrange("p (t g) -> p t g", g=KH)[:, :, :, None].to_broadcast([P, TT, KH, DH])
                src = src.rearrange("p t (g d) -> p t g d", g=KH)
                link(tt_op(dst[:, :, :, 0, :], src, r, ALU.mult))
                tt_op(dst[:, :, :, 1, :], src, r, ALU.mult).then_inc(ev[name + "_dup"], 1)

            scale_dup("ks", ks_dup, p_kv1[:, :, 2 * KVW:3 * KVW])
            split_panel(6)
            ps = wait_full(ve, ("kv_a", 0))
            drained(nc.vector.tensor_copy(kv_a[:, :, :], ps.rearrange("p (t n) -> p t n", t=TT)), ("kv_a", 0))
            for i in range(4):
                t, g = divmod(i, KH)
                ps = wait_full(ve, ("cmpT", i))
                for par in range(2):
                    rows = slice(par * DH, (par + 1) * DH)
                    for v in range(2):
                        pe = gains[rows, R_PE + 8 * v:R_PE + 8 * v + 8]
                        ins = tt_op(cmp_in[rows, t, v, g, :].rearrange("p (c j) -> p c j", j=8),
                                    ps.rearrange("p (c j a) -> p c j a", j=8, a=2)[rows, :, :, par],
                                    pe[:, None, :].to_broadcast([DH, S // 16, 8]), ALU.add)
                        if par and v:
                            drained(ins, ("cmpT", i))
                        else:
                            link(ins)
            r = norm("ka", DH, TT)
            r = r[:, :, None].to_broadcast([P, TT, DH])
            link(tt_op(ka_dup[:, :, 0, :], kv_a[:, :, 0:DH], r, ALU.mult))
            tt_op(ka_dup[:, :, 1, :], kv_a[:, :, 0:DH], r, ALU.mult).then_inc(ev["ka_dup"], 1)
            for u, (tt, h) in enumerate(INDEX_UNITS):
                w = (tt + 1) * P
                dst = score[:, score_at[tt]:score_at[tt] + w]
                wait_drained(ve, ("index", u))
                if h == 0:
                    ins = nc.vector.tensor_scalar(dst, relu[:, u % 2, 0:w], wi[:, tt, h:h + 1], None, ALU.mult)
                else:
                    ve.wait_ge(index_added, u)
                    ins = nc.vector.scalar_tensor_tensor(out=dst, in0=relu[:, u % 2, 0:w], scalar=wi[:, tt, h:h + 1],
                                                         in1=dst, op0=ALU.mult, op1=ALU.add)
                ins.then_inc(index_added, 1)
            split_panel(7)
            scale_dup("kw", kw_dup, p_kv2[:, :, KVW:2 * KVW])
            ve.wait_ge(ev["gate_exp"], 1)
            link(nc.vector.tensor_scalar(gate_b[:, :, :], gate_b[:, :, :], 1.0, None, ALU.add))
            nc.vector.reciprocal(gate_b[:, :, :], gate_b[:, :, :]).then_inc(ev["gate_b"], 1)
            split_panel(8)
            for t in range(2):
                ps = wait_full(ve, ("hidden", t))
                drained(nc.vector.tensor_copy(hid[:, t, :, :].rearrange("p g c -> p (g c)"), ps[:, 0:KH * NCMP]),
                        ("hidden", t))
                wait_drained(ve, ("hidden", t))
            link(tt_op(gel[:, :, :, :], hid[:, :, :, :], hid[:, :, :, :], ALU.mult))
            link(nc.vector.tensor_scalar(gel[:, :, :, :], gel[:, :, :, :], GELU_CUBE, 1.0, ALU.mult, ALU.add))
            tt_op(gel[:, :, :, :], gel[:, :, :, :], hid[:, :, :, :], ALU.mult).then_inc(ev["gelu_in"], 1)
            ve.wait_ge(ev["tanh"], 1)
            link(nc.vector.tensor_scalar(gel[:, :, :, :], gel[:, :, :, :], 1.0, 0.5, ALU.add, ALU.mult))
            ve.wait_ge(consts, CONSTS_ALL)
            link(tt_op(gel_k[:, :, 0:NCMP], gel[:, 0, :, :], hid[:, 0, :, :], ALU.mult))
            tt_op(gel_v[:, :, :, 0:NCMP], gel[:, 1, :, None, :].to_broadcast([P, KH, G, NCMP]),
                  hid[:, 1, :, None, :].to_broadcast([P, KH, G, NCMP]), ALU.mult).then_inc(ev["gelu"], 1)
            split_panel(9)

            def scale_q(name):
                r = norm(name, DH, TT * H)
                r3 = r.rearrange("p (t h) -> p t h", h=H)
                link(tt_op(r3, r3, q_scale[:, None, :].to_broadcast([P, TT, H]), ALU.mult))
                q3 = p_q[:, :, :].rearrange("p t (h d) -> p (t h) d", d=DH)
                tt_op(q3, q3, r[:, :, None].to_broadcast([P, TT * H, DH]), ALU.mult).then_inc(ev[name + "_n"], 1)

            scale_q("qb")
            split_panel(10)
            ps = wait_full(ve, "kc")
            drained(nc.vector.tensor_copy(kc[:, :], ps[0:CP * KH, 0:DH]), "kc")
            ps = wait_full(ve, "vc")
            for i in range(G):
                rows = slice(i * CP, (i + 1) * CP)
                ins = nc.vector.tensor_copy(vc_diag[rows, :, i, :],
                                            ps[rows, 0:KH * DH].rearrange("p (g d) -> p g d", g=KH))
                if i == G - 1:
                    drained(ins, "vc")
                else:
                    link(ins)
            r = norm("kc", DH, 1)
            for d in range(2):
                ins = nc.vector.tensor_scalar(kc_dup[:, d, :], kc[:, :], r, None, ALU.mult)
                if d:
                    ins.then_inc(ev["kc_dup"], 1)
                else:
                    link(ins)
            split_panel(11)
            scale_q("qa")
            for i in range(4):
                pair, par = divmod(i, 2)
                ps = wait_full(ve, ("cmpS", i))
                for t2 in range(2):
                    ins = tt_op(cmp_e[:, 2 * pair + t2, par:H:2, :],
                                ps[:, t2 * P:(t2 + 1) * P].rearrange("p (h c) -> p h c", c=CP),
                                cmp_scale[:, :].rearrange("p (h c) -> p h c", c=CP)[:, par:H:2, :], ALU.mult)
                    if t2:
                        drained(ins, ("cmpS", i))
                        wait_drained(ve, ("cmpS", i))
                    else:
                        link(ins)
            e = cmp_e[:, :, :, :]
            e_rows = e.rearrange("p t h c -> p (t h) c")
            link(tt_op(e, e, cmp_mask[:, :, None, :].to_broadcast([P, TT, H, CP]), ALU.add))
            link(nc.vector.tensor_reduce(cmp_max[:, :], e_rows, AX.X, ALU.max))
            tt_op(e_rows, e_rows, cmp_max[:, :, None].to_broadcast([P, TT * H, CP]), ALU.subtract)\
                .then_inc(ev["cmp_soft_in"], 1)
            ve.wait_ge(ev["cmp_exp"], 1)
            link(nc.vector.tensor_reduce(cmp_sum[:, :], e_rows, AX.X, ALU.add))
            link(nc.vector.reciprocal(cmp_sum[:, :], cmp_sum[:, :]))
            ve.wait_ge(ev["gate_b"], 1)
            gates = gate_b[:, :, :].rearrange("p t (h b) -> p t h b", b=3)
            cs3 = cmp_sum[:, :].rearrange("p (t h) -> p t h", h=H)
            link(tt_op(cs3, cs3, gates[:, :, :, 0], ALU.mult))
            tt_op(e, e, cmp_valid[:, :, None, :].to_broadcast([P, TT, H, CP]), ALU.mult).then_inc(ev["cmp_p"], 1)

            rounds = [(tt, k) for tt in range(1, TT) for k in range(TOPK // 8)]
            ve.wait_ge(score_masked, TT - 1)
            for s in range(STEPS):
                if s < NU:
                    br, tt, h = units[s]
                    w = (tt + 1) * P
                    ps = wait_full(ve, ("S", s))
                    if s >= 3:
                        wait_full(ve, ("PT", s - 3))
                    if br == DSA and tt:
                        d = score[:, score_at[tt]:score_at[tt] + w]
                    else:
                        d = dist[:, S - w:S]
                    drained(nc.vector.tensor_tensor_reduce(out=prob[:, s % 3, 0:w], in0=ps[:, 0:w], in1=d,
                                                           scale=float(2.0 ** -(h + 1)), scalar=3e38, op0=ALU.add,
                                                           op1=ALU.min, accum_out=neg_max[:, s % 4:s % 4 + 1]),
                            ("S", s))
                if rounds and s >= 3:
                    tt1, k = rounds.pop(0)
                    sc = score[:, score_at[tt1]:score_at[tt1] + (tt1 + 1) * P]
                    link(nc.vector.max(top8[:, :], sc))
                    link(nc.vector.match_replace(sc, top8[:, :], sc, TAKEN))
                    if k == TOPK // 8 - 1:
                        w1 = (tt1 + 1) * P
                        link(nc.vector.tensor_scalar(sc, sc, TAKEN, MASKED, ALU.not_equal, ALU.mult))
                        link(tt_op(sc, sc, dist[:, S - w1:S], ALU.add))
                u = s - T_LAG
                if 0 <= u < NU and drains_probT(u) == "vector":
                    w = (units[u][1] + 1) * P
                    ps = wait_full(ve, ("PT", u))
                    wait_pv(ve, u - 3)
                    drained(nc.vector.tensor_copy(probT[:, u % 3, 0:w], ps[:, 0:w]), ("PT", u))
                if s == CMP_STEP:
                    for tt2 in range(TT):
                        ps = wait_full(ve, ("cmpO", tt2))
                        weigh(ve, link, tt2, ps, cs3[:, tt2, :], ("cmpO", tt2))
                u = s - PV_LAG - 1
                if 0 <= u < NU and u % H == H - 1:
                    br, tt, _ = units[u]
                    ti = u // H
                    b, _ = bank[("O", ti)]
                    wait_pv(ve, u)
                    ve.wait_ge(exp_done, u + 1)
                    inv = row_inv[:, ti * H:(ti + 1) * H]
                    link(nc.vector.reciprocal(inv, row_sum[:, ti * H:(ti + 1) * H]))
                    if br == DSA:
                        drained(tt_op(o_a[:, tt, :].rearrange("p (h d) -> p h d", d=DH),
                                      psum[:, b, :].rearrange("p (h d) -> p h d", d=DH),
                                      inv[:, :, None].to_broadcast([P, H, DH]), ALU.mult), ("O", ti))
                    else:
                        link(tt_op(inv, inv, gates[:, tt, :, 1 + br], ALU.mult))
                        if br == SLC:
                            drained(tt_op(o_b[:, tt, :].rearrange("p (h d) -> p h d", d=DH),
                                          psum[:, b, :].rearrange("p (h d) -> p h d", d=DH),
                                          inv[:, :, None].to_broadcast([P, H, DH]), ALU.mult), ("O", ti))
                            wait_drained(ve, ("O", ti))
                        else:
                            weigh(ve, link, tt, psum[:, b, :], inv, ("O", ti))
                if s == NSA_DONE + 2:
                    for tt2 in range(TT):
                        split_oT(ve, tt_op, 1, tt2)
            for tt in range(TT):
                split_oT(ve, tt_op, 0, tt)

            for p in range(GATE0, OUT0):
                n, m, j = (p - GATE0) // 6, (p - GATE0) // 3 % 2, (p - GATE0) % 3
                split_panel(p + 2)
                if j == 2:
                    for i in range(4):
                        ps = wait_full(ve, ("up", n, m, i))
                        wait_drained(ve, ("gate", n, m, i))
                        if m == 0:
                            drained(tt_op(mg[:, i, :], sg[:, i, :], ps, ALU.mult), ("up", n, m, i))
                            wait_drained(ve, ("up", n, m, i))
                        else:
                            drained(tt_op(sg[:, i, :], sg[:, i, :], ps, ALU.mult), ("up", n, m, i))
                            wait_drained(ve, ("up", n, m, i))
                            tt_op(mg[:, i, :], mg[:, i, :], sg[:, i, :], ALU.add).then_inc(mixed, 1)
                    if m == 1:
                        for i in range(4):
                            ve.wait_ge(m_hi_done, 4 * n + i + 1)
                            tt_op(mT_lo[:, 4 * n + i, :], mg[:, i, :], mT_hi[:, 4 * n + i, :].bitcast(F32),
                                  ALU.subtract).then_inc(m_lo_done, 1)
            split_panel(OUT0 + 2)
            split_panel(OUT0 + 3)
            ve.wait_ge(x_reloaded, 16)

            def add_residual(n, tt):
                ps = wait_full(ve, ("out", n, tt))
                dst = xt[:, tt, n * BANK:(n + 1) * BANK]
                drained(tt_op(dst, dst, ps, ALU.add), ("out", n, tt))
                wait_drained(ve, ("out", n, tt))

            for tt in range(TT):
                add_residual(0, tt)
            split_panel(FF1)
            for tt in range(TT):
                add_residual(1, tt)
                scale_x(TT + tt, tt)
                if tt >= 1:
                    drain_h(2 * TT + 2 * (tt - 1), tt - 1, "h2T", R_GMLP)
            drain_h(4 * TT - 2, TT - 1, "h2T", R_GMLP)
            split_panel(FF1 + 1)
            with ve.Fori(0, NFF1 // 4) as i:
                for k in range(4):
                    b0 = 4 * (k // 2)
                    ve.wait_ge(hi_done, 4 * i + (FF1 + 2 + k + 1))
                    tt_op(w_lo[:, k % 2, :], stage[:, k % 2, :], w_hi[:, k % 2, :].bitcast(F32), ALU.subtract)\
                        .then_inc(split_done, 1)
                    if k % 2:
                        for j in range(4):
                            a = act[:, bass.ds(8 * i + (b0 + j), 1), :].rearrange("p a t -> p (a t)")
                            ve.wait_ge(bank_drained[b0 + j], i + ff1_first[b0 + j])
                            tt_op(a, a, a, ALU.mult).then_inc(act_done, 1)

            def split_act(q, pair):
                ve.wait_ge(a_hi_done, q + 1)
                tt_op(a_lo[:, q % 2, :], act[:, pair, :].rearrange("p a t -> p (a t)"),
                      a_hi[:, q % 2, :].bitcast(F32), ALU.subtract).then_inc(a_lo_done, 1)

            for q in range(2):
                split_act(q, slice(2 * q, 2 * q + 2))
            with ve.Fori(0, NFF2 // 2 - 1) as i:
                for k in range(2):
                    ve.wait_ge(hi_done, 2 * i + (FF2 + 2 + k + 1))
                    tt_op(w_lo[:, k, :], stage[:, k, :], w_hi[:, k, :].bitcast(F32), ALU.subtract)\
                        .then_inc(split_done, 1)
                    ve.wait_ge(a_hi_done, 2 * i + (k + 3))
                    tt_op(a_lo[:, k, :], act[:, bass.ds(4 * i + (4 + 2 * k), 2), :].rearrange("p a t -> p (a t)"),
                          a_hi[:, k, :].bitcast(F32), ALU.subtract).then_inc(a_lo_done, 1)
            for tt in range(TT):
                for n in range(2):
                    ps = wait_full(ve, ("y", 2 * tt + n))
                    dst = xt[:, tt, n * BANK:(n + 1) * BANK]
                    tt_op(dst, dst, ps, ALU.add).then_inc(y_done, 1)

        @block.tensor
        def _(te):
            mm = nc.tensor.matmul

            def open_bank(key):
                b, n = bank[key]
                if n >= 2:
                    te.wait_ge(bank_drained[b], n - 1)
                return psum[:, b, :]

            def full(ins, key):
                ins.then_inc(bank_full[bank[key][0]], 1)

            def product(dst, a_h, a_l, b_h, b_l, start, stop):
                mm(dst, a_h, b_h, start=start, stop=False)
                mm(dst, a_h, b_l, start=False, stop=False)
                return mm(dst, a_l, b_h, start=False, stop=stop)

            def natural_panel(p, keys, lhs_hi, lhs_lo, half):
                n = panels[p][2]
                te.wait_ge(split_done, p + 1)
                for tt in range(TT):
                    dst = (open_bank(keys[tt]) if half == 0 else psum[:, bank[keys[tt]][0], :])[:, 0:n]
                    tok = slice(tt * P, (tt + 1) * P)
                    for k in range(4):
                        cols = slice(k * n, (k + 1) * n)
                        last = product(dst, lhs_hi[:, 4 * half + k, tok], lhs_lo[:, 4 * half + k, tok],
                                       w_hi[:, p % 2, cols], w_lo[:, p % 2, cols],
                                       start=half == 0 and k == 0, stop=half == 1 and k == 3)
                    if half:
                        full(last, keys[tt])
                if not half:
                    last.then_inc(half_used, 1)

            def transposes(key, blocks):
                dst = open_bank(key)
                for i, src in enumerate(blocks):
                    rows, cols = src.shape
                    last = nc.tensor.transpose(dst[0:cols, i * rows:(i + 1) * rows], src, ident[0:rows, 0:rows])
                full(last, key)

            te.wait_ge(consts, 2)
            te.wait_ge(gains_loaded, 16 * 16)
            transposes("gains", [gain_rows[:, :]])
            def h_transposes(key, i0):
                for tt in range(TT):
                    te.wait_ge(x_scaled, i0 + tt + 1)
                    for hfl in range(2):
                        transposes((key, tt, hfl),
                                   [xs[:, tt, (4 * hfl + k) * P:(4 * hfl + k + 1) * P] for k in range(4)])

            h_transposes("hT", 0)
            p = 0

            def proj(c, half):
                keys = [("proj", c, tt) for tt in range(TT)]
                natural_panel(2 * c + half, keys, hT_hi, hT_lo, half)

            te.wait_ge(h_lo_done, 2 * TT)
            proj(C_IDX, 0)
            proj(C_IDX, 1)
            proj(C_KV1, 0)
            te.wait_ge(ev["cn"], 1)
            transposes(("T_idx", 0), [p_idx[:, tt, 0:LAT] for tt in range(TT)])
            for i in range(2):
                transposes(("T_idx", 1 + i), [p_idx[:, tt, LAT + i * P:LAT + (i + 1) * P] for tt in range(TT)])
            te.wait_ge(ev["ki_dup"], 1)
            transposes(("T_idx", 3), [ki_dup[:, tt, :, :].rearrange("p r d -> p (r d)") for tt in range(TT)])
            proj(C_KV1, 1)
            proj(C_KV2, 0)
            te.wait_ge(small_loaded, 16 * 4)
            wait_drained(te, ("T_idx", 0))
            dst = open_bank(("kv_a", 0))
            for tt in range(TT):
                last = mm(dst[:, tt * P:(tt + 1) * P], cT[:, tt * P:(tt + 1) * P],
                          w_ukv[:, :, :].rearrange("p a d -> p (a d)"), start=True, stop=True)
            full(last, ("kv_a", 0))
            te.wait_ge(ev["cmp_dup"], 4)
            for i in range(4):
                t, g = divmod(i, KH)
                transposes(("cmpT", i), [cmp_dup[:, t, tt, g, :, :].rearrange("p r d -> p (r d)")
                                         for tt in range(TT)])
            te.wait_ge(ev["ks_dup"], 1)
            for g in range(KH):
                transposes(("ksT", g), [ks_dup[:, tt, g, :, :].rearrange("p r d -> p (r d)") for tt in range(TT)])
            for i in range(1, 4):
                wait_drained(te, ("T_idx", i))
            for u, (tt, h) in enumerate(INDEX_UNITS):
                rows = slice(h % 4 * ID, (h % 4 + 1) * ID)
                dst = open_bank(("index", u))
                full(mm(dst[:, 0:(tt + 1) * P], qiT[rows, h // 4, tt * P:(tt + 1) * P], kiT[rows, 0:(tt + 1) * P],
                        start=True, stop=True), ("index", u))
            proj(C_KV2, 1)
            proj(C_QB, 0)
            te.wait_ge(ev["ka_dup"], 1)
            transposes("kaT", [ka_dup[:, tt, :, :].rearrange("p r d -> p (r d)") for tt in range(TT)])
            te.wait_ge(ev["kw_dup"], 1)
            for g in range(KH):
                transposes(("kwT", g), [kw_dup[:, tt, g, :, :].rearrange("p r d -> p (r d)") for tt in range(TT)])
            te.wait_ge(phi1_loaded, 32)
            for t in range(2):
                for g in range(KH):
                    wait_drained(te, ("cmpT", KH * t + g))
                dst = open_bank(("hidden", t))
                for j in range(CMP_LEN // 2):
                    v = j // 8
                    src = cmp_in[:, t, v, :, :].rearrange("p g (c j) -> p g c j", j=8)[:, :, v:v + NCMP, j % 8]
                    last = mm(dst[:, 0:KH * NCMP], phi1[t][:, j, :], src, start=j == 0, stop=j == CMP_LEN // 2 - 1)
                full(last, ("hidden", t))
            proj(C_QB, 1)
            proj(C_QA, 0)
            te.wait_ge(ev["qb_n"], 1)
            for i in range(4):
                transposes(("qbT", i), [p_q[:, tt, i * P:(i + 1) * P] for tt in range(TT)])
            te.wait_ge(ev["gelu"], 1)
            full(mm(open_bank("kc")[0:CP * KH, 0:DH], gel_k[:, :, :].rearrange("p g c -> p (g c)"), phi2[:, 0, :],
                    start=True, stop=True), "kc")
            dst = open_bank("vc")
            for g in range(KH):
                last = mm(dst[:, g * DH:(g + 1) * DH], gel_v[:, g, :, :].rearrange("p r c -> p (r c)"),
                          phi2[:, 1, :], start=True, stop=True)
            full(last, "vc")
            proj(C_QA, 1)
            te.wait_ge(ev["kc_dup"], 1)
            transposes("kcT", [kc_dup[:, :, :].rearrange("p r d -> p (r d)")])
            te.wait_ge(ev["qa_n"], 1)
            for i in range(4):
                transposes(("qaT", i), [p_q[:, tt, i * P:(i + 1) * P] for tt in range(TT)])
            wait_drained(te, "kcT")
            for i in range(4):
                wait_drained(te, ("qbT", i))
            for i in range(4):
                pair, par = divmod(i, 2)
                rows = slice(par * DH, (par + 1) * DH)
                dst = open_bank(("cmpS", i))
                for t2 in range(2):
                    tok = slice((2 * pair + t2) * P, (2 * pair + t2 + 1) * P)
                    for hh in range(H // 2):
                        g = (2 * hh + par) // G
                        last = mm(dst[:, t2 * P + hh * CP:t2 * P + (hh + 1) * CP], qbT[rows, hh, tok],
                                  kcT[rows, g * CP:(g + 1) * CP], start=True, stop=True)
                full(last, ("cmpS", i))

            keysT = {SLC: ksT, WIN: kwT}
            for g in range(KH):
                wait_drained(te, ("ksT", g))
                wait_drained(te, ("kwT", g))
            wait_drained(te, "kaT")
            for s in range(STEPS):
                if s < NU:
                    br, tt, h = units[s]
                    w = (tt + 1) * P
                    if br == DSA and h == 0 and tt == 0:
                        for i in range(4):
                            wait_drained(te, ("qaT", i))
                    rows = slice(h % 2 * DH, (h % 2 + 1) * DH)
                    q = qaT if br == DSA else qbT
                    k = kaT[rows, 0:w] if br == DSA else keysT[br][rows, h // G, 0:w]
                    full(mm(open_bank(("S", s))[:, 0:w], q[rows, h // 2, tt * P:(tt + 1) * P], k,
                            start=True, stop=True), ("S", s))
                if s == CMP_STEP:
                    te.wait_ge(ev["cmp_p"], 1)
                    for g in range(KH):
                        transposes(("cmpPT", g), [cmp_e[:, tt2, g * G:(g + 1) * G, :].rearrange("p h c -> p (h c)")
                                                  for tt2 in range(TT)])
                    for g in range(KH):
                        wait_drained(te, ("cmpPT", g))
                    wait_drained(te, "vc")
                    for tt2 in range(TT):
                        dst = open_bank(("cmpO", tt2))
                        for g in range(KH):
                            last = mm(dst[:, g * G * DH:(g + 1) * G * DH], cmp_pT[:, g, tt2 * P:(tt2 + 1) * P],
                                      vc_diag[:, g, :, :].rearrange("p i d -> p (i d)"), start=True, stop=True)
                        full(last, ("cmpO", tt2))
                u = s - T_LAG
                if 0 <= u < NU:
                    te.wait_ge(exp_done, u + 1)
                    transposes(("PT", u), [prob[:, u % 3, j * P:(j + 1) * P] for j in range(units[u][1] + 1)])
                u = s - PV_LAG
                if 0 <= u < NU:
                    br, tt, h = units[u]
                    if u % H == 0:
                        open_bank(("O", u // H))
                    wait_drained(te, ("PT", u))
                    dst = psum[:, bank[("O", u // H)][0], h * DH:(h + 1) * DH]
                    for j in range(tt + 1):
                        v = {SLC: p_kv2[:, j, h // G * DH:(h // G + 1) * DH],
                             WIN: p_kv2[:, j, 2 * KVW + h // G * DH:2 * KVW + (h // G + 1) * DH],
                             DSA: kv_a[:, j, DH:2 * DH]}[br]
                        last = mm(dst, probT[:, u % 3, j * P:(j + 1) * P], v, start=j == 0, stop=j == tt)
                    if h == H - 1:
                        full(last, ("O", u // H))
                    else:
                        last.then_inc(pv_done, 1)
                if s == NSA_DONE + 2:
                    wait_drained(te, ("O", 2 * TT - 1))
                    for tt2 in range(TT):
                        transposes(("oT", 1, tt2), [o_b[:, tt2, k * P:(k + 1) * P] for k in range(4)])
            for tt in range(TT):
                wait_drained(te, ("O", 2 * TT + tt))
                transposes(("oT", 0, tt), [o_a[:, tt, k * P:(k + 1) * P] for k in range(4)])

            for n in range(2):
                for m in range(2):
                    p = GATE0 + 3 * (2 * n + m)
                    for half in range(2):
                        te.wait_ge(split_done, p + half + 1)
                        for i in range(4):
                            key = ("gate", n, m, i)
                            dst = open_bank(key) if half == 0 else psum[:, bank[key][0], :]
                            for k in range(4):
                                cols = slice(k * BANK + i * P, k * BANK + (i + 1) * P)
                                last = product(dst, w_hi[:, (p + half) % 2, cols], w_lo[:, (p + half) % 2, cols],
                                               hT_hi[:, 4 * half + k, :], hT_lo[:, 4 * half + k, :],
                                               start=half == 0 and k == 0, stop=half == 1 and k == 3)
                            if half:
                                full(last, key)
                        if not half:
                            last.then_inc(half_used, 1)
                    for tt in range(TT):
                        wait_drained(te, ("oT", m, tt))
                    te.wait_ge(split_done, p + 3)
                    for i in range(4):
                        key = ("up", n, m, i)
                        dst = open_bank(key)
                        for k in range(4):
                            cols = slice(k * BANK + i * P, k * BANK + (i + 1) * P)
                            last = product(dst, w_hi[:, p % 2, cols], w_lo[:, p % 2, cols], oT_hi[m][:, k, :],
                                           oT_lo[m][:, k, :], start=k == 0, stop=k == 3)
                        full(last, key)
            for n in range(2):
                for half in range(2):
                    if n == 0:
                        te.wait_ge(m_lo_done, 4 * half + 4)
                    natural_panel(OUT0 + 2 * n + half, [("out", n, tt) for tt in range(TT)], mT_hi, mT_lo, half)
            h_transposes("h2T", TT)
            te.wait_ge(h_lo_done, 4 * TT)
            with te.Fori(0, NFF1 // 4) as i:
                for k4 in range(4):
                    gg, half = divmod(k4, 2)
                    te.wait_ge(split_done, 4 * i + (FF1 + k4 + 1))
                    for j in range(4):
                        b = 4 * gg + j
                        if half == 0:
                            te.wait_ge(bank_drained[b], i + (ff1_first[b] - 1))
                        for k in range(4):
                            cols = slice(k * BANK + j * P, k * BANK + (j + 1) * P)
                            last = product(psum[:, b, :], w_hi[:, half, cols], w_lo[:, half, cols],
                                           hT_hi[:, 4 * half + k, :], hT_lo[:, 4 * half + k, :],
                                           start=half == 0 and k == 0, stop=half == 1 and k == 3)
                        if half:
                            last.then_inc(bank_full[b], 1)
                    if not half:
                        last.then_inc(half_used, 1)

            def down_panel(slot, start, stop):
                for b in range(8):
                    tt, n = divmod(b, 2)
                    dst = open_bank(("y", b)) if start else psum[:, b, :]
                    for k in range(2):
                        tok = slice(k * S + tt * P, k * S + (tt + 1) * P)
                        cols = slice(k * D + n * BANK, k * D + (n + 1) * BANK)
                        last = product(dst, a_hi[:, slot, tok], a_lo[:, slot, tok], w_hi[:, slot, cols],
                                       w_lo[:, slot, cols], start=start and k == 0, stop=stop and k == 1)
                    if stop:
                        full(last, ("y", b))
                if not stop:
                    last.then_inc(ff2_used, 1)

            for q in range(2):
                te.wait_ge(split_done, FF2 + q + 1)
                te.wait_ge(a_lo_done, q + 1)
                down_panel(q, q == 0, False)
            with te.Fori(1, NFF2 // 2 - 1) as i:
                for k in range(2):
                    te.wait_ge(split_done, 2 * i + (FF2 + k + 1))
                    te.wait_ge(a_lo_done, 2 * i + (k + 1))
                    down_panel(k, False, False)
            for k in range(2):
                q = NFF2 - 2 + k
                te.wait_ge(split_done, FF2 + q + 1)
                te.wait_ge(a_lo_done, q + 1)
                down_panel(k, False, k == 1)


_INS = ['x', 'g_mix', 'w_in', 'g_q_a', 'g_k_a', 'g_lat_a', 'w_uk_a', 'w_uv_a', 'g_q_b', 'g_kc_b', 'g_ks_b',
        'g_kw_b', 'pe_cmp_b', 'phi_k1_b', 'phi_k2_b', 'phi_v1_b', 'phi_v2_b', 'w_up_a', 'w_up_b', 'w_out', 'g_mlp',
        'w_ff1', 'w_ff2']


def kernel(**inputs):
    import numpy as np
    import concourse.bacc as bacc
    from concourse.bass_utils import run_bass_kernel_spmd

    nc = bacc.Bacc("TRN2", target_bir_lowering=False, num_devices=1)
    arrays, args = {}, []
    for name in _INS:
        a = np.ascontiguousarray(inputs[name])
        arrays[f"in_{name}"] = a
        args.append(nc.dram_tensor(f"in_{name}", a.shape, mybir.dt.from_np(a.dtype), kind="ExternalInput").ap())
    out = nc.dram_tensor("out_x", inputs["x"].shape, mybir.dt.float32, kind="ExternalOutput").ap()
    hybrid_layer(nc, *args, out)
    r = run_bass_kernel_spmd(nc, [arrays], core_ids=[0])
    return r.results[0]["out_x"]
```

```python
from contextlib import ExitStack

import concourse.bass as bass
from concourse import mybir

F32 = mybir.dt.float32
F32R = mybir.dt.float32r
ALU = mybir.AluOpType
ACT = mybir.ActivationFunctionType
AX = mybir.AxisListType

P = 128
BANK = 512
SLC_LEN, SLC_TOPN, WINDOW, TOPK_MAX = 64, 16, 512, 256
CMP_LEN, CMP_STRIDE = 32, 16
EPS = 1e-6
MASKED = 1e33
FUTURE = -3.0e38
TAKEN = -3.4e38
FILL = ((2, 2, 2, 1), (2, 2, 2, 1), (1, 1, 1, 0), (2, 2, 2, 2))
TAIL = 6
PARTS = 4
GELU_IN, GELU_CUBE = 0.7978845608028654, 0.044715


class Banks:

    def __init__(self):
        self.uses = [0] * 8
        self.at = {}

    def use(self, key, bank):
        self.uses[bank] += 1
        self.at[key] = (bank, self.uses[bank])

    def __getitem__(self, key):
        return self.at[key]


def hybrid_layer(nc, x, g_mix, w_in, g_q_a, g_k_a, g_lat_a, w_uk_a, w_uv_a, g_q_b, g_kc_b, g_ks_b, g_kw_b,
                 pe_cmp_b, phi_k1_b, phi_k2_b, phi_v1_b, phi_v2_b, w_up_a, w_up_b, w_out, g_mlp, w_ff1, w_ff2,
                 out):
    _, S, D = x.shape
    DH = g_q_a.shape[1]
    LAT = g_lat_a.shape[1]
    WA, WB = w_up_a.shape[1], w_up_b.shape[1]
    H = WA // DH
    KH = 2
    G = H // KH
    IH, ID = 8, 32
    FF = w_ff1.shape[2]
    HID = phi_k1_b.shape[2]
    TT = S // P
    KT = D // P
    NCMP = (S - CMP_LEN) // CMP_STRIDE + 1
    CP = NCMP + 1
    TOPK = min(TOPK_MAX, S // 4)
    assert S == BANK and KT == 8 and TT == 4 and H == 8 and DH == 64 and LAT == P and HID == P and CP == 32
    assert min(SLC_TOPN, S // SLC_LEN) == S // SLC_LEN and WINDOW >= S and TOPK == P and WA == WB == 4 * P
    KVW = KH * DH

    Q_A = 0
    IDX = WA
    Q_B = IDX + LAT + IH * ID + ID + IH
    KV = Q_B + WB
    GATE_M = KV + 6 * KVW + 3 * H
    C_IDX, C_KV1, C_KV2, C_QB, C_QA = range(5)
    PROJ = [(IDX, Q_B - IDX), (KV, 3 * KVW), (KV + 3 * KVW, 3 * KVW + 3 * H), (Q_B, WB), (Q_A, WA)]

    def ktiles(w, n=None):
        return w.rearrange("(k p) n -> p k n", p=P)

    w_in_k, w_ff1_k, w_ff2_k = ktiles(w_in[0]), ktiles(w_ff1[0]), ktiles(w_ff2[0])
    w_out_k = ktiles(w_out[0])

    panels = []
    for c0, n in PROJ:
        panels += [(w_in_k[:, 4 * hf:4 * hf + 4, c0:c0 + n], 4, n) for hf in range(2)]
    TILE0 = len(panels)
    tiles = []
    for m in (1, 0):
        for i in range(KT):
            if i % 2 == 0:
                c0 = GATE_M + m * D + i * P
                panels.append((w_in_k[:, :, c0:c0 + 2 * P], KT, 2 * P))
            tiles.append(("gate", m, i, len(panels) - 1, KT, i % 2 * P))
    for m in (1, 0):
        up_k = ktiles((w_up_a, w_up_b)[m][0])
        for i in range(KT):
            if i % 4 == 0:
                panels.append((up_k[:, :, i * P:(i + 4) * P], 4, BANK))
            tiles.append(("up", m, i, len(panels) - 1, 4, i % 4 * P))
    tile_at = {tile[:3]: t for t, tile in enumerate(tiles)}
    OUT0 = len(panels)
    for n in range(2):
        panels += [(w_out_k[:, 4 * hf:4 * hf + 4, n * BANK:(n + 1) * BANK], 4, BANK) for hf in range(2)]
    FF1 = len(panels)
    NFF1 = 2 * FF // BANK
    FF2 = FF1 + NFF1
    NFF2 = FF // P // 2
    assert FF1 % 2 == 0 and NFF1 % 4 == 0 and NFF2 % 2 == 0

    SLC, WIN, DSA = range(3)
    units = [(br, tt, h) for br in (SLC, WIN, DSA) for tt in range(TT) for h in range(H)]
    NU = len(units)
    T_LAG, PV_LAG = 2, 3

    script = []

    def step(*what):
        script.append(what)

    atoms = [(t, k) for t, tile in enumerate(tiles) for k in range(tile[4])]
    UP_A_ATOM = min(i for i, (t, _) in enumerate(atoms) if t == tile_at[("up", 0, 0)])
    next_atom = 0
    parts = []

    def fill(n, until=UP_A_ATOM):
        nonlocal next_atom
        for _ in range(min(n, until - next_atom)):
            t, k = atoms[next_atom]
            next_atom += 1
            p = tiles[t][3]
            while any(part[0] <= p for part in parts):
                step("split", *parts.pop(0))
            step("tile", t, k)
            if k == tiles[t][4] - 1 and (t + 1 == len(tiles) or tiles[t + 1][3] != p):
                parts.extend((p + 2, i) for i in range(PARTS))

    SIGMOID_B = 2 * TT * H + 2
    rounds = [(tt, k) for tt in range(TT - 1, 0, -1) for k in range(TOPK // 8)]
    late = {2 + 2 * tt: [("qaT", tt)] for tt in range(TT)}
    for tt in range(TT):
        s0 = (tt + 1) * H + PV_LAG + 1
        for i, kind in enumerate(("cmpS", "cmp_norm", "cmpPT", "cmpO")):
            late.setdefault(s0 + i, []).append((kind, tt))
        late.setdefault(2 * TT * H + PV_LAG + 2 + tt, []).append(("oT", 1, tt))
    for u in range(NU + PV_LAG):
        if u < NU:
            step("qk", u)
            if rounds and u // H % TT < TT - 1:
                step("topk", *rounds.pop(0))
        if 0 <= u - T_LAG < NU:
            step("pT", u - T_LAG)
        for what in late.pop(u, []):
            step(*what)
        if u == SIGMOID_B:
            step("sigmoid", 1)
            fill(8)
        fill(FILL[min(u // (TT * H), 3)][u // H % TT])
        if parts:
            step("split", *parts.pop(0))
        if u >= PV_LAG:
            step("pv", u - PV_LAG)
            if u - PV_LAG == NU - 1:
                for tt in range(TT - 1):
                    step("oT", 0, tt)
            if u - PV_LAG == NU - 1 or u > PV_LAG and (u - PV_LAG) % H == 0:
                step("close", (u - PV_LAG) // H if u - PV_LAG == NU - 1 else (u - PV_LAG) // H - 1)
    assert not late and not rounds
    fill(TAIL)
    step("oT", 0, TT - 1)
    step("sigmoid", 0)
    fill(len(atoms))
    fill(len(atoms), len(atoms))
    for part in parts:
        step("split", *part)

    bank = Banks()
    bank.use("gains", 0)
    for tt in range(TT):
        for hf in range(2):
            bank.use(("hT", tt, hf), 2 * tt + hf)

    def use_set(prefix, s, count=4):
        for i in range(count):
            bank.use((*prefix, i), 4 * s + i % 4)

    use_set(("proj", C_IDX), 0)
    use_set(("proj", C_KV1), 1)
    use_set(("T_idx",), 0)
    use_set(("proj", C_KV2), 0)
    INDEX_UNITS = [(tt, h) for tt in range(1, TT) for h in range(IH)]
    use_set(("kv_a",), 1, 1)
    for i in range(4):
        bank.use(("cmpT", i), 4 + (1 + i) % 4)
    for g in range(KH):
        bank.use(("ksT", g), 4 + (5 + g) % 4)
    for u in range(len(INDEX_UNITS)):
        bank.use(("index", u), 4 + (7 + u) % 4)
    use_set(("proj", C_QB), 1)
    bank.use("kaT", 0)
    for g in range(KH):
        bank.use(("kwT", g), 1 + g)
    for t in range(2):
        bank.use(("hidden", t), (3 + t) % 4)
    use_set(("proj", C_QA), 0)
    for i in range(4):
        bank.use(("qbT", i), 4 + i)
    bank.use("kc", 4)
    bank.use("vc", 5)
    bank.use("kcT", 6)
    rings = {"O": (0, 1), "S": (2, 3), "PT": (4, 5), "tile": (6, 7)}
    turn = dict.fromkeys(rings, 0)

    def use_ring(ring, key):
        bank.use(key, rings[ring][turn[ring] % 2])
        turn[ring] += 1

    for kind, *a in script:
        if kind == "qk":
            use_ring("S", ("S", a[0]))
        elif kind == "cmpS":
            for par in range(2):
                use_ring("S", ("cmpS", a[0], par))
        elif kind in ("cmpPT", "cmpO", "qaT", "oT"):
            use_ring("S", (kind, *a))
        elif kind == "pT":
            use_ring("PT", ("PT", a[0]))
        elif kind == "pv" and a[0] % H == 0:
            use_ring("O", ("O", a[0] // H))
        elif kind == "tile" and a[1] == 0:
            use_ring("tile", ("tile", a[0]))
    for n in range(2):
        use_set(("out", n), n)
    for tt in range(TT):
        for hf in range(2):
            bank.use(("h2T", tt, hf), 2 * (tt % 2) + hf)
    ff1_first = []
    for b in range(8):
        bank.use(("ff1", b), b)
        ff1_first.append(bank[("ff1", b)][1])
        for _ in range(FF // P // 8 - 1):
            bank.use(("ff1 later", b), b)
    for b in range(8):
        bank.use(("y", b), b)

    released = {}
    halves = 0
    for c in range(5):
        halves += 1
        released[2 * c], released[2 * c + 1] = ("half", halves), ("full", ("proj", c, 3))
    for t, tile in enumerate(tiles):
        released[tile[3]] = ("full", ("tile", t))
    for n in range(2):
        halves += 1
        released[OUT0 + 2 * n], released[OUT0 + 2 * n + 1] = ("half", halves), ("full", ("out", n, 3))
    HALVES_FF1 = halves

    with ExitStack() as ctx:
        def sem(name):
            return ctx.enter_context(nc.semaphore(name))

        psum = ctx.enter_context(nc.psum_tensor("psum", [P, 8, BANK], F32))
        base = (nc.sbuf_base + 511) // 512 * 512
        names = set()

        def place(name, shape, at, dt=F32):
            assert name not in names
            names.add(name)
            return nc.alloc_sbuf_tensor_at(name, shape, dt, offset=base + at)

        K = 1024
        stage = place("stage", [P, 2, 2048], 0)
        w_hi = place("w_hi", [P, 2, 2048], 16 * K, F32R)
        w_lo = place("w_lo", [P, 2, 2048], 32 * K, F32R)
        hT_hi = place("hT_hi", [P, KT, S], 48 * K, F32R)
        hT_lo = place("hT_lo", [P, KT, S], 64 * K, F32R)
        small = 80 * K

        def place_small(name, shape):
            nonlocal small
            n = 4
            for d in shape[1:]:
                n *= d
            t = place(name, shape, small)
            small += (n + 31) // 32 * 32
            return t

        R_GMIX, R_GMLP, R_LAT = 0, KT, 2 * KT
        R_QA, R_KA, R_QB, R_KS, R_KW, R_KC = range(2 * KT + 1, 2 * KT + 7)
        R_PE = 2 * KT + 7
        NG = R_PE + CMP_LEN // 2
        ident = place_small("ident", [P, P])
        gain_rows = place_small("gain_rows", [NG, P])
        gains = place_small("gains", [P, NG])
        dist = place_small("dist", [P, S])
        q_scale = place_small("q_scale", [P, H])
        cmp_scale = place_small("cmp_scale", [P, H * CP])
        cmp_valid = place_small("cmp_valid", [P, TT, CP])
        cmp_mask = place_small("cmp_mask", [P, TT, CP])
        neg_half = place_small("neg_half", [P, H * TT])
        xss = place_small("xss", [P, 2 * TT])
        xvar = place_small("xvar", [P, 2 * TT])
        xrstd = place_small("xrstd", [P, 2 * TT])
        NORMS = {}
        at = 0
        for name, n in (("c", TT), ("ks", TT * KH), ("ka", TT), ("kw", TT * KH), ("qb", TT * H), ("kc", 1),
                        ("qa", TT * H)):
            NORMS[name] = (len(NORMS) + 1, slice(at, at + n))
            at += n
        nss = place_small("nss", [P, at])
        nvar = place_small("nvar", [P, at])
        nrstd = place_small("nrstd", [P, at])
        wi = place_small("wi", [P, TT, IH])
        top8 = place_small("top8", [P, 8])
        neg_max = place_small("neg_max", [P, 4])
        row_sum = place_small("row_sum", [P, 3 * TT * H])
        row_inv = place_small("row_inv", [P, 3 * TT * H])
        gate_b = place_small("gate_b", [P, TT, 3 * H])
        cmp_max = place_small("cmp_max", [P, TT * H])
        cmp_sum = place_small("cmp_sum", [P, TT * H])
        kc = place_small("kc", [CP * KH, DH])
        kcT = place_small("kcT", [P, KH * CP])
        hid = place_small("hid", [P, 2, KH, NCMP])
        gel = place_small("gel", [P, 2, KH, NCMP])
        gel_k = place_small("gel_k", [P, KH, CP])
        phi2 = place_small("phi2", [P, 2, DH])
        w_ukv = place_small("w_ukv", [P, 2, DH])
        small = (small + 511) // 512 * 512
        hf = place("hf", [P, 2, BANK], small)
        Z = small + 4 * K
        xs = place("xs", [P, TT, D], Z + 76 * K)
        xt = place("xt", [P, TT, D], Z + 92 * K)
        p_idx = place("p_idx", [P, TT, PROJ[C_IDX][1]], Z)
        p_kv1 = place("p_kv1", [P, TT, PROJ[C_KV1][1]], Z + 7 * K)
        cmp_in = place("cmp_in", [P, 2, 2, KH, S // 2], Z + 16 * K)
        qbT = place("qbT", [P, H // 2, S], Z + 24 * K)
        p_kv2 = place("p_kv2", [P, TT, PROJ[C_KV2][1]], Z + 32 * K)
        p_q = place("p_q", [P, TT, H * DH], Z + 39 * K)
        cmp_dup = place("cmp_dup", [P, 2, TT, KH, 2, DH], Z + 47 * K)
        ks_dup = place("ks_dup", [P, TT, KH, 2, DH], Z + 55 * K)
        kw_dup = place("kw_dup", [P, TT, KH, 2, DH], Z + 59 * K)
        ka_dup = place("ka_dup", [P, TT, 2, DH], Z + 63 * K)
        ki_dup = place("ki_dup", [P, TT, G, ID], Z + 65 * K)
        qaT = place("qaT", [P, H // 2, S], Z + 67 * K)
        kaT = place("kaT", [P, S], Z + 75 * K)
        ksT = place("ksT", [P, KH, S], Z + 77 * K)
        kwT = place("kwT", [P, KH, S], Z + 81 * K)
        kv_a = place("kv_a", [P, TT, 2 * DH], Z + 85 * K)
        o_b = place("o_b", [P, TT, H * DH], Z + 87 * K)
        cT = place("cT", [P, S], Z + 89 * K)
        score_at = [None, 0, 2 * P, 5 * P]
        score = place("score", [P, 9 * P], Z + 95 * K)
        prob = place("prob", [P, 3, S], Z + 100 * K)
        probT = place("probT", [P, 2, S], Z + 106 * K)
        square = place("square", [P, TT * H * DH], Z + 100 * K)
        relu = place("relu", [P, 2, S], Z + 108 * K)
        o_a = place("o_a", [P, TT, H * DH], Z + 39 * K)
        cmp_e = place("cmp_e", [P, TT, H, CP], Z + 47 * K)
        cmp_pT = place("cmp_pT", [P, KH, S], Z + 51 * K)
        phi1 = [place(f"phi1_{i}", [P, CMP_LEN // 2, HID], Z + at * K) for i, at in ((0, 67), (1, 39))]
        qiT = place("qiT", [P, 2, S], Z + 91 * K)
        kiT = place("kiT", [P, S], Z + 87 * K)
        vc_diag = place("vc_diag", [P, KH, G, DH], Z + 13 * K)
        gel_v = place("gel_v", [P, KH, G, CP], Z + 15 * K)
        kc_dup = place("kc_dup", [CP * KH, 2, DH], Z + 38 * K + 512)
        merge = [[place(f"g{m}_{i}", [P, S], at) for i, at in enumerate(ats)] for m, ats in enumerate((
            [Z + k * K for k in (0, 2, 4, 6, 8, 10, 16, 18)],
            [Z + k * K for k in (20, 22, 57, 59, 61, 63)] + [small, small + 2 * K]))]
        oT_hi = [place(f"oT_hi{m}", [P, 4, S], Z + k * K, F32R) for m, k in enumerate((67, 24))]
        oT_lo = [place(f"oT_lo{m}", [P, 4, S], Z + k * K, F32R) for m, k in enumerate((48, 77))]
        mT_hi = place("mT_hi", [P, KT, S], Z + 32 * K, F32R)
        mT_lo = [place(f"mT_lo{i}", [P, S], Z + k * K, F32R) for i, k in enumerate((0, 2, 4, 6, 8, 10, 16, 18))]
        act = place("act", [P, FF // P, S], Z)
        a_hi = place("a_hi", [P, 2, 2 * S], Z + 64 * K, F32R)
        a_lo = place("a_lo", [P, 2, 2 * S], Z + 72 * K, F32R)
        assert base + Z + 112 * K <= nc.sbuf_usable_end

        bank_full = [sem(f"bank_full{b}") for b in range(8)]
        bank_drained = [sem(f"bank_drained{b}") for b in range(8)]
        stage_loaded = [sem(f"stage_loaded{i}") for i in range(2)]
        hi_done = sem("hi_done")
        split_done = sem("split_done")
        half_used = sem("half_used")
        ff2_used = sem("ff2_used")
        x_loaded = [sem(f"x_loaded{tt}") for tt in range(TT)]
        x_reloaded = sem("x_reloaded")
        gains_loaded = sem("gains_loaded")
        small_loaded = sem("small_loaded")
        phi1_loaded = sem("phi1_loaded")
        stored = sem("stored")
        consts = sem("consts")
        x_squared = sem("x_squared")
        x_var = sem("x_var")
        x_rstd = sem("x_rstd")
        x_scaled = sem("x_scaled")
        h_hi_done = sem("h_hi_done")
        h_lo_done = sem("h_lo_done")
        norm_squared = sem("norm_squared")
        norm_summed = sem("norm_summed")
        norm_rstd = sem("norm_rstd")
        ev_names = ["cn", "ki_dup", "cmp_dup", "ks_dup", "ka_dup", "kw_dup", "qb_n", "qa_n", "kc_dup", "gelu_in",
                    "tanh", "gelu", "gate_exp", "gate_b"]
        ev = {n: sem("ev_" + n) for n in ev_names}
        index_added = sem("index_added")
        score_masked = sem("score_masked")
        exp_done = sem("exp_done")
        pv_done = sem("pv_done")
        oT_hi_done = sem("oT_hi_done")
        sigmoids = sem("sigmoids")
        mixed = sem("mixed")
        cmp_soft_in = sem("cmp_soft_in")
        cmp_exp = sem("cmp_exp")
        cmp_p = sem("cmp_p")
        m_hi_done = sem("m_hi_done")
        m_lo_done = sem("m_lo_done")
        relu_done = sem("relu_done")
        act_done = sem("act_done")
        a_hi_done = sem("a_hi_done")
        a_lo_done = sem("a_lo_done")
        y_done = sem("y_done")
        dve_chain = sem("dve_chain")
        pool_chain = sem("pool_chain")
        act_chain = sem("act_chain")

        def chained(eng, semaphore):
            count = [0]

            def link(ins):
                count[0] += 1
                ins.then_inc(semaphore, 1)
                eng.wait_ge(semaphore, count[0])
            return link

        def wait_full(eng, key):
            b, n = bank[key]
            eng.wait_ge(bank_full[b], n)
            return psum[:, b, :]

        def wait_drained(eng, key):
            b, n = bank[key]
            eng.wait_ge(bank_drained[b], n)

        def drained(ins, key):
            ins.then_inc(bank_drained[bank[key][0]], 1)

        def wait_released(eng, p):
            kind, what = released[p]
            if kind == "half":
                eng.wait_ge(half_used, what)
            else:
                wait_full(eng, what)

        def wait_pv(eng, u):
            if u % H == H - 1:
                wait_full(eng, ("O", u // H))
            else:
                eng.wait_ge(pv_done, u + 1 - u // H)

        SPLIT_SIZE = [k * n for _, k, n in panels] + [2048, 2048]

        def panel_part(p, part):
            n = SPLIT_SIZE[p]
            if part is None:
                return slice(0, n), PARTS
            return slice(part * n // PARTS, (part + 1) * n // PARTS), 1

        def drains_probT(u):
            return "vector" if units[u][0] == DSA and u % 2 else "scalar"

        def round_oT(se, copy, m, tt):
            ps = wait_full(se, ("oT", m, tt))
            copy(oT_hi[m][:, :, tt * P:(tt + 1) * P], ps.rearrange("p (k t) -> p k t", k=4)).then_inc(oT_hi_done, 1)

        def weigh(ve, link, tt, ps, factor, key):
            o3 = ps.rearrange("p (h d) -> p h d", d=DH)
            link(nc.vector.tensor_tensor(o3, o3, factor[:, :, None].to_broadcast([P, H, DH]), ALU.mult))
            drained(nc.vector.tensor_tensor(o_b[:, tt, :], o_b[:, tt, :], ps, ALU.add), key)
            wait_drained(ve, key)

        def split_oT(ve, tt_op, m, tt):
            i = tt if m else TT + tt
            ps = wait_full(ve, ("oT", m, tt))
            ve.wait_ge(oT_hi_done, i + 1)
            tok = slice(tt * P, (tt + 1) * P)
            drained(tt_op(oT_lo[m][:, :, tok], ps.rearrange("p (k t) -> p k t", k=4),
                          oT_hi[m][:, :, tok].bitcast(F32), ALU.subtract), ("oT", m, tt))

        block = ctx.enter_context(nc.Block())

        @block.sync
        def _(sp):
            xv = x[0].rearrange("(t p) d -> p t d", p=P)
            for tt in range(TT):
                sp.dma_start(xt[:, tt, :], xv[:, tt, :]).then_inc(x_loaded[tt], 16)
                if tt == 0:
                    rows = [(R_GMIX, g_mix[0].rearrange("(k p) -> k p", p=P)),
                            (R_GMLP, g_mlp[0].rearrange("(k p) -> k p", p=P)), (R_LAT, g_lat_a)]
                    for r, g in ((R_QA, g_q_a), (R_KA, g_k_a), (R_QB, g_q_b), (R_KS, g_ks_b), (R_KW, g_kw_b),
                                 (R_KC, g_kc_b)):
                        rows += [(r, g), (r, g)]
                    rows += [(R_PE, pe_cmp_b[0].rearrange("(j a) d -> j (a d)", a=2))]
                    seen = set()
                    for r, src in rows:
                        n = src.shape[0]
                        width = src.shape[1]
                        c0 = width if r in seen else 0
                        seen.add(r)
                        sp.dma_start(gain_rows[r:r + n, c0:c0 + width], src).then_inc(gains_loaded, 16)

            def load_panel(p):
                src, k, n = panels[p]
                if p >= 2:
                    sp.wait_ge(split_done, PARTS * (p - 1))
                sp.dma_start(stage[:, p % 2, 0:k * n].rearrange("p (k n) -> p k n", k=k), src)\
                  .then_inc(stage_loaded[p % 2], 16)

            load_panel(0)
            load_panel(1)
            sp.dma_start(w_ukv[:, 0, :], w_uk_a[0]).then_inc(small_loaded, 16)
            sp.dma_start(w_ukv[:, 1, :], w_uv_a[0]).then_inc(small_loaded, 16)
            sp.dma_start(phi2[:, 0, :], phi_k2_b[0]).then_inc(small_loaded, 16)
            sp.dma_start(phi2[:, 1, :], phi_v2_b[0]).then_inc(small_loaded, 16)
            for p in range(2, 4):
                load_panel(p)
            for i, w in enumerate((phi_k1_b, phi_v1_b)):
                sp.dma_start(phi1[i][:, :, :], w[0].rearrange("(j p) h -> p j h", p=P)).then_inc(phi1_loaded, 16)
            for p in range(4, OUT0 + 2):
                load_panel(p)
            for tt in range(TT):
                wait_drained(sp, ("oT", 0, tt))
            sp.dma_start(xt[:, :, :], xv).then_inc(x_reloaded, 16)
            for p in range(OUT0 + 2, FF1):
                load_panel(p)

            def load_ff1(p, q_half, col, settled):
                sp.wait_ge(split_done, settled)
                sp.dma_start(stage[:, q_half, :].rearrange("p (k n) -> p k n", k=4),
                             w_ff1_k[:, 4 * q_half:4 * q_half + 4, col]).then_inc(stage_loaded[q_half], 16)

            for q in range(2):
                load_ff1(FF1 + q, q, slice(0, BANK), PARTS * (FF1 + q - 1))
            with sp.Fori(0, NFF1 // 2 - 1) as i:
                for hfl in range(2):
                    load_ff1(None, hfl, bass.ds(i * BANK + BANK, BANK), 2 * PARTS * i + PARTS * (FF1 + 1 + hfl))
            with sp.Fori(0, NFF2 // 2) as i:
                for k in range(2):
                    sp.wait_ge(split_done, 2 * PARTS * i + PARTS * (FF2 + k - 1))
                    sp.dma_start(stage[:, k, :].rearrange("p (k n) -> p k n", k=2),
                                 w_ff2_k[:, bass.ds(4 * i + 2 * k, 2), :]).then_inc(stage_loaded[k], 16)
            ov = out[0].rearrange("(t p) d -> p t d", p=P)
            for tt in range(TT):
                sp.wait_ge(y_done, 2 * (tt + 1))
                sp.dma_start(ov[:, tt, :], xt[:, tt, :]).then_inc(stored, 16)
            sp.wait_ge(stored, 16 * TT)

        @block.gpsimd
        def _(pool):
            link = chained(pool, pool_chain)
            link(nc.gpsimd.memset(ident[:, :], 0.0))
            nc.gpsimd.affine_select(out=ident[:, :], in_=ident[:, :], compare_op=ALU.not_equal, fill=1.0, base=0,
                                    pattern=[[-1, P]], channel_multiplier=1).then_inc(consts, 1)
            nc.gpsimd.memset(neg_half[:, :], -0.5).then_inc(consts, 1)
            pool.wait_ge(consts, 2)

            def rstd_of_x(i):
                pool.wait_ge(x_var, i + 1)
                nc.gpsimd.tensor_tensor(xrstd[:, i:i + 1], xvar[:, i:i + 1], neg_half[:, 0:1], ALU.pow)\
                    .then_inc(x_rstd, 1)

            for tt in range(TT):
                rstd_of_x(tt)
            link(nc.gpsimd.iota(dist[:, :], pattern=[[-1, S]], base=S - P, channel_multiplier=1,
                                allow_small_or_imprecise_dtypes=True))
            nc.gpsimd.affine_select(out=dist[:, S - P:S], in_=dist[:, S - P:S], compare_op=ALU.is_ge, fill=MASKED,
                                    base=0, pattern=[[-1, P]], channel_multiplier=1).then_inc(consts, 1)
            for h in range(H):
                nc.gpsimd.memset(q_scale[:, h:h + 1], -float(2 ** (h + 1)) * DH ** -0.5).then_inc(consts, 1)
                nc.gpsimd.memset(cmp_scale[:, h * CP:(h + 1) * CP], -float(2.0 ** -(h + 1))).then_inc(consts, 1)
            for t in (gel_k[:, :, :], gel_v[:, :, :, :], vc_diag[:, :, :, :]):
                nc.gpsimd.memset(t, 0.0).then_inc(consts, 1)
            link(nc.gpsimd.memset(cmp_valid[:, :, :], 1.0))
            link(nc.gpsimd.affine_select(out=cmp_valid[:, :, :], in_=cmp_valid[:, :, :], compare_op=ALU.is_ge,
                                         fill=0.0, base=1 - CMP_LEN, pattern=[[P, TT], [-CMP_STRIDE, CP]],
                                         channel_multiplier=1))
            nc.gpsimd.tensor_scalar(cmp_mask[:, :, :], cmp_valid[:, :, :], -1.0, 1e30, ALU.add, ALU.mult)\
                .then_inc(consts, 1)

            def rstd(name):
                i, cols = NORMS[name]
                rows = CP * KH if name == "kc" else P
                n = cols.stop - cols.start
                pool.wait_ge(norm_summed, i)
                nc.gpsimd.tensor_tensor(nrstd[0:rows, cols], nvar[0:rows, cols], neg_half[0:rows, 0:n], ALU.pow)\
                    .then_inc(norm_rstd, 1)

            rstd("c")
            for tt in range(TT):
                wait_drained(pool, ("proj", C_KV1, tt))
            for t in range(2):
                for d in range(2):
                    nc.gpsimd.tensor_copy(cmp_dup[:, t, :, :, d, :],
                                          p_kv1[:, :, t * KVW:(t + 1) * KVW]
                                          .rearrange("p t (g d) -> p t g d", g=KH)).then_inc(ev["cmp_dup"], 1)
            rstd("ks")
            rstd("ka")
            for tt in range(1, TT):
                pool.wait_ge(index_added, IH * tt)
                diag = score[:, score_at[tt] + tt * P:score_at[tt] + (tt + 1) * P]
                nc.gpsimd.affine_select(out=diag, in_=diag, compare_op=ALU.is_ge, fill=FUTURE, base=0,
                                        pattern=[[-1, P]], channel_multiplier=1).then_inc(score_masked, 1)
            for name in ("kw", "qb", "kc", "qa"):
                rstd(name)
            for tt in range(TT):
                rstd_of_x(TT + tt)

        CONSTS_ALL = 2 + 1 + 2 * H + 3 + 1

        @block.scalar
        def _(se):
            link = chained(se, act_chain)

            def copy(dst, src, scale=1.0):
                return nc.scalar.activation(dst, src, ACT.Copy, scale=scale)

            def round_panel(p, part=None):
                se.wait_ge(stage_loaded[p % 2], 16 * (p // 2 + 1))
                if p >= 2:
                    wait_released(se, p - 2)
                cols, count = panel_part(p, part)
                copy(w_hi[:, p % 2, cols], stage[:, p % 2, cols]).then_inc(hi_done, count)

            def round_h(key, tt, hfl):
                i = 2 * tt + hfl
                wait_drained(se, (key, tt, hfl))
                copy(hT_hi[:, 4 * hfl:4 * hfl + 4, tt * P:(tt + 1) * P],
                     hf[:, i % 2, :].rearrange("p (k t) -> p k t", k=4)).then_inc(h_hi_done, 1)

            def squares(name, src, dst):
                i, _ = NORMS[name]
                if i >= 2:
                    se.wait_ge(norm_summed, i - 1)
                nc.scalar.activation(dst, src, ACT.Square).then_inc(norm_squared, 1)

            def drain_proj(c, dst):
                for tt in range(TT):
                    ps = wait_full(se, ("proj", c, tt))
                    drained(copy(dst[:, tt, :], ps[:, 0:PROJ[c][1]]), ("proj", c, tt))

            def drain_T(key, dst, gain=None):
                ps = wait_full(se, key)
                scale = 1.0 if gain is None else gains[:, gain:gain + 1]
                drained(copy(dst, ps[:, 0:dst.shape[1]], scale), key)

            for tt in range(TT):
                se.wait_ge(x_loaded[tt], 16)
                nc.scalar.activation(xs[:, tt, :], xt[:, tt, :], ACT.Square, accum_out=xss[:, tt:tt + 1])\
                    .then_inc(x_squared, 1)
            for hfl in range(2):
                round_h("hT", 0, hfl)
            round_panel(0)
            for i in range(2, 2 * TT):
                round_h("hT", i // 2, i % 2)
            round_panel(1)
            round_panel(2)
            drain_proj(C_IDX, p_idx)
            for tt in range(TT):
                wait_drained(se, ("proj", C_IDX, tt))
            squares("c", p_idx[:, :, 0:LAT], square[:, 0:TT * LAT].rearrange("p (t n) -> p t n", t=TT))
            ki = p_idx[:, :, LAT + IH * ID:LAT + IH * ID + ID]
            copy(ki_dup[:, :, :, :], ki[:, :, None, :].to_broadcast([P, TT, G, ID])).then_inc(ev["ki_dup"], 1)
            round_panel(3)
            round_panel(4)
            se.wait_ge(gains_loaded, 16 * 16)
            se.wait_ge(bank_drained[0], 1)
            drain_T(("T_idx", 0), cT[:, :], R_LAT)
            drain_T(("T_idx", 1), qiT[:, 0, :])
            drain_T(("T_idx", 2), qiT[:, 1, :])
            drain_T(("T_idx", 3), kiT[:, :])
            round_panel(5)
            drain_proj(C_KV1, p_kv1)
            for tt in range(TT):
                wait_drained(se, ("proj", C_KV1, tt))
            squares("ks", p_kv1[:, :, 2 * KVW:3 * KVW], square[:, 0:TT * KVW].rearrange("p (t n) -> p t n", t=TT))
            round_panel(6)
            wait_drained(se, ("kv_a", 0))
            squares("ka", kv_a[:, :, 0:DH], square[:, 0:TT * DH].rearrange("p (t n) -> p t n", t=TT))
            def relu_unit(u):
                tt, h = INDEX_UNITS[u]
                w = (tt + 1) * P
                ps = wait_full(se, ("index", u))
                if u >= 2:
                    se.wait_ge(index_added, u - 1)
                drained(nc.scalar.activation(relu[:, u % 2, 0:w], ps[:, 0:w], ACT.Relu), ("index", u))

            for u in range(len(INDEX_UNITS)):
                if u == 0:
                    for g in range(KH):
                        drain_T(("ksT", g), ksT[:, g, :], R_KS)
                relu_unit(u)
            round_panel(7)
            drain_proj(C_KV2, p_kv2)
            for tt in range(TT):
                wait_drained(se, ("proj", C_KV2, tt))
            squares("kw", p_kv2[:, :, KVW:2 * KVW], square[:, 0:TT * KVW].rearrange("p (t n) -> p t n", t=TT))
            nc.scalar.activation(gate_b[:, :, :], p_kv2[:, :, 3 * KVW:], ACT.Exp, scale=-1.0)\
                .then_inc(ev["gate_exp"], 1)
            round_panel(8)
            drain_T("kaT", kaT[:, :], R_KA)
            for g in range(KH):
                drain_T(("kwT", g), kwT[:, g, :], R_KW)
            se.wait_ge(ev["gelu_in"], 1)
            nc.scalar.activation(gel[:, :, :, :], gel[:, :, :, :], ACT.Tanh, scale=GELU_IN).then_inc(ev["tanh"], 1)
            round_panel(9)
            drain_proj(C_QB, p_q)
            for tt in range(TT):
                wait_drained(se, ("proj", C_QB, tt))
            pq = p_q[:, :, :].rearrange("p t n -> p (t n)")
            squares("qb", pq, square[:, :])
            round_panel(10)
            for i in range(4):
                drain_T(("qbT", i), qbT[:, i, :], R_QB)
            wait_drained(se, "kc")
            squares("kc", kc[:, :], square[0:CP * KH, 0:DH])
            round_panel(11)
            drain_proj(C_QA, p_q)
            for tt in range(TT):
                wait_drained(se, ("proj", C_QA, tt))
            squares("qa", pq, square[:, :])
            drain_T("kcT", kcT[:, :], R_KC)

            def drain_tok(key, dst, tt, gain=None):
                n = dst.shape[1]
                ps = wait_full(se, key)[:, 0:n * P].rearrange("p (k t) -> p k t", k=n)
                scale = 1.0 if gain is None else gains[:, gain:gain + 1]
                drained(copy(dst[:, :, tt * P:(tt + 1) * P], ps, scale), key)

            for kind, *a in script:
                if kind == "qk":
                    s, = a
                    w = (units[s][1] + 1) * P
                    wait_drained(se, ("S", s))
                    nc.scalar.activation(prob[:, s % 3, 0:w], prob[:, s % 3, 0:w], ACT.Exp, scale=-1.0,
                                         bias=neg_max[:, s % 4:s % 4 + 1],
                                         accum_out=row_sum[:, s:s + 1]).then_inc(exp_done, 1)
                elif kind == "pT" and drains_probT(a[0]) == "scalar":
                    u, = a
                    w = (units[u][1] + 1) * P
                    ps = wait_full(se, ("PT", u))
                    if u >= 2:
                        wait_pv(se, u - 2)
                    drained(copy(probT[:, u % 2, 0:w], ps[:, 0:w]), ("PT", u))
                elif kind == "qaT":
                    drain_tok(("qaT", a[0]), qaT, a[0], R_QA)
                elif kind == "cmpS":
                    tt, = a
                    se.wait_ge(cmp_soft_in, tt + 1)
                    nc.scalar.activation(cmp_e[:, tt, :, :], cmp_e[:, tt, :, :], ACT.Exp).then_inc(cmp_exp, 1)
                elif kind == "cmpPT":
                    drain_tok(("cmpPT", a[0]), cmp_pT, a[0])
                elif kind == "oT":
                    round_oT(se, copy, *a)
                elif kind == "sigmoid":
                    m, = a
                    for i in range(KT):
                        t = tile_at[("gate", m, i)]
                        wait_drained(se, ("tile", t))
                        gi = merge[m][i][:, :]
                        nc.scalar.activation(gi, gi, ACT.Sigmoid).then_inc(sigmoids, 1)
                elif kind == "split":
                    round_panel(*a)
                elif kind == "tile":
                    t, k = a
                    what, m, i, _, nk, _ = tiles[t]
                    if k == nk - 1 and what == "gate":
                        ps = wait_full(se, ("tile", t))
                        drained(copy(merge[m][i][:, :], ps), ("tile", t))
                    elif k == nk - 1 and m == 0:
                        se.wait_ge(mixed, i + 1)
                        copy(mT_hi[:, i, :], merge[0][i][:, :]).then_inc(m_hi_done, 1)
            for p in range(OUT0, FF1 - 1):
                round_panel(p + 2)
            for tt in range(TT):
                wait_drained(se, ("out", 1, tt))
                nc.scalar.activation(xs[:, tt, :], xt[:, tt, :], ACT.Square,
                                     accum_out=xss[:, TT + tt:TT + tt + 1]).then_inc(x_squared, 1)
                if tt >= 1:
                    for hfl in range(2):
                        round_h("h2T", tt - 1, hfl)
            for hfl in range(2):
                round_h("h2T", TT - 1, hfl)
            round_panel(FF1 + 1)

            with se.Fori(0, NFF1 // 4) as i:
                for k in range(4):
                    b0 = 4 * (k // 2)
                    if k % 2 == 0:
                        se.wait_ge(half_used, 2 * i + (HALVES_FF1 + 1 + k // 2))
                    else:
                        se.wait_ge(bank_full[b0 + 3], i + ff1_first[b0 + 3])
                    se.wait_ge(stage_loaded[k % 2], 32 * i + 16 * ((FF1 + 2 + k) // 2 + 1))
                    copy(w_hi[:, k % 2, :], stage[:, k % 2, :]).then_inc(hi_done, PARTS)
                    if k % 2:
                        for j in range(4):
                            nc.scalar.activation(act[:, bass.ds(8 * i + (b0 + j), 1), :].rearrange("p a t -> p (a t)"),
                                                 psum[:, b0 + j, :], ACT.Relu).then_inc(bank_drained[b0 + j], 1)

            def round_act(q, pair, count):
                se.wait_ge(act_done, count)
                copy(a_hi[:, q % 2, :], act[:, pair, :].rearrange("p a t -> p (a t)")).then_inc(a_hi_done, 1)

            for q in range(2):
                round_act(q, slice(2 * q, 2 * q + 2), FF // P)
            with se.Fori(0, NFF2 // 2 - 1) as i:
                for k in range(2):
                    se.wait_ge(ff2_used, 2 * i + (k + 1))
                    se.wait_ge(stage_loaded[k], 16 * i + 16 * ((FF2 + 2 + k) // 2 + 1))
                    copy(w_hi[:, k, :], stage[:, k, :]).then_inc(hi_done, PARTS)
                    copy(a_hi[:, k, :], act[:, bass.ds(4 * i + (4 + 2 * k), 2), :].rearrange("p a t -> p (a t)"))\
                        .then_inc(a_hi_done, 1)

        @block.vector
        def _(ve):
            link = chained(ve, dve_chain)
            tt_op = nc.vector.tensor_tensor

            def split_panel(p, part=None):
                cols, count = panel_part(p, part)
                ve.wait_ge(hi_done, PARTS * (p + 1) if part is None else PARTS * p + part + 1)
                tt_op(w_lo[:, p % 2, cols], stage[:, p % 2, cols], w_hi[:, p % 2, cols].bitcast(F32), ALU.subtract)\
                    .then_inc(split_done, count)

            def scale_x(i, tt):
                ve.wait_ge(x_squared, i + 1)
                nc.vector.tensor_scalar(xvar[:, i:i + 1], xss[:, i:i + 1], 1.0 / D, EPS, ALU.mult, ALU.add)\
                    .then_inc(x_var, 1)
                ve.wait_ge(x_rstd, i + 1)
                nc.vector.tensor_scalar(xs[:, tt, :], xt[:, tt, :], xrstd[:, i:i + 1], None, ALU.mult)\
                    .then_inc(x_scaled, 1)

            def drain_h(i, tt, key, row):
                for hfl in range(2):
                    j = i + hfl
                    ps = wait_full(ve, (key, tt, hfl))
                    g = gains[:, row + 4 * hfl:row + 4 * hfl + 4]
                    if j >= 2:
                        ve.wait_ge(h_lo_done, j - 1)
                    drained(tt_op(hf[:, j % 2, :].rearrange("p (k t) -> p k t", k=4), ps.rearrange("p (k t) -> p k t", k=4),
                                  g[:, :, None].to_broadcast([P, 4, P]), ALU.mult), (key, tt, hfl))
                for hfl in range(2):
                    j = i + hfl
                    ve.wait_ge(h_hi_done, j + 1)
                    tok = slice(tt * P, (tt + 1) * P)
                    tt_op(hT_lo[:, 4 * hfl:4 * hfl + 4, tok],
                          hf[:, j % 2, :].rearrange("p (k t) -> p k t", k=4),
                          hT_hi[:, 4 * hfl:4 * hfl + 4, tok].bitcast(F32), ALU.subtract).then_inc(h_lo_done, 1)

            def norm(name, n, count, src=None):
                i, cols = NORMS[name]
                rows = CP * KH if name == "kc" else P
                ve.wait_ge(norm_squared, i)
                link(nc.vector.tensor_reduce(nss[0:rows, cols],
                                             square[0:rows, 0:count * n].rearrange("p (a n) -> p a n", n=n),
                                             AX.X, ALU.add))
                nc.vector.tensor_scalar(nvar[0:rows, cols], nss[0:rows, cols], 1.0 / n, EPS, ALU.mult, ALU.add)\
                    .then_inc(norm_summed, 1)
                ve.wait_ge(norm_rstd, i)
                return nrstd[0:rows, cols]

            ve.wait_ge(consts, 2)
            b, _ = bank["gains"]
            ps = wait_full(ve, "gains")
            drained(nc.vector.tensor_copy(gains[:, :], ps[:, 0:NG]), "gains")
            ve.wait_ge(bank_drained[b], 1)
            for tt in range(TT):
                scale_x(tt, tt)
                if tt >= 1:
                    drain_h(2 * (tt - 1), tt - 1, "hT", R_GMIX)
                if tt == 1:
                    split_panel(0)
            drain_h(2 * TT - 2, TT - 1, "hT", R_GMIX)
            split_panel(1)
            split_panel(2)
            r = norm("c", LAT, TT)
            c = p_idx[:, :, 0:LAT]
            tt_op(c, c, r[:, :, None].to_broadcast([P, TT, LAT]), ALU.mult).then_inc(ev["cn"], 1)
            link(nc.vector.tensor_scalar(wi[:, :, :], p_idx[:, :, LAT + IH * ID + ID:],
                                         float(IH ** -0.5 * ID ** -0.5), None, ALU.mult))
            split_panel(3)
            split_panel(4)
            split_panel(5)

            def scale_dup(name, dst, src):
                r = norm(name, DH, TT * KH)
                r = r.rearrange("p (t g) -> p t g", g=KH)[:, :, :, None].to_broadcast([P, TT, KH, DH])
                src = src.rearrange("p t (g d) -> p t g d", g=KH)
                link(tt_op(dst[:, :, :, 0, :], src, r, ALU.mult))
                tt_op(dst[:, :, :, 1, :], src, r, ALU.mult).then_inc(ev[name + "_dup"], 1)

            scale_dup("ks", ks_dup, p_kv1[:, :, 2 * KVW:3 * KVW])
            split_panel(6)
            ps = wait_full(ve, ("kv_a", 0))
            drained(nc.vector.tensor_copy(kv_a[:, :, :], ps.rearrange("p (t n) -> p t n", t=TT)), ("kv_a", 0))
            for i in range(4):
                t, g = divmod(i, KH)
                ps = wait_full(ve, ("cmpT", i))
                for par in range(2):
                    rows = slice(par * DH, (par + 1) * DH)
                    for v in range(2):
                        pe = gains[rows, R_PE + 8 * v:R_PE + 8 * v + 8]
                        ins = tt_op(cmp_in[rows, t, v, g, :].rearrange("p (c j) -> p c j", j=8),
                                    ps.rearrange("p (c j a) -> p c j a", j=8, a=2)[rows, :, :, par],
                                    pe[:, None, :].to_broadcast([DH, S // 16, 8]), ALU.add)
                        if par and v:
                            drained(ins, ("cmpT", i))
                        else:
                            link(ins)
            r = norm("ka", DH, TT)
            r = r[:, :, None].to_broadcast([P, TT, DH])
            link(tt_op(ka_dup[:, :, 0, :], kv_a[:, :, 0:DH], r, ALU.mult))
            tt_op(ka_dup[:, :, 1, :], kv_a[:, :, 0:DH], r, ALU.mult).then_inc(ev["ka_dup"], 1)
            for u, (tt, h) in enumerate(INDEX_UNITS):
                w = (tt + 1) * P
                dst = score[:, score_at[tt]:score_at[tt] + w]
                wait_drained(ve, ("index", u))
                if h == 0:
                    ins = nc.vector.tensor_scalar(dst, relu[:, u % 2, 0:w], wi[:, tt, h:h + 1], None, ALU.mult)
                else:
                    ve.wait_ge(index_added, u)
                    ins = nc.vector.scalar_tensor_tensor(out=dst, in0=relu[:, u % 2, 0:w], scalar=wi[:, tt, h:h + 1],
                                                         in1=dst, op0=ALU.mult, op1=ALU.add)
                ins.then_inc(index_added, 1)
            split_panel(7)
            scale_dup("kw", kw_dup, p_kv2[:, :, KVW:2 * KVW])
            ve.wait_ge(ev["gate_exp"], 1)
            link(nc.vector.tensor_scalar(gate_b[:, :, :], gate_b[:, :, :], 1.0, None, ALU.add))
            nc.vector.reciprocal(gate_b[:, :, :], gate_b[:, :, :]).then_inc(ev["gate_b"], 1)
            split_panel(8)
            for t in range(2):
                ps = wait_full(ve, ("hidden", t))
                drained(nc.vector.tensor_copy(hid[:, t, :, :].rearrange("p g c -> p (g c)"), ps[:, 0:KH * NCMP]),
                        ("hidden", t))
                wait_drained(ve, ("hidden", t))
            link(tt_op(gel[:, :, :, :], hid[:, :, :, :], hid[:, :, :, :], ALU.mult))
            link(nc.vector.tensor_scalar(gel[:, :, :, :], gel[:, :, :, :], GELU_CUBE, 1.0, ALU.mult, ALU.add))
            tt_op(gel[:, :, :, :], gel[:, :, :, :], hid[:, :, :, :], ALU.mult).then_inc(ev["gelu_in"], 1)
            ve.wait_ge(ev["tanh"], 1)
            link(nc.vector.tensor_scalar(gel[:, :, :, :], gel[:, :, :, :], 1.0, 0.5, ALU.add, ALU.mult))
            ve.wait_ge(consts, CONSTS_ALL)
            link(tt_op(gel_k[:, :, 0:NCMP], gel[:, 0, :, :], hid[:, 0, :, :], ALU.mult))
            tt_op(gel_v[:, :, :, 0:NCMP], gel[:, 1, :, None, :].to_broadcast([P, KH, G, NCMP]),
                  hid[:, 1, :, None, :].to_broadcast([P, KH, G, NCMP]), ALU.mult).then_inc(ev["gelu"], 1)
            split_panel(9)

            def scale_q(name):
                r = norm(name, DH, TT * H)
                r3 = r.rearrange("p (t h) -> p t h", h=H)
                link(tt_op(r3, r3, q_scale[:, None, :].to_broadcast([P, TT, H]), ALU.mult))
                q3 = p_q[:, :, :].rearrange("p t (h d) -> p (t h) d", d=DH)
                tt_op(q3, q3, r[:, :, None].to_broadcast([P, TT * H, DH]), ALU.mult).then_inc(ev[name + "_n"], 1)

            scale_q("qb")
            split_panel(10)
            ps = wait_full(ve, "kc")
            drained(nc.vector.tensor_copy(kc[:, :], ps[0:CP * KH, 0:DH]), "kc")
            ps = wait_full(ve, "vc")
            for i in range(G):
                rows = slice(i * CP, (i + 1) * CP)
                ins = nc.vector.tensor_copy(vc_diag[rows, :, i, :],
                                            ps[rows, 0:KH * DH].rearrange("p (g d) -> p g d", g=KH))
                if i == G - 1:
                    drained(ins, "vc")
                else:
                    link(ins)
            r = norm("kc", DH, 1)
            for d in range(2):
                ins = nc.vector.tensor_scalar(kc_dup[:, d, :], kc[:, :], r, None, ALU.mult)
                if d:
                    ins.then_inc(ev["kc_dup"], 1)
                else:
                    link(ins)
            split_panel(11)
            scale_q("qa")
            def split_merged(i):
                ve.wait_ge(m_hi_done, i + 1)
                tt_op(mT_lo[i][:, :], merge[0][i][:, :], mT_hi[:, i, :].bitcast(F32), ALU.subtract).then_inc(m_lo_done, 1)

            gates = gate_b[:, :, :].rearrange("p t (h b) -> p t h b", b=3)
            cs3 = cmp_sum[:, :].rearrange("p (t h) -> p t h", h=H)

            ve.wait_ge(score_masked, TT - 1)
            ve.wait_ge(ev["gate_b"], 1)
            for kind, *a in script:
                if kind == "qk":
                    s, = a
                    br, tt, h = units[s]
                    w = (tt + 1) * P
                    ps = wait_full(ve, ("S", s))
                    if s >= 3:
                        wait_full(ve, ("PT", s - 3))
                    if br == DSA and tt:
                        d = score[:, score_at[tt]:score_at[tt] + w]
                    else:
                        d = dist[:, S - w:S]
                    drained(nc.vector.tensor_tensor_reduce(out=prob[:, s % 3, 0:w], in0=ps[:, 0:w], in1=d,
                                                           scale=float(2.0 ** -(h + 1)), scalar=3e38, op0=ALU.add,
                                                           op1=ALU.min, accum_out=neg_max[:, s % 4:s % 4 + 1]),
                            ("S", s))
                elif kind == "topk":
                    tt, k = a
                    w = (tt + 1) * P
                    sc = score[:, score_at[tt]:score_at[tt] + w]
                    link(nc.vector.max(top8[:, :], sc))
                    link(nc.vector.match_replace(sc, top8[:, :], sc, TAKEN))
                    if k == TOPK // 8 - 1:
                        link(nc.vector.tensor_scalar(sc, sc, TAKEN, MASKED, ALU.not_equal, ALU.mult))
                        link(tt_op(sc, sc, dist[:, S - w:S], ALU.add))
                elif kind == "pT" and drains_probT(a[0]) == "vector":
                    u, = a
                    w = (units[u][1] + 1) * P
                    ps = wait_full(ve, ("PT", u))
                    wait_pv(ve, u - 2)
                    drained(nc.vector.tensor_copy(probT[:, u % 2, 0:w], ps[:, 0:w]), ("PT", u))
                elif kind == "cmpS":
                    tt, = a
                    e = cmp_e[:, tt, :, :]
                    for par in range(2):
                        ps = wait_full(ve, ("cmpS", tt, par))
                        drained(tt_op(e[:, par:H:2, :], ps[:, 0:H // 2 * CP].rearrange("p (h c) -> p h c", c=CP),
                                      cmp_scale[:, :].rearrange("p (h c) -> p h c", c=CP)[:, par:H:2, :], ALU.mult),
                                ("cmpS", tt, par))
                        wait_drained(ve, ("cmpS", tt, par))
                    link(tt_op(e, e, cmp_mask[:, tt, None, :].to_broadcast([P, H, CP]), ALU.add))
                    m = cmp_max[:, tt * H:(tt + 1) * H]
                    link(nc.vector.tensor_reduce(m, e, AX.X, ALU.max))
                    tt_op(e, e, m[:, :, None].to_broadcast([P, H, CP]), ALU.subtract).then_inc(cmp_soft_in, 1)
                elif kind == "cmp_norm":
                    tt, = a
                    e = cmp_e[:, tt, :, :]
                    ve.wait_ge(cmp_exp, tt + 1)
                    cs = cs3[:, tt, :]
                    link(nc.vector.tensor_reduce(cs, e, AX.X, ALU.add))
                    link(nc.vector.reciprocal(cs, cs))
                    link(tt_op(cs, cs, gates[:, tt, :, 0], ALU.mult))
                    tt_op(e, e, cmp_valid[:, tt, None, :].to_broadcast([P, H, CP]), ALU.mult).then_inc(cmp_p, 1)
                elif kind == "cmpO":
                    weigh(ve, link, a[0], wait_full(ve, ("cmpO", a[0])), cs3[:, a[0], :], ("cmpO", a[0]))
                elif kind == "close":
                    ti, = a
                    br, tt, _ = units[ti * H]
                    ps = wait_full(ve, ("O", ti))
                    ve.wait_ge(exp_done, (ti + 1) * H)
                    inv = row_inv[:, ti * H:(ti + 1) * H]
                    link(nc.vector.reciprocal(inv, row_sum[:, ti * H:(ti + 1) * H]))
                    if br != DSA:
                        link(tt_op(inv, inv, gates[:, tt, :, 1 + br], ALU.mult))
                    if br == WIN:
                        weigh(ve, link, tt, ps, inv, ("O", ti))
                    else:
                        o = o_a if br == DSA else o_b
                        drained(tt_op(o[:, tt, :].rearrange("p (h d) -> p h d", d=DH),
                                      ps.rearrange("p (h d) -> p h d", d=DH),
                                      inv[:, :, None].to_broadcast([P, H, DH]), ALU.mult), ("O", ti))
                        wait_drained(ve, ("O", ti))
                elif kind == "oT":
                    split_oT(ve, tt_op, *a)
                elif kind == "split":
                    split_panel(*a)
                elif kind == "tile":
                    t, k = a
                    what, m, i, _, nk, _ = tiles[t]
                    gi = merge[m][i][:, :]
                    if k == nk - 1 and what == "up":
                        ps = wait_full(ve, ("tile", t))
                        ve.wait_ge(sigmoids, i + 1 if m else KT + i + 1)
                        drained(tt_op(gi, gi, ps, ALU.mult), ("tile", t))
                        wait_drained(ve, ("tile", t))
                        if m == 0:
                            tt_op(gi, gi, merge[1][i][:, :], ALU.add).then_inc(mixed, 1)
                            if i:
                                split_merged(i - 1)
            split_merged(KT - 1)
            split_panel(OUT0 + 2)
            split_panel(OUT0 + 3)
            ve.wait_ge(x_reloaded, 16)

            def add_residual(n, tt):
                ps = wait_full(ve, ("out", n, tt))
                dst = xt[:, tt, n * BANK:(n + 1) * BANK]
                drained(tt_op(dst, dst, ps, ALU.add), ("out", n, tt))
                wait_drained(ve, ("out", n, tt))

            for tt in range(TT):
                add_residual(0, tt)
            split_panel(FF1)
            for tt in range(TT):
                add_residual(1, tt)
                scale_x(TT + tt, tt)
                if tt >= 1:
                    drain_h(2 * TT + 2 * (tt - 1), tt - 1, "h2T", R_GMLP)
            drain_h(4 * TT - 2, TT - 1, "h2T", R_GMLP)
            split_panel(FF1 + 1)
            with ve.Fori(0, NFF1 // 4) as i:
                for k in range(4):
                    b0 = 4 * (k // 2)
                    ve.wait_ge(hi_done, 4 * PARTS * i + PARTS * (FF1 + 2 + k + 1))
                    tt_op(w_lo[:, k % 2, :], stage[:, k % 2, :], w_hi[:, k % 2, :].bitcast(F32), ALU.subtract)\
                        .then_inc(split_done, PARTS)
                    if k % 2:
                        for j in range(4):
                            a = act[:, bass.ds(8 * i + (b0 + j), 1), :].rearrange("p a t -> p (a t)")
                            ve.wait_ge(bank_drained[b0 + j], i + ff1_first[b0 + j])
                            tt_op(a, a, a, ALU.mult).then_inc(act_done, 1)

            def split_act(q, pair):
                ve.wait_ge(a_hi_done, q + 1)
                tt_op(a_lo[:, q % 2, :], act[:, pair, :].rearrange("p a t -> p (a t)"),
                      a_hi[:, q % 2, :].bitcast(F32), ALU.subtract).then_inc(a_lo_done, 1)

            for q in range(2):
                split_act(q, slice(2 * q, 2 * q + 2))
            with ve.Fori(0, NFF2 // 2 - 1) as i:
                for k in range(2):
                    ve.wait_ge(hi_done, 2 * PARTS * i + PARTS * (FF2 + 2 + k + 1))
                    tt_op(w_lo[:, k, :], stage[:, k, :], w_hi[:, k, :].bitcast(F32), ALU.subtract)\
                        .then_inc(split_done, PARTS)
                    ve.wait_ge(a_hi_done, 2 * i + (k + 3))
                    tt_op(a_lo[:, k, :], act[:, bass.ds(4 * i + (4 + 2 * k), 2), :].rearrange("p a t -> p (a t)"),
                          a_hi[:, k, :].bitcast(F32), ALU.subtract).then_inc(a_lo_done, 1)
            for tt in range(TT):
                for n in range(2):
                    ps = wait_full(ve, ("y", 2 * tt + n))
                    dst = xt[:, tt, n * BANK:(n + 1) * BANK]
                    tt_op(dst, dst, ps, ALU.add).then_inc(y_done, 1)

        @block.tensor
        def _(te):
            mm = nc.tensor.matmul

            def open_bank(key):
                b, n = bank[key]
                if n >= 2:
                    te.wait_ge(bank_drained[b], n - 1)
                return psum[:, b, :]

            def full(ins, key):
                ins.then_inc(bank_full[bank[key][0]], 1)

            def product(dst, a_h, a_l, b_h, b_l, start, stop):
                mm(dst, a_h, b_h, start=start, stop=False)
                mm(dst, a_h, b_l, start=False, stop=False)
                return mm(dst, a_l, b_h, start=False, stop=stop)

            def natural_panel(p, keys, lhs_hi, lhs_lo, half):
                n = panels[p][2]
                te.wait_ge(split_done, PARTS * (p + 1))
                for tt in range(TT):
                    dst = (open_bank(keys[tt]) if half == 0 else psum[:, bank[keys[tt]][0], :])[:, 0:n]
                    tok = slice(tt * P, (tt + 1) * P)
                    for k in range(4):
                        cols = slice(k * n, (k + 1) * n)
                        last = product(dst, lhs_hi[4 * half + k][:, tok], lhs_lo[4 * half + k][:, tok],
                                       w_hi[:, p % 2, cols], w_lo[:, p % 2, cols],
                                       start=half == 0 and k == 0, stop=half == 1 and k == 3)
                    if half:
                        full(last, keys[tt])
                if not half:
                    last.then_inc(half_used, 1)

            def transposes(key, blocks):
                dst = open_bank(key)
                for i, src in enumerate(blocks):
                    rows, cols = src.shape
                    last = nc.tensor.transpose(dst[0:cols, i * rows:(i + 1) * rows], src, ident[0:rows, 0:rows])
                full(last, key)

            te.wait_ge(consts, 2)
            te.wait_ge(gains_loaded, 16 * 16)
            transposes("gains", [gain_rows[:, :]])
            def h_transposes(key, i0):
                for tt in range(TT):
                    te.wait_ge(x_scaled, i0 + tt + 1)
                    for hfl in range(2):
                        transposes((key, tt, hfl),
                                   [xs[:, tt, (4 * hfl + k) * P:(4 * hfl + k + 1) * P] for k in range(4)])

            h_transposes("hT", 0)
            p = 0

            def proj(c, half):
                keys = [("proj", c, tt) for tt in range(TT)]
                natural_panel(2 * c + half, keys, [hT_hi[:, k, :] for k in range(KT)],
                              [hT_lo[:, k, :] for k in range(KT)], half)

            te.wait_ge(h_lo_done, 2 * TT)
            proj(C_IDX, 0)
            proj(C_IDX, 1)
            proj(C_KV1, 0)
            te.wait_ge(ev["cn"], 1)
            transposes(("T_idx", 0), [p_idx[:, tt, 0:LAT] for tt in range(TT)])
            for i in range(2):
                transposes(("T_idx", 1 + i), [p_idx[:, tt, LAT + i * P:LAT + (i + 1) * P] for tt in range(TT)])
            te.wait_ge(ev["ki_dup"], 1)
            transposes(("T_idx", 3), [ki_dup[:, tt, :, :].rearrange("p r d -> p (r d)") for tt in range(TT)])
            proj(C_KV1, 1)
            proj(C_KV2, 0)
            te.wait_ge(small_loaded, 16 * 4)
            wait_drained(te, ("T_idx", 0))
            dst = open_bank(("kv_a", 0))
            for tt in range(TT):
                last = mm(dst[:, tt * P:(tt + 1) * P], cT[:, tt * P:(tt + 1) * P],
                          w_ukv[:, :, :].rearrange("p a d -> p (a d)"), start=True, stop=True)
            full(last, ("kv_a", 0))
            te.wait_ge(ev["cmp_dup"], 4)
            for i in range(4):
                t, g = divmod(i, KH)
                transposes(("cmpT", i), [cmp_dup[:, t, tt, g, :, :].rearrange("p r d -> p (r d)")
                                         for tt in range(TT)])
            te.wait_ge(ev["ks_dup"], 1)
            for g in range(KH):
                transposes(("ksT", g), [ks_dup[:, tt, g, :, :].rearrange("p r d -> p (r d)") for tt in range(TT)])
            for i in range(1, 4):
                wait_drained(te, ("T_idx", i))
            for u, (tt, h) in enumerate(INDEX_UNITS):
                rows = slice(h % 4 * ID, (h % 4 + 1) * ID)
                dst = open_bank(("index", u))
                full(mm(dst[:, 0:(tt + 1) * P], qiT[rows, h // 4, tt * P:(tt + 1) * P], kiT[rows, 0:(tt + 1) * P],
                        start=True, stop=True), ("index", u))
            proj(C_KV2, 1)
            proj(C_QB, 0)
            te.wait_ge(ev["ka_dup"], 1)
            transposes("kaT", [ka_dup[:, tt, :, :].rearrange("p r d -> p (r d)") for tt in range(TT)])
            te.wait_ge(ev["kw_dup"], 1)
            for g in range(KH):
                transposes(("kwT", g), [kw_dup[:, tt, g, :, :].rearrange("p r d -> p (r d)") for tt in range(TT)])
            te.wait_ge(phi1_loaded, 32)
            for t in range(2):
                for g in range(KH):
                    wait_drained(te, ("cmpT", KH * t + g))
                dst = open_bank(("hidden", t))
                for j in range(CMP_LEN // 2):
                    v = j // 8
                    src = cmp_in[:, t, v, :, :].rearrange("p g (c j) -> p g c j", j=8)[:, :, v:v + NCMP, j % 8]
                    last = mm(dst[:, 0:KH * NCMP], phi1[t][:, j, :], src, start=j == 0, stop=j == CMP_LEN // 2 - 1)
                full(last, ("hidden", t))
            proj(C_QB, 1)
            proj(C_QA, 0)
            te.wait_ge(ev["qb_n"], 1)
            for i in range(4):
                transposes(("qbT", i), [p_q[:, tt, i * P:(i + 1) * P] for tt in range(TT)])
            te.wait_ge(ev["gelu"], 1)
            full(mm(open_bank("kc")[0:CP * KH, 0:DH], gel_k[:, :, :].rearrange("p g c -> p (g c)"), phi2[:, 0, :],
                    start=True, stop=True), "kc")
            dst = open_bank("vc")
            for g in range(KH):
                last = mm(dst[:, g * DH:(g + 1) * DH], gel_v[:, g, :, :].rearrange("p r c -> p (r c)"),
                          phi2[:, 1, :], start=True, stop=True)
            full(last, "vc")
            proj(C_QA, 1)
            te.wait_ge(ev["kc_dup"], 1)
            transposes("kcT", [kc_dup[:, :, :].rearrange("p r d -> p (r d)")])

            wait_drained(te, "kcT")
            for i in range(4):
                wait_drained(te, ("qbT", i))
            wait_drained(te, "kaT")
            wait_drained(te, "vc")
            keysT = {SLC: ksT, WIN: kwT}
            for g_ in range(KH):
                wait_drained(te, ("ksT", g_))
                wait_drained(te, ("kwT", g_))
            for kind, *a in script:
                if kind == "qk":
                    s, = a
                    br, tt, h = units[s]
                    w = (tt + 1) * P
                    if br == DSA and h == 0:
                        wait_drained(te, ("qaT", tt))
                    rows = slice(h % 2 * DH, (h % 2 + 1) * DH)
                    q = qaT if br == DSA else qbT
                    k = kaT[rows, 0:w] if br == DSA else keysT[br][rows, h // G, 0:w]
                    full(mm(open_bank(("S", s))[:, 0:w], q[rows, h // 2, tt * P:(tt + 1) * P], k,
                            start=True, stop=True), ("S", s))
                elif kind == "pT":
                    u, = a
                    te.wait_ge(exp_done, u + 1)
                    transposes(("PT", u), [prob[:, u % 3, j * P:(j + 1) * P] for j in range(units[u][1] + 1)])
                elif kind == "pv":
                    u, = a
                    br, tt, h = units[u]
                    if h == 0:
                        open_bank(("O", u // H))
                    wait_drained(te, ("PT", u))
                    dst = psum[:, bank[("O", u // H)][0], h * DH:(h + 1) * DH]
                    for j in range(tt + 1):
                        v = {SLC: p_kv2[:, j, h // G * DH:(h // G + 1) * DH],
                             WIN: p_kv2[:, j, 2 * KVW + h // G * DH:2 * KVW + (h // G + 1) * DH],
                             DSA: kv_a[:, j, DH:2 * DH]}[br]
                        last = mm(dst, probT[:, u % 2, j * P:(j + 1) * P], v, start=j == 0, stop=j == tt)
                    if h == H - 1:
                        full(last, ("O", u // H))
                    else:
                        last.then_inc(pv_done, 1)
                elif kind == "qaT":
                    te.wait_ge(ev["qa_n"], 1)
                    transposes(("qaT", a[0]), [p_q[:, a[0], i * P:(i + 1) * P] for i in range(4)])
                elif kind == "cmpS":
                    tt, = a
                    for par in range(2):
                        rows = slice(par * DH, (par + 1) * DH)
                        dst = open_bank(("cmpS", tt, par))
                        for hh in range(H // 2):
                            cols = slice((2 * hh + par) // G * CP, (2 * hh + par) // G * CP + CP)
                            last = mm(dst[:, hh * CP:(hh + 1) * CP], qbT[rows, hh, tt * P:(tt + 1) * P],
                                      kcT[rows, cols], start=True, stop=True)
                        full(last, ("cmpS", tt, par))
                elif kind == "cmpPT":
                    tt, = a
                    te.wait_ge(cmp_p, tt + 1)
                    transposes(("cmpPT", tt), [cmp_e[:, tt, i * G:(i + 1) * G, :].rearrange("p h c -> p (h c)")
                                               for i in range(KH)])
                elif kind == "cmpO":
                    tt, = a
                    wait_drained(te, ("cmpPT", tt))
                    dst = open_bank(("cmpO", tt))
                    for i in range(KH):
                        last = mm(dst[:, i * G * DH:(i + 1) * G * DH], cmp_pT[:, i, tt * P:(tt + 1) * P],
                                  vc_diag[:, i, :, :].rearrange("p i d -> p (i d)"), start=True, stop=True)
                    full(last, ("cmpO", tt))
                elif kind == "oT":
                    m, tt = a
                    wait_drained(te, ("O", 2 * TT + tt if m == 0 else TT + tt))
                    transposes(("oT", m, tt), [(o_b if m else o_a)[:, tt, k * P:(k + 1) * P] for k in range(4)])
                elif kind == "tile":
                    t, k = a
                    what, m, i, p, nk, c0 = tiles[t]
                    if what == "up" and i == 0 and k == 0:
                        for tt in range(TT):
                            wait_drained(te, ("oT", m, tt))
                    te.wait_ge(split_done, PARTS * (p + 1))
                    dst = open_bank(("tile", t)) if k == 0 else psum[:, bank[("tile", t)][0], :]
                    n = panels[p][2]
                    cols = slice(k * n + c0, k * n + c0 + P)
                    b_hi, b_lo = (hT_hi, hT_lo) if what == "gate" else (oT_hi[m], oT_lo[m])
                    last = product(dst, w_hi[:, p % 2, cols], w_lo[:, p % 2, cols], b_hi[:, k, :], b_lo[:, k, :],
                                   start=k == 0, stop=k == nk - 1)
                    if k == nk - 1:
                        full(last, ("tile", t))
            for n in range(2):
                for half in range(2):
                    if n == 0:
                        te.wait_ge(m_lo_done, 4 * half + 4)
                    natural_panel(OUT0 + 2 * n + half, [("out", n, tt) for tt in range(TT)],
                                  [mT_hi[:, k, :] for k in range(KT)], [mT[:, :] for mT in mT_lo], half)
            h_transposes("h2T", TT)
            te.wait_ge(h_lo_done, 4 * TT)
            with te.Fori(0, NFF1 // 4) as i:
                for k4 in range(4):
                    gg, half = divmod(k4, 2)
                    te.wait_ge(split_done, 4 * PARTS * i + PARTS * (FF1 + k4 + 1))
                    for j in range(4):
                        b = 4 * gg + j
                        if half == 0:
                            te.wait_ge(bank_drained[b], i + (ff1_first[b] - 1))
                        for k in range(4):
                            cols = slice(k * BANK + j * P, k * BANK + (j + 1) * P)
                            last = product(psum[:, b, :], w_hi[:, half, cols], w_lo[:, half, cols],
                                           hT_hi[:, 4 * half + k, :], hT_lo[:, 4 * half + k, :],
                                           start=half == 0 and k == 0, stop=half == 1 and k == 3)
                        if half:
                            last.then_inc(bank_full[b], 1)
                    if not half:
                        last.then_inc(half_used, 1)

            def down_panel(slot, start, stop):
                for b in range(8):
                    tt, n = divmod(b, 2)
                    dst = open_bank(("y", b)) if start else psum[:, b, :]
                    for k in range(2):
                        tok = slice(k * S + tt * P, k * S + (tt + 1) * P)
                        cols = slice(k * D + n * BANK, k * D + (n + 1) * BANK)
                        last = product(dst, a_hi[:, slot, tok], a_lo[:, slot, tok], w_hi[:, slot, cols],
                                       w_lo[:, slot, cols], start=start and k == 0, stop=stop and k == 1)
                    if stop:
                        full(last, ("y", b))
                if not stop:
                    last.then_inc(ff2_used, 1)

            for q in range(2):
                te.wait_ge(split_done, PARTS * (FF2 + q + 1))
                te.wait_ge(a_lo_done, q + 1)
                down_panel(q, q == 0, False)
            with te.Fori(1, NFF2 // 2 - 1) as i:
                for k in range(2):
                    te.wait_ge(split_done, 2 * PARTS * i + PARTS * (FF2 + k + 1))
                    te.wait_ge(a_lo_done, 2 * i + (k + 1))
                    down_panel(k, False, False)
            for k in range(2):
                q = NFF2 - 2 + k
                te.wait_ge(split_done, PARTS * (FF2 + q + 1))
                te.wait_ge(a_lo_done, q + 1)
                down_panel(k, False, k == 1)


_INS = ['x', 'g_mix', 'w_in', 'g_q_a', 'g_k_a', 'g_lat_a', 'w_uk_a', 'w_uv_a', 'g_q_b', 'g_kc_b', 'g_ks_b',
        'g_kw_b', 'pe_cmp_b', 'phi_k1_b', 'phi_k2_b', 'phi_v1_b', 'phi_v2_b', 'w_up_a', 'w_up_b', 'w_out', 'g_mlp',
        'w_ff1', 'w_ff2']


def kernel(**inputs):
    import numpy as np
    import concourse.bacc as bacc
    from concourse.bass_utils import run_bass_kernel_spmd

    nc = bacc.Bacc("TRN2", target_bir_lowering=False, num_devices=1)
    arrays, args = {}, []
    for name in _INS:
        a = np.ascontiguousarray(inputs[name])
        arrays[f"in_{name}"] = a
        args.append(nc.dram_tensor(f"in_{name}", a.shape, mybir.dt.from_np(a.dtype), kind="ExternalInput").ap())
    out = nc.dram_tensor("out_x", inputs["x"].shape, mybir.dt.float32, kind="ExternalOutput").ap()
    hybrid_layer(nc, *args, out)
    r = run_bass_kernel_spmd(nc, [arrays], core_ids=[0])
    return r.results[0]["out_x"]
```

```python
from contextlib import ExitStack

import concourse.bass as bass
from concourse import mybir

F32 = mybir.dt.float32
F32R = mybir.dt.float32r
ALU = mybir.AluOpType
ACT = mybir.ActivationFunctionType
AX = mybir.AxisListType

P = 128
BANK = 512
SLC_LEN, SLC_TOPN, WINDOW, TOPK_MAX = 64, 16, 512, 256
CMP_LEN, CMP_STRIDE = 32, 16
EPS = 1e-6
MASKED = 1e33
FUTURE = -3.0e38
TAKEN = -3.4e38
FILL = ((2, 2, 2, 2), (2, 2, 2, 2), (1, 1, 1, 1), (2, 2, 2, 2))
SIGMOID_FILL = 10
TAIL = 8
PARTS = 4
GELU_IN, GELU_CUBE = 0.7978845608028654, 0.044715


class Banks:

    def __init__(self):
        self.uses = [0] * 8
        self.at = {}

    def use(self, key, bank):
        self.uses[bank] += 1
        self.at[key] = (bank, self.uses[bank])

    def __getitem__(self, key):
        return self.at[key]


def hybrid_layer(nc, x, g_mix, w_in, g_q_a, g_k_a, g_lat_a, w_uk_a, w_uv_a, g_q_b, g_kc_b, g_ks_b, g_kw_b,
                 pe_cmp_b, phi_k1_b, phi_k2_b, phi_v1_b, phi_v2_b, w_up_a, w_up_b, w_out, g_mlp, w_ff1, w_ff2,
                 out):
    _, S, D = x.shape
    DH = g_q_a.shape[1]
    LAT = g_lat_a.shape[1]
    WA, WB = w_up_a.shape[1], w_up_b.shape[1]
    H = WA // DH
    KH = 2
    G = H // KH
    IH, ID = 8, 32
    FF = w_ff1.shape[2]
    HID = phi_k1_b.shape[2]
    TT = S // P
    KT = D // P
    NCMP = (S - CMP_LEN) // CMP_STRIDE + 1
    CP = NCMP + 1
    TOPK = min(TOPK_MAX, S // 4)
    assert S == BANK and KT == 8 and TT == 4 and H == 8 and DH == 64 and LAT == P and HID == P and CP == 32
    assert min(SLC_TOPN, S // SLC_LEN) == S // SLC_LEN and WINDOW >= S and TOPK == P and WA == WB == 4 * P
    KVW = KH * DH

    Q_A = 0
    IDX = WA
    Q_B = IDX + LAT + IH * ID + ID + IH
    KV = Q_B + WB
    GATE_M = KV + 6 * KVW + 3 * H
    C_IDX, C_KV1, C_QB, C_KV2 = range(4)
    PROJ = [(IDX, Q_B - IDX), (KV, 3 * KVW), (Q_B, WB), (KV + 3 * KVW, 3 * KVW + 3 * H)]

    def ktiles(w, n=None):
        return w.rearrange("(k p) n -> p k n", p=P)

    w_in_k, w_ff1_k, w_ff2_k = ktiles(w_in[0]), ktiles(w_ff1[0]), ktiles(w_ff2[0])
    w_out_k = ktiles(w_out[0])

    panels = []
    for c0, n in PROJ:
        panels += [(w_in_k[:, 4 * hf:4 * hf + 4, c0:c0 + n], 4, n) for hf in range(2)]
    tiles = []

    def gate_tiles(m):
        for i in range(KT):
            if i % 2 == 0:
                c0 = GATE_M + m * D + i * P
                panels.append((w_in_k[:, :, c0:c0 + 2 * P], KT, 2 * P))
            tiles.append(("gate", m, i, len(panels) - 1, KT, i % 2 * P))

    gate_tiles(1)
    for hf in range(2):
        panels.append((w_in_k[:, :, Q_A + hf * 2 * P:Q_A + (hf + 1) * 2 * P], KT, 2 * P))
        tiles += [("qa", hf, tt, len(panels) - 1, KT // 2, 0) for tt in range(TT)]
    gate_tiles(0)
    for m in (1, 0):
        up_k = ktiles((w_up_a, w_up_b)[m][0])
        for i in range(KT):
            if i % 4 == 0:
                panels.append((up_k[:, :, i * P:(i + 4) * P], 4, BANK))
            tiles.append(("up", m, i, len(panels) - 1, 4, i % 4 * P))
    tile_at = {tile[:3]: t for t, tile in enumerate(tiles)}
    OUT0 = len(panels)
    for n in range(2):
        panels += [(w_out_k[:, 4 * hf:4 * hf + 4, n * BANK:(n + 1) * BANK], 4, BANK) for hf in range(2)]
    FF1 = len(panels)
    NFF1 = 2 * FF // BANK
    FF2 = FF1 + NFF1
    NFF2 = FF // P // 2
    assert FF1 % 2 == 0 and NFF1 % 4 == 0 and NFF2 % 2 == 0

    SLC, WIN, DSA = range(3)
    units = [(br, tt, h) for br in (SLC, WIN, DSA) for tt in range(TT) for h in range(H)]
    NU = len(units)
    T_LAG, PV_LAG = 2, 3

    script = []

    def step(*what):
        script.append(what)

    atoms = [(t, k) for t, tile in enumerate(tiles) for k in range(tile[4])]
    UP_A_ATOM = min(i for i, (t, _) in enumerate(atoms) if t == tile_at[("up", 0, 0)])
    next_atom = 0
    parts = [(2 * len(PROJ) + 1, i) for i in range(PARTS)]

    def fill(n, until=UP_A_ATOM, now=None):
        nonlocal next_atom
        for _ in range(min(n, until - next_atom)):
            t, k = atoms[next_atom]
            next_atom += 1
            p = tiles[t][3]
            while any(part[0] <= p for part in parts):
                step("split", *parts.pop(0))
            step("tile", t, k)
            if now is None and parts and k % 2:
                step("split", *parts.pop(0))
            if tiles[t][0] == "qa" and k == tiles[t][4] - 1:
                hf, tt = tiles[t][1:3]
                late.setdefault(now + 1, []).append(("qa_sum", hf, tt))
                late.setdefault(now + 3, []).append(("qa_scale", hf, tt))
                if hf:
                    late.setdefault(now + 4, []).append(("qaT", tt))
            if k == tiles[t][4] - 1 and (t + 1 == len(tiles) or tiles[t + 1][3] != p):
                parts.extend((p + 2, i) for i in range(PARTS))

    SIGMOID_B = 2 * TT * H + 2
    rounds = {tt: list(range(TOPK // 8)) for tt in range(1, TT)}
    late = {2: [("kc",)], 3: [("kw",)], 4: [("gate_b",)], 5: [("kw_dup",)],
            7: [("kcT",), ("kwT", 0)], 8: [("kwT", 1)]}
    for tt in range(TT):
        s0 = (tt + 1) * H + PV_LAG + 2
        for i, kind in enumerate(("cmpS", "cmp_norm", "cmpPT", "cmpO")):
            late.setdefault(s0 + i, []).append((kind, tt))
        late.setdefault(2 * TT * H + PV_LAG + 3 + 2 * tt, []).append(("oT", 1, tt))
    for u in range(NU + PV_LAG):
        if u < NU:
            step("qk", u)
        if 0 <= u - T_LAG < NU:
            step("pT", u - T_LAG)
        n = FILL[min(u // (TT * H), 3)][u // H % TT]
        fill(n - 1, now=u)
        for what in late.pop(u, []):
            step(*what)
        if u == SIGMOID_B:
            step("sigmoid", 1)
            fill(SIGMOID_FILL, now=u)
        fill(min(n, 1), now=u)
        if rounds.get(u // H % TT):
            step("topk", u // H % TT, rounds[u // H % TT].pop(0))
        if parts:
            step("split", *parts.pop(0))
        if u >= PV_LAG:
            step("pv", u - PV_LAG)
            if u - PV_LAG == NU - 1:
                for tt in range(TT - 1):
                    step("oT", 0, tt)
            if u - PV_LAG == NU - 1 or u > PV_LAG and (u - PV_LAG) % H == 0:
                step("close", (u - PV_LAG) // H if u - PV_LAG == NU - 1 else (u - PV_LAG) // H - 1)
    assert not late and not any(rounds.values())
    fill(TAIL)
    step("oT", 0, TT - 1)
    step("sigmoid", 0)
    fill(len(atoms))
    fill(len(atoms), len(atoms))
    for part in parts:
        step("split", *part)

    START = [("square", 0), ("square", 1), ("scale", 0), ("square", 2), ("T", 0), ("scale", 1), ("T", 1),
             ("square", 3), ("scale", 2), ("split", 0), ("chunk", 0), ("T", 2), ("chunk", 1), ("scale", 3),
             ("T", 3), ("chunk", 2), ("chunk", 3), ("split", 1)]
    RENORM = [("chunk", 0), ("square", 0), ("chunk", 1), ("square", 1), ("scale", 0), ("chunk", 2), ("square", 2),
              ("scale", 1), ("T", 0), ("chunk", 3), ("square", 3), ("scale", 2), ("T", 1), ("scale", 3), ("T", 2),
              ("T", 3)]

    bank = Banks()
    bank.use("gains", 0)
    for tt in range(TT):
        for hf in range(2):
            bank.use(("hT", tt, hf), 2 * tt + hf)

    def use_set(prefix, s, count=4):
        for i in range(count):
            bank.use((*prefix, i), 4 * s + i % 4)

    use_set(("proj", C_IDX), 0)
    bank.use("more_gains", 7)
    use_set(("proj", C_KV1), 1)
    use_set(("T_idx",), 0)
    use_set(("proj", C_QB), 0)
    INDEX_UNITS = [(tt, h) for tt in range(1, TT) for h in range(IH)]
    use_set(("kv_a",), 1, 1)
    for i in range(4):
        bank.use(("cmpT", i), 4 + (1 + i) % 4)
    for g in range(KH):
        bank.use(("ksT", g), 4 + (5 + g) % 4)
    for u in range(len(INDEX_UNITS)):
        bank.use(("index", u), 4 + (7 + u) % 4)
    use_set(("proj", C_KV2), 1)
    bank.use("kaT", 0)
    for t in range(2):
        bank.use(("hidden", t), 1 + t)
    for tt in range(TT):
        bank.use(("qbT", tt), (3 + tt) % 4)
    rings = {"O": (0, 1), "S": (2, 3), "PT": (4, 5), "tile": (6, 7)}
    turn = dict.fromkeys(rings, 0)

    def use_ring(ring, key):
        bank.use(key, rings[ring][turn[ring] % 2])
        turn[ring] += 1

    for kind, *a in script:
        if kind == "qk":
            use_ring("S", ("S", a[0]))
        elif kind == "cmpS":
            bank.use(("cmpS", a[0], 0), a[0] % 2)
            use_ring("S", ("cmpS", a[0], 1))
        elif kind in ("cmpPT", "cmpO"):
            bank.use((kind, a[0]), a[0] % 2)
        elif kind == "kc":
            bank.use("kc", 1)
            use_ring("S", "vc")
        elif kind == "kcT":
            bank.use("kcT", 1)
        elif kind == "kwT":
            bank.use(("kwT", a[0]), 1)
        elif kind in ("qaT", "oT"):
            use_ring("S", (kind, *a))
        elif kind == "pT":
            use_ring("PT", ("PT", a[0]))
        elif kind == "pv" and a[0] % H == 0:
            use_ring("O", ("O", a[0] // H))
        elif kind == "tile" and a[1] == 0:
            use_ring("tile", ("tile", a[0]))
    for n in range(2):
        use_set(("out", n), n)
    for tt in range(TT):
        for hf in range(2):
            bank.use(("h2T", tt, hf), 2 * (tt % 2) + hf)
    ff1_first = []
    for b in range(8):
        bank.use(("ff1", b), b)
        ff1_first.append(bank[("ff1", b)][1])
        for _ in range(FF // P // 8 - 1):
            bank.use(("ff1 later", b), b)
    for b in range(8):
        bank.use(("y", b), b)

    released = {}
    halves = 0
    for c in range(len(PROJ)):
        halves += 1
        released[2 * c], released[2 * c + 1] = ("half", halves), ("full", ("proj", c, 3))
    for t, tile in enumerate(tiles):
        released[tile[3]] = ("full", ("tile", t))
    for n in range(2):
        halves += 1
        released[OUT0 + 2 * n], released[OUT0 + 2 * n + 1] = ("half", halves), ("full", ("out", n, 3))
    HALVES_FF1 = halves

    with ExitStack() as ctx:
        def sem(name):
            return ctx.enter_context(nc.semaphore(name))

        psum = ctx.enter_context(nc.psum_tensor("psum", [P, 8, BANK], F32))
        base = (nc.sbuf_base + 511) // 512 * 512
        names = set()

        def place(name, shape, at, dt=F32):
            assert name not in names
            names.add(name)
            return nc.alloc_sbuf_tensor_at(name, shape, dt, offset=base + at)

        K = 1024
        stage = place("stage", [P, 2, 2048], 0)
        w_hi = place("w_hi", [P, 2, 2048], 16 * K, F32R)
        w_lo = place("w_lo", [P, 2, 2048], 32 * K, F32R)
        hT_hi = place("hT_hi", [P, KT, S], 48 * K, F32R)
        hT_lo = place("hT_lo", [P, KT, S], 64 * K, F32R)
        small = 80 * K

        def place_small(name, shape):
            nonlocal small
            n = 4
            for d in shape[1:]:
                n *= d
            t = place(name, shape, small)
            small += (n + 31) // 32 * 32
            return t

        R_GMIX, R_GMLP, R_LAT = 0, KT, 2 * KT
        R_QA, R_KA, R_QB, R_KS, R_KW, R_KC = range(2 * KT + 1, 2 * KT + 7)
        R_PE = 2 * KT + 7
        NG = R_PE + CMP_LEN // 2
        ident = place_small("ident", [P, P])
        gains = place_small("gains", [P, NG])
        dist = place_small("dist", [P, S])
        q_scale = place_small("q_scale", [P, H])
        cmp_scale = place_small("cmp_scale", [P, H * CP])
        cmp_valid = place_small("cmp_valid", [P, TT, CP])
        cmp_mask = place_small("cmp_mask", [P, TT, CP])
        neg_half = place_small("neg_half", [P, H * TT])
        xss = place_small("xss", [P, 2 * TT])
        xvar = place_small("xvar", [P, 2 * TT])
        xrstd = place_small("xrstd", [P, 2 * TT])
        NORMS = {}
        at = 0
        sizes = [("c", TT), ("ks", TT * KH), ("ka", TT)] + [(f"qb{tt}", H) for tt in range(TT)]
        sizes += [("kc", 1), ("kw", TT * KH)] + [(f"qa{hf}{tt}", H // 2) for hf in range(2) for tt in range(TT)]
        for name, n in sizes:
            NORMS[name] = (len(NORMS) + 1, slice(at, at + n))
            at += n
        nss = place_small("nss", [P, at])
        nvar = place_small("nvar", [P, at])
        nrstd = place_small("nrstd", [P, at])
        wi = place_small("wi", [P, TT, IH])
        top8 = place_small("top8", [P, 8])
        neg_max = place_small("neg_max", [P, 4])
        row_sum = place_small("row_sum", [P, 3 * TT * H])
        row_inv = place_small("row_inv", [P, 3 * TT * H])
        gate_b = place_small("gate_b", [P, TT, 3 * H])
        cmp_max = place_small("cmp_max", [P, TT * H])
        cmp_sum = place_small("cmp_sum", [P, TT * H])
        kc = place_small("kc", [CP * KH, DH])
        kcT = place_small("kcT", [P, KH * CP])
        hid = place_small("hid", [P, 2, KH, NCMP])
        gel = place_small("gel", [P, 2, KH, NCMP])
        gel_k = place_small("gel_k", [P, KH, CP])
        phi2 = place_small("phi2", [P, 2, DH])
        w_ukv = place_small("w_ukv", [P, 2, DH])
        small = (small + 511) // 512 * 512
        hf = place("hf", [P, 2, BANK], small)
        Z = small + 4 * K
        xs = place("xs", [P, TT, D], Z + 76 * K)
        xt = place("xt", [P, TT, D], Z + 92 * K)
        p_idx = place("p_idx", [P, TT, PROJ[C_IDX][1]], Z)
        p_kv1 = place("p_kv1", [P, TT, PROJ[C_KV1][1]], Z + 7 * K)
        cmp_in = place("cmp_in", [P, 2, 2, KH, S // 2], Z + 16 * K)
        qbT = place("qbT", [P, H // 2, S], Z + 24 * K)
        p_kv2 = place("p_kv2", [P, TT, PROJ[C_KV2][1]], Z + 32 * K)
        gain_rows = place("gain_rows", [R_LAT, P], Z + 39 * K)
        more_rows = place("more_rows", [NG - R_LAT, P], Z + 40 * K)
        p_q = place("p_q", [P, TT, H * DH], Z + 39 * K)
        cmp_dup = place("cmp_dup", [P, 2, TT, KH, 2, DH], Z + 47 * K)
        ks_dup = place("ks_dup", [P, TT, KH, 2, DH], Z + 55 * K)
        kw_dup = place("kw_dup", [P, TT, KH, 2, DH], Z + 59 * K)
        ka_dup = place("ka_dup", [P, TT, 2, DH], Z + 63 * K)
        ki_dup = place("ki_dup", [P, TT, G, ID], Z + 65 * K)
        qaT = place("qaT", [P, H // 2, S], Z + 67 * K)
        kaT = place("kaT", [P, S], Z + 75 * K)
        ksT = place("ksT", [P, KH, S], Z + 77 * K)
        kwT = place("kwT", [P, KH, S], Z + 81 * K)
        kv_a = place("kv_a", [P, TT, 2 * DH], Z + 85 * K)
        o_b = place("o_b", [P, TT, H * DH], Z + 87 * K)
        cT = place("cT", [P, S], Z + 89 * K)
        score_at = [None, 0, 2 * P, 5 * P]
        score = place("score", [P, 9 * P], Z + 95 * K)
        prob = place("prob", [P, 3, S], Z + 100 * K)
        probT = place("probT", [P, 2, S], Z + 106 * K)
        square = place("square", [P, TT * H * DH], Z + 100 * K)
        square_late = place("square_late", [P, S], Z + 110 * K)
        relu = place("relu", [P, 2, S], Z + 108 * K)
        o_a = place("o_a", [P, TT, H * DH], Z + 39 * K)
        cmp_e = place("cmp_e", [P, TT, H, CP], Z + 47 * K)
        cmp_pT = place("cmp_pT", [P, KH, S], Z + 51 * K)
        phi1 = [place(f"phi1_{i}", [P, CMP_LEN // 2, HID], Z + at * K) for i, at in ((0, 67), (1, 24))]
        qiT = place("qiT", [P, 2, S], Z + 91 * K)
        kiT = place("kiT", [P, S], Z + 87 * K)
        vc_diag = place("vc_diag", [P, KH, G, DH], Z + 13 * K)
        gel_v = place("gel_v", [P, KH, G, CP], Z + 15 * K)
        kc_dup = place("kc_dup", [CP * KH, 2, DH], Z + 38 * K + 512)
        merge = [[place(f"g{m}_{i}", [P, S], at) for i, at in enumerate(ats)] for m, ats in enumerate((
            [Z + k * K for k in (0, 2, 4, 6, 8, 10, 16, 18)],
            [Z + k * K for k in (20, 22, 57, 59, 61, 63)] + [small, small + 2 * K]))]
        oT_hi = [place(f"oT_hi{m}", [P, 4, S], Z + k * K, F32R) for m, k in enumerate((67, 24))]
        oT_lo = [place(f"oT_lo{m}", [P, 4, S], Z + k * K, F32R) for m, k in enumerate((48, 77))]
        mT_hi = place("mT_hi", [P, KT, S], Z + 32 * K, F32R)
        mT_lo = [place(f"mT_lo{i}", [P, S], Z + k * K, F32R) for i, k in enumerate((0, 2, 4, 6, 8, 10, 16, 18))]
        act = place("act", [P, FF // P, S], Z)
        a_hi = place("a_hi", [P, 2, 2 * S], Z + 64 * K, F32R)
        a_lo = place("a_lo", [P, 2, 2 * S], Z + 72 * K, F32R)
        assert base + Z + 112 * K <= nc.sbuf_usable_end

        bank_full = [sem(f"bank_full{b}") for b in range(8)]
        bank_drained = [sem(f"bank_drained{b}") for b in range(8)]
        stage_loaded = [sem(f"stage_loaded{i}") for i in range(2)]
        hi_done = sem("hi_done")
        split_done = sem("split_done")
        half_used = sem("half_used")
        ff2_used = sem("ff2_used")
        x_loaded = [sem(f"x_loaded{tt}") for tt in range(TT)]
        x_reloaded = sem("x_reloaded")
        gains_loaded = sem("gains_loaded")
        more_gains_loaded = sem("more_gains_loaded")
        small_loaded = sem("small_loaded")
        phi1_loaded = sem("phi1_loaded")
        stored = sem("stored")
        consts = sem("consts")
        x_squared = sem("x_squared")
        x_rstd = sem("x_rstd")
        x_scaled = sem("x_scaled")
        h_hi_done = sem("h_hi_done")
        h_lo_done = sem("h_lo_done")
        norm_squared = sem("norm_squared")
        norm_summed = sem("norm_summed")
        norm_rstd = sem("norm_rstd")
        ev_names = ["cn", "ki_dup", "cmp_dup", "ks_dup", "ka_dup", "kw_dup", "kc_dup", "gelu_in",
                    "tanh", "gelu", "gate_exp", "gate_b"]
        ev = {n: sem("ev_" + n) for n in ev_names}
        cmp_in_added = sem("cmp_in_added")
        index_added = sem("index_added")
        score_masked = sem("score_masked")
        exp_done = sem("exp_done")
        pv_done = sem("pv_done")
        oT_hi_done = sem("oT_hi_done")
        qb_scaled = sem("qb_scaled")
        qa_scaled = sem("qa_scaled")
        sigmoids = sem("sigmoids")
        mixed = sem("mixed")
        cmp_soft_in = sem("cmp_soft_in")
        cmp_exp = sem("cmp_exp")
        cmp_p = sem("cmp_p")
        m_hi_done = sem("m_hi_done")
        m_lo_done = sem("m_lo_done")
        act_done = sem("act_done")
        a_hi_done = sem("a_hi_done")
        a_lo_done = sem("a_lo_done")
        y_done = sem("y_done")
        dve_chain = sem("dve_chain")
        pool_chain = sem("pool_chain")
        act_chain = sem("act_chain")

        def chained(eng, semaphore):
            count = [0]

            def link(ins):
                count[0] += 1
                ins.then_inc(semaphore, 1)
                eng.wait_ge(semaphore, count[0])
            return link

        def wait_full(eng, key):
            b, n = bank[key]
            eng.wait_ge(bank_full[b], n)
            return psum[:, b, :]

        def wait_drained(eng, key):
            b, n = bank[key]
            eng.wait_ge(bank_drained[b], n)

        def drained(ins, key):
            ins.then_inc(bank_drained[bank[key][0]], 1)

        def wait_released(eng, p):
            kind, what = released[p]
            if kind == "half":
                eng.wait_ge(half_used, what)
            else:
                wait_full(eng, what)

        def wait_pv(eng, u):
            if u % H == H - 1:
                wait_full(eng, ("O", u // H))
            else:
                eng.wait_ge(pv_done, u + 1 - u // H)

        SPLIT_SIZE = [k * n for _, k, n in panels] + [2048, 2048]

        def panel_part(p, part):
            n = SPLIT_SIZE[p]
            if part is None:
                return slice(0, n), PARTS
            return slice(part * n // PARTS, (part + 1) * n // PARTS), 1

        def drains_probT(u):
            return "vector" if units[u][0] == DSA and u % 2 else "scalar"

        def round_oT(se, copy, m, tt):
            ps = wait_full(se, ("oT", m, tt))
            copy(oT_hi[m][:, :, tt * P:(tt + 1) * P], ps.rearrange("p (k t) -> p k t", k=4)).then_inc(oT_hi_done, 1)

        def weigh(ve, link, tt, ps, factor, key):
            o3 = ps.rearrange("p (h d) -> p h d", d=DH)
            link(nc.vector.tensor_tensor(o3, o3, factor[:, :, None].to_broadcast([P, H, DH]), ALU.mult))
            drained(nc.vector.tensor_tensor(o_b[:, tt, :], o_b[:, tt, :], ps, ALU.add), key)
            wait_drained(ve, key)

        def split_oT(ve, tt_op, m, tt):
            i = tt if m else TT + tt
            ps = wait_full(ve, ("oT", m, tt))
            ve.wait_ge(oT_hi_done, i + 1)
            tok = slice(tt * P, (tt + 1) * P)
            drained(tt_op(oT_lo[m][:, :, tok], ps.rearrange("p (k t) -> p k t", k=4),
                          oT_hi[m][:, :, tok].bitcast(F32), ALU.subtract), ("oT", m, tt))

        block = ctx.enter_context(nc.Block())

        @block.sync
        def _(sp):
            xv = x[0].rearrange("(t p) d -> p t d", p=P)

            def load_x(tt):
                sp.dma_start(xt[:, tt, :], xv[:, tt, :]).then_inc(x_loaded[tt], 16)

            def load_panel(p):
                src, k, n = panels[p]
                if p >= 2:
                    sp.wait_ge(split_done, PARTS * (p - 1))
                sp.dma_start(stage[:, p % 2, 0:k * n].rearrange("p (k n) -> p k n", k=k), src)\
                  .then_inc(stage_loaded[p % 2], 16)

            for tt in range(TT - 1):
                load_x(tt)
            load_panel(0)
            load_x(TT - 1)
            load_panel(1)
            sp.dma_start(more_rows[0:1, :], g_lat_a).then_inc(more_gains_loaded, 16)
            for r, src in ((R_QA, g_q_a), (R_KA, g_k_a), (R_QB, g_q_b), (R_KS, g_ks_b), (R_KW, g_kw_b),
                           (R_KC, g_kc_b)):
                for i in range(2):
                    sp.dma_start(more_rows[r - R_LAT:r - R_LAT + 1, i * DH:(i + 1) * DH], src)\
                        .then_inc(more_gains_loaded, 16)
            sp.dma_start(more_rows[R_PE - R_LAT:NG - R_LAT, :], pe_cmp_b[0].rearrange("(j a) d -> j (a d)", a=2))\
                .then_inc(more_gains_loaded, 16)
            sp.dma_start(w_ukv[:, 0, :], w_uk_a[0]).then_inc(small_loaded, 16)
            sp.dma_start(w_ukv[:, 1, :], w_uv_a[0]).then_inc(small_loaded, 16)
            sp.dma_start(phi2[:, 0, :], phi_k2_b[0]).then_inc(small_loaded, 16)
            sp.dma_start(phi2[:, 1, :], phi_v2_b[0]).then_inc(small_loaded, 16)
            for p in range(2, 4):
                load_panel(p)
            for i, w in enumerate((phi_k1_b, phi_v1_b)):
                sp.dma_start(phi1[i][:, :, :], w[0].rearrange("(j p) h -> p j h", p=P)).then_inc(phi1_loaded, 16)
            for p in range(4, OUT0 + 2):
                load_panel(p)
            for tt in range(TT):
                wait_drained(sp, ("oT", 0, tt))
            sp.dma_start(xt[:, :, :], xv).then_inc(x_reloaded, 16)
            for p in range(OUT0 + 2, FF1):
                load_panel(p)

            def load_ff1(p, q_half, col, settled):
                sp.wait_ge(split_done, settled)
                sp.dma_start(stage[:, q_half, :].rearrange("p (k n) -> p k n", k=4),
                             w_ff1_k[:, 4 * q_half:4 * q_half + 4, col]).then_inc(stage_loaded[q_half], 16)

            for q in range(2):
                load_ff1(FF1 + q, q, slice(0, BANK), PARTS * (FF1 + q - 1))
            with sp.Fori(0, NFF1 // 2 - 1) as i:
                for hfl in range(2):
                    load_ff1(None, hfl, bass.ds(i * BANK + BANK, BANK), 2 * PARTS * i + PARTS * (FF1 + 1 + hfl))
            with sp.Fori(0, NFF2 // 2) as i:
                for k in range(2):
                    sp.wait_ge(split_done, 2 * PARTS * i + PARTS * (FF2 + k - 1))
                    sp.dma_start(stage[:, k, :].rearrange("p (k n) -> p k n", k=2),
                                 w_ff2_k[:, bass.ds(4 * i + 2 * k, 2), :]).then_inc(stage_loaded[k], 16)
            ov = out[0].rearrange("(t p) d -> p t d", p=P)
            for tt in range(TT):
                sp.wait_ge(y_done, 2 * (tt + 1))
                sp.dma_start(ov[:, tt, :], xt[:, tt, :]).then_inc(stored, 16)
            sp.wait_ge(stored, 16 * TT)

        @block.gpsimd
        def _(pool):
            link = chained(pool, pool_chain)
            link(nc.gpsimd.memset(ident[:, :], 0.0))
            nc.gpsimd.affine_select(out=ident[:, :], in_=ident[:, :], compare_op=ALU.not_equal, fill=1.0, base=0,
                                    pattern=[[-1, P]], channel_multiplier=1).then_inc(consts, 1)
            nc.gpsimd.memset(neg_half[:, :], -0.5).then_inc(consts, 1)
            pool.wait_ge(consts, 2)

            def rstd_of_x(i):
                pool.wait_ge(x_squared, i + 1)
                link(nc.gpsimd.tensor_scalar(xvar[:, i:i + 1], xss[:, i:i + 1], 1.0 / D, EPS, ALU.mult, ALU.add))
                nc.gpsimd.tensor_tensor(xrstd[:, i:i + 1], xvar[:, i:i + 1], neg_half[:, 0:1], ALU.pow)\
                    .then_inc(x_rstd, 1)

            for tt in range(TT):
                rstd_of_x(tt)
            link(nc.gpsimd.iota(dist[:, :], pattern=[[-1, S]], base=S - P, channel_multiplier=1,
                                allow_small_or_imprecise_dtypes=True))
            nc.gpsimd.affine_select(out=dist[:, S - P:S], in_=dist[:, S - P:S], compare_op=ALU.is_ge, fill=MASKED,
                                    base=0, pattern=[[-1, P]], channel_multiplier=1).then_inc(consts, 1)
            for h in range(H):
                nc.gpsimd.memset(q_scale[:, h:h + 1], -float(2 ** (h + 1)) * DH ** -0.5).then_inc(consts, 1)
                nc.gpsimd.memset(cmp_scale[:, h * CP:(h + 1) * CP], -float(2.0 ** -(h + 1))).then_inc(consts, 1)
            for t in (gel_k[:, :, :], gel_v[:, :, :, :], vc_diag[:, :, :, :]):
                nc.gpsimd.memset(t, 0.0).then_inc(consts, 1)
            link(nc.gpsimd.memset(cmp_valid[:, :, :], 1.0))
            link(nc.gpsimd.affine_select(out=cmp_valid[:, :, :], in_=cmp_valid[:, :, :], compare_op=ALU.is_ge,
                                         fill=0.0, base=1 - CMP_LEN, pattern=[[P, TT], [-CMP_STRIDE, CP]],
                                         channel_multiplier=1))
            nc.gpsimd.tensor_scalar(cmp_mask[:, :, :], cmp_valid[:, :, :], -1.0, 1e30, ALU.add, ALU.mult)\
                .then_inc(consts, 1)

            def rstd(name):
                i, cols = NORMS[name]
                rows = CP * KH if name == "kc" else P
                n = cols.stop - cols.start
                pool.wait_ge(norm_summed, i)
                nc.gpsimd.tensor_tensor(nrstd[0:rows, cols], nvar[0:rows, cols], neg_half[0:rows, 0:n], ALU.pow)\
                    .then_inc(norm_rstd, 1)

            rstd("c")
            for tt in range(TT):
                wait_drained(pool, ("proj", C_KV1, tt))
            for t in range(2):
                for d in range(2):
                    nc.gpsimd.tensor_copy(cmp_dup[:, t, :, :, d, :],
                                          p_kv1[:, :, t * KVW:(t + 1) * KVW]
                                          .rearrange("p t (g d) -> p t g d", g=KH)).then_inc(ev["cmp_dup"], 1)
            rstd("ks")
            rstd("ka")
            for tt in range(1, TT):
                pool.wait_ge(index_added, IH * tt)
                diag = score[:, score_at[tt] + tt * P:score_at[tt] + (tt + 1) * P]
                nc.gpsimd.affine_select(out=diag, in_=diag, compare_op=ALU.is_ge, fill=FUTURE, base=0,
                                        pattern=[[-1, P]], channel_multiplier=1).then_inc(score_masked, 1)
            for name in NORMS:
                if name not in ("c", "ks", "ka"):
                    rstd(name)
            for tt in range(TT):
                rstd_of_x(TT + tt)

        CONSTS_ALL = 2 + 1 + 2 * H + 3 + 1

        @block.scalar
        def _(se):
            link = chained(se, act_chain)

            def copy(dst, src, scale=1.0):
                return nc.scalar.activation(dst, src, ACT.Copy, scale=scale)

            def round_panel(p, part=None):
                se.wait_ge(stage_loaded[p % 2], 16 * (p // 2 + 1))
                if p >= 2:
                    wait_released(se, p - 2)
                cols, count = panel_part(p, part)
                copy(w_hi[:, p % 2, cols], stage[:, p % 2, cols]).then_inc(hi_done, count)

            def round_h(key, tt, hfl):
                i = 2 * tt + hfl
                wait_drained(se, (key, tt, hfl))
                copy(hT_hi[:, 4 * hfl:4 * hfl + 4, tt * P:(tt + 1) * P],
                     hf[:, i % 2, :].rearrange("p (k t) -> p k t", k=4)).then_inc(h_hi_done, 1)

            def squares(name, src, dst):
                i, _ = NORMS[name]
                if i >= 2:
                    se.wait_ge(norm_summed, i - 1)
                nc.scalar.activation(dst, src, ACT.Square).then_inc(norm_squared, 1)

            def drain_proj(c, dst):
                for tt in range(TT):
                    ps = wait_full(se, ("proj", c, tt))
                    drained(copy(dst[:, tt, :], ps[:, 0:PROJ[c][1]]), ("proj", c, tt))

            def drain_T(key, dst, gain=None):
                ps = wait_full(se, key)
                scale = 1.0 if gain is None else gains[:, gain:gain + 1]
                drained(copy(dst, ps[:, 0:dst.shape[1]], scale), key)

            for r, src in ((R_GMIX, g_mix), (R_GMLP, g_mlp)):
                se.dma_start(gain_rows[r:r + KT, :], src[0].rearrange("(k p) -> k p", p=P)).then_inc(gains_loaded, 16)

            def square_x(i, tt):
                nc.scalar.activation(xs[:, tt, :], xt[:, tt, :], ACT.Square, accum_out=xss[:, i:i + 1])\
                    .then_inc(x_squared, 1)

            for what, tt in START:
                if what == "square":
                    se.wait_ge(x_loaded[tt], 16)
                    square_x(tt, tt)
                elif what == "T":
                    for hfl in range(2):
                        round_h("hT", tt, hfl)
                elif what == "split":
                    round_panel(tt)
            round_panel(2)
            drain_proj(C_IDX, p_idx)
            for tt in range(TT):
                wait_drained(se, ("proj", C_IDX, tt))
            squares("c", p_idx[:, :, 0:LAT], square[:, 0:TT * LAT].rearrange("p (t n) -> p t n", t=TT))
            ki = p_idx[:, :, LAT + IH * ID:LAT + IH * ID + ID]
            copy(ki_dup[:, :, :, :], ki[:, :, None, :].to_broadcast([P, TT, G, ID])).then_inc(ev["ki_dup"], 1)
            round_panel(3)
            round_panel(4)
            wait_drained(se, "more_gains")
            drain_T(("T_idx", 0), cT[:, :], R_LAT)
            drain_T(("T_idx", 1), qiT[:, 0, :])
            drain_T(("T_idx", 2), qiT[:, 1, :])
            drain_T(("T_idx", 3), kiT[:, :])
            round_panel(5)
            drain_proj(C_KV1, p_kv1)
            for tt in range(TT):
                wait_drained(se, ("proj", C_KV1, tt))
            squares("ks", p_kv1[:, :, 2 * KVW:3 * KVW], square[:, 0:TT * KVW].rearrange("p (t n) -> p t n", t=TT))
            wait_drained(se, ("kv_a", 0))
            squares("ka", kv_a[:, :, 0:DH], square[:, 0:TT * DH].rearrange("p (t n) -> p t n", t=TT))
            round_panel(6)

            def relu_unit(u):
                tt, h = INDEX_UNITS[u]
                w = (tt + 1) * P
                ps = wait_full(se, ("index", u))
                if u >= 2:
                    se.wait_ge(index_added, u - 1)
                drained(nc.scalar.activation(relu[:, u % 2, 0:w], ps[:, 0:w], ACT.Relu), ("index", u))

            for u in range(len(INDEX_UNITS)):
                if u == 0:
                    for g in range(KH):
                        drain_T(("ksT", g), ksT[:, g, :], R_KS)
                relu_unit(u)
            round_panel(7)
            for tt in range(TT):
                ps = wait_full(se, ("proj", C_QB, tt))
                drained(copy(p_q[:, tt, :], ps), ("proj", C_QB, tt))
                i, _ = NORMS["ka"]
                se.wait_ge(norm_summed, i)
                wait_drained(se, ("proj", C_QB, tt))
                nc.scalar.activation(square[:, tt * S:(tt + 1) * S], p_q[:, tt, :], ACT.Square)\
                    .then_inc(norm_squared, 1)
            round_panel(8)
            drain_T("kaT", kaT[:, :], R_KA)
            se.wait_ge(ev["gelu_in"], 1)
            nc.scalar.activation(gel[:, :, :, :], gel[:, :, :, :], ACT.Tanh, scale=GELU_IN).then_inc(ev["tanh"], 1)

            def drain_tok(key, dst, tt, gain=None):
                n = dst.shape[1]
                ps = wait_full(se, key)[:, 0:n * P].rearrange("p (k t) -> p k t", k=n)
                scale = 1.0 if gain is None else gains[:, gain:gain + 1]
                drained(copy(dst[:, :, tt * P:(tt + 1) * P], ps, scale), key)

            for tt in range(TT):
                drain_tok(("qbT", tt), qbT, tt, R_QB)
            drain_proj(C_KV2, p_kv2)

            for kind, *a in script:
                if kind == "qk":
                    s, = a
                    w = (units[s][1] + 1) * P
                    wait_drained(se, ("S", s))
                    nc.scalar.activation(prob[:, s % 3, 0:w], prob[:, s % 3, 0:w], ACT.Exp, scale=-1.0,
                                         bias=neg_max[:, s % 4:s % 4 + 1],
                                         accum_out=row_sum[:, s:s + 1]).then_inc(exp_done, 1)
                elif kind == "pT" and drains_probT(a[0]) == "scalar":
                    u, = a
                    w = (units[u][1] + 1) * P
                    ps = wait_full(se, ("PT", u))
                    if u >= 2:
                        wait_pv(se, u - 2)
                    drained(copy(probT[:, u % 2, 0:w], ps[:, 0:w]), ("PT", u))
                elif kind == "qaT":
                    drain_tok(("qaT", a[0]), qaT, a[0], R_QA)
                elif kind == "cmpS":
                    tt, = a
                    se.wait_ge(cmp_soft_in, tt + 1)
                    nc.scalar.activation(cmp_e[:, tt, :, :], cmp_e[:, tt, :, :], ACT.Exp).then_inc(cmp_exp, 1)
                elif kind == "cmpPT":
                    drain_tok(("cmpPT", a[0]), cmp_pT, a[0])
                elif kind == "oT":
                    round_oT(se, copy, *a)
                elif kind == "kc":
                    wait_drained(se, "kc")
                    squares("kc", kc[:, :], square_late[0:CP * KH, 0:DH])
                elif kind == "kw":
                    wait_drained(se, ("proj", C_KV2, TT - 1))
                    squares("kw", p_kv2[:, :, KVW:2 * KVW], square_late[:, :].rearrange("p (t n) -> p t n", t=TT))
                elif kind == "gate_b":
                    nc.scalar.activation(gate_b[:, :, :], p_kv2[:, :, 3 * KVW:], ACT.Exp, scale=-1.0)\
                        .then_inc(ev["gate_exp"], 1)
                elif kind == "kcT":
                    drain_T("kcT", kcT[:, :], R_KC)
                elif kind == "kwT":
                    drain_T(("kwT", a[0]), kwT[:, a[0], :], R_KW)
                elif kind == "sigmoid":
                    m, = a
                    for i in range(KT):
                        t = tile_at[("gate", m, i)]
                        wait_drained(se, ("tile", t))
                        gi = merge[m][i][:, :]
                        nc.scalar.activation(gi, gi, ACT.Sigmoid).then_inc(sigmoids, 1)
                elif kind == "split":
                    round_panel(*a)
                elif kind == "tile":
                    t, k = a
                    what, m, i, _, nk, _ = tiles[t]
                    if k == nk - 1 and what == "gate":
                        ps = wait_full(se, ("tile", t))
                        drained(copy(merge[m][i][:, :], ps), ("tile", t))
                    elif k == nk - 1 and what == "qa":
                        ps = wait_full(se, ("tile", t))
                        q = p_q[:, i, m * 2 * P:(m + 1) * 2 * P]
                        drained(copy(q, ps[:, 0:2 * P]), ("tile", t))
                        wait_drained(se, ("tile", t))
                        squares(f"qa{m}{i}", q, square_late[:, 0:2 * P])
                    elif k == nk - 1 and m == 0:
                        se.wait_ge(mixed, i + 1)
                        copy(mT_hi[:, i, :], merge[0][i][:, :]).then_inc(m_hi_done, 1)
            for p in range(OUT0, FF1 - 1):
                round_panel(p + 2)
            for what, tt in RENORM:
                if what == "square":
                    wait_drained(se, ("out", 1, tt))
                    square_x(TT + tt, tt)
                elif what == "T":
                    for hfl in range(2):
                        round_h("h2T", tt, hfl)
            round_panel(FF1 + 1)

            def up_groups(i):
                for k in range(4):
                    b0 = 4 * (k // 2)
                    if k % 2 == 0:
                        se.wait_ge(half_used, 2 * i + (HALVES_FF1 + 1 + k // 2))
                    else:
                        se.wait_ge(bank_full[b0 + 3], i + ff1_first[b0 + 3])
                    se.wait_ge(stage_loaded[k % 2], 32 * i + 16 * ((FF1 + 2 + k) // 2 + 1))
                    copy(w_hi[:, k % 2, :], stage[:, k % 2, :]).then_inc(hi_done, PARTS)
                    if k % 2:
                        for j in range(4):
                            nc.scalar.activation(act[:, bass.ds(8 * i + (b0 + j), 1), :].rearrange("p a t -> p (a t)"),
                                                 psum[:, b0 + j, :], ACT.Relu).then_inc(bank_drained[b0 + j], 1)

            def round_act(q, pair, count):
                se.wait_ge(act_done, count)
                copy(a_hi[:, q % 2, :], act[:, pair, :].rearrange("p a t -> p (a t)")).then_inc(a_hi_done, 1)

            with se.Fori(0, NFF1 // 4 - 1) as i:
                up_groups(i)
            for q in range(2):
                round_act(q, slice(2 * q, 2 * q + 2), 2 * q + 2)
            up_groups(NFF1 // 4 - 1)
            se.wait_ge(act_done, FF // P)

            with se.Fori(0, NFF2 // 2 - 1) as i:
                for k in range(2):
                    se.wait_ge(ff2_used, 2 * i + (k + 1))
                    se.wait_ge(stage_loaded[k], 16 * i + 16 * ((FF2 + 2 + k) // 2 + 1))
                    copy(w_hi[:, k, :], stage[:, k, :]).then_inc(hi_done, PARTS)
                    copy(a_hi[:, k, :], act[:, bass.ds(4 * i + (4 + 2 * k), 2), :].rearrange("p a t -> p (a t)"))\
                        .then_inc(a_hi_done, 1)

        @block.vector
        def _(ve):
            link = chained(ve, dve_chain)
            tt_op = nc.vector.tensor_tensor

            def split_panel(p, part=None):
                cols, count = panel_part(p, part)
                ve.wait_ge(hi_done, PARTS * (p + 1) if part is None else PARTS * p + part + 1)
                tt_op(w_lo[:, p % 2, cols], stage[:, p % 2, cols], w_hi[:, p % 2, cols].bitcast(F32), ALU.subtract)\
                    .then_inc(split_done, count)

            def scale_x(i, tt):
                ve.wait_ge(x_rstd, i + 1)
                nc.vector.tensor_scalar(xs[:, tt, :], xt[:, tt, :], xrstd[:, i:i + 1], None, ALU.mult)\
                    .then_inc(x_scaled, 1)

            def drain_h(i, tt, key, row):
                for hfl in range(2):
                    j = i + hfl
                    ps = wait_full(ve, (key, tt, hfl))
                    g = gains[:, row + 4 * hfl:row + 4 * hfl + 4]
                    if j >= 2:
                        ve.wait_ge(h_lo_done, j - 1)
                    drained(tt_op(hf[:, j % 2, :].rearrange("p (k t) -> p k t", k=4), ps.rearrange("p (k t) -> p k t", k=4),
                                  g[:, :, None].to_broadcast([P, 4, P]), ALU.mult), (key, tt, hfl))
                for hfl in range(2):
                    j = i + hfl
                    ve.wait_ge(h_hi_done, j + 1)
                    tok = slice(tt * P, (tt + 1) * P)
                    tt_op(hT_lo[:, 4 * hfl:4 * hfl + 4, tok],
                          hf[:, j % 2, :].rearrange("p (k t) -> p k t", k=4),
                          hT_hi[:, 4 * hfl:4 * hfl + 4, tok].bitcast(F32), ALU.subtract).then_inc(h_lo_done, 1)

            def norm_sum(name, n, squared):
                i, cols = NORMS[name]
                rows = squared.shape[0]
                ve.wait_ge(norm_squared, i)
                link(nc.vector.tensor_reduce(nss[0:rows, cols], squared.rearrange("p (a n) -> p a n", n=n),
                                             AX.X, ALU.add))
                nc.vector.tensor_scalar(nvar[0:rows, cols], nss[0:rows, cols], 1.0 / n, EPS, ALU.mult, ALU.add)\
                    .then_inc(norm_summed, 1)

            def rstd_of(name):
                i, cols = NORMS[name]
                ve.wait_ge(norm_rstd, i)
                return nrstd[0:CP * KH if name == "kc" else P, cols]

            def scale_q(name, q, heads):
                r = rstd_of(name)
                link(tt_op(r, r, q_scale[:, heads], ALU.mult))
                q3 = q.rearrange("p (h d) -> p h d", d=DH)
                return tt_op(q3, q3, r[:, :, None].to_broadcast([P, q3.shape[1], DH]), ALU.mult)

            ve.wait_ge(consts, 2)
            b, _ = bank["gains"]
            ps = wait_full(ve, "gains")
            drained(nc.vector.tensor_copy(gains[:, 0:R_LAT], ps[:, 0:R_LAT]), "gains")
            ve.wait_ge(bank_drained[b], 1)
            for what, tt in START:
                if what == "scale":
                    scale_x(tt, tt)
                elif what == "T":
                    drain_h(2 * tt, tt, "hT", R_GMIX)
                elif what == "split":
                    split_panel(tt)
            split_panel(2)
            ps = wait_full(ve, "more_gains")
            drained(nc.vector.tensor_copy(gains[:, R_LAT:NG], ps[:, 0:NG - R_LAT]), "more_gains")
            wait_drained(ve, "more_gains")
            norm_sum("c", LAT, square[:, 0:TT * LAT])
            r = rstd_of("c")
            c = p_idx[:, :, 0:LAT]
            tt_op(c, c, r[:, :, None].to_broadcast([P, TT, LAT]), ALU.mult).then_inc(ev["cn"], 1)
            link(nc.vector.tensor_scalar(wi[:, :, :], p_idx[:, :, LAT + IH * ID + ID:],
                                         float(IH ** -0.5 * ID ** -0.5), None, ALU.mult))
            split_panel(3)
            split_panel(4)
            split_panel(5)

            def scale_dup(name, dst, src):
                r = rstd_of(name)
                r = r.rearrange("p (t g) -> p t g", g=KH)[:, :, :, None].to_broadcast([P, TT, KH, DH])
                src = src.rearrange("p t (g d) -> p t g d", g=KH)
                link(tt_op(dst[:, :, :, 0, :], src, r, ALU.mult))
                tt_op(dst[:, :, :, 1, :], src, r, ALU.mult).then_inc(ev[name + "_dup"], 1)

            norm_sum("ks", DH, square[:, 0:TT * KVW])
            scale_dup("ks", ks_dup, p_kv1[:, :, 2 * KVW:3 * KVW])
            ps = wait_full(ve, ("kv_a", 0))
            drained(nc.vector.tensor_copy(kv_a[:, :, :], ps.rearrange("p (t n) -> p t n", t=TT)), ("kv_a", 0))
            for i in range(4):
                t, g = divmod(i, KH)
                ps = wait_full(ve, ("cmpT", i))
                for par in range(2):
                    rows = slice(par * DH, (par + 1) * DH)
                    for v in range(2):
                        pe = gains[rows, R_PE + 8 * v:R_PE + 8 * v + 8]
                        ins = tt_op(cmp_in[rows, t, v, g, :].rearrange("p (c j) -> p c j", j=8),
                                    ps.rearrange("p (c j a) -> p c j a", j=8, a=2)[rows, :, :, par],
                                    pe[:, None, :].to_broadcast([DH, S // 16, 8]), ALU.add)
                        if par and v:
                            drained(ins, ("cmpT", i))
                        else:
                            ins.then_inc(cmp_in_added, 1)
            norm_sum("ka", DH, square[:, 0:TT * DH])
            r = rstd_of("ka")
            r = r[:, :, None].to_broadcast([P, TT, DH])
            link(tt_op(ka_dup[:, :, 0, :], kv_a[:, :, 0:DH], r, ALU.mult))
            tt_op(ka_dup[:, :, 1, :], kv_a[:, :, 0:DH], r, ALU.mult).then_inc(ev["ka_dup"], 1)
            split_panel(6)
            for u, (tt, h) in enumerate(INDEX_UNITS):
                w = (tt + 1) * P
                dst = score[:, score_at[tt]:score_at[tt] + w]
                wait_drained(ve, ("index", u))
                if h == 0:
                    ins = nc.vector.tensor_scalar(dst, relu[:, u % 2, 0:w], wi[:, tt, h:h + 1], None, ALU.mult)
                else:
                    ve.wait_ge(index_added, u)
                    ins = nc.vector.scalar_tensor_tensor(out=dst, in0=relu[:, u % 2, 0:w], scalar=wi[:, tt, h:h + 1],
                                                         in1=dst, op0=ALU.mult, op1=ALU.add)
                ins.then_inc(index_added, 1)
            split_panel(7)
            for tt in range(TT + 1):
                if tt < TT:
                    norm_sum(f"qb{tt}", DH, square[:, tt * S:(tt + 1) * S])
                if tt:
                    scale_q(f"qb{tt - 1}", p_q[:, tt - 1, :], slice(0, H)).then_inc(qb_scaled, 1)
            split_panel(8)
            for t in range(2):
                ps = wait_full(ve, ("hidden", t))
                drained(nc.vector.tensor_copy(hid[:, t, :, :].rearrange("p g c -> p (g c)"), ps[:, 0:KH * NCMP]),
                        ("hidden", t))
                wait_drained(ve, ("hidden", t))
            link(tt_op(gel[:, :, :, :], hid[:, :, :, :], hid[:, :, :, :], ALU.mult))
            link(nc.vector.tensor_scalar(gel[:, :, :, :], gel[:, :, :, :], GELU_CUBE, 1.0, ALU.mult, ALU.add))
            tt_op(gel[:, :, :, :], gel[:, :, :, :], hid[:, :, :, :], ALU.mult).then_inc(ev["gelu_in"], 1)
            ve.wait_ge(ev["tanh"], 1)
            link(nc.vector.tensor_scalar(gel[:, :, :, :], gel[:, :, :, :], 1.0, 0.5, ALU.add, ALU.mult))
            ve.wait_ge(consts, CONSTS_ALL)
            link(tt_op(gel_k[:, :, 0:NCMP], gel[:, 0, :, :], hid[:, 0, :, :], ALU.mult))
            tt_op(gel_v[:, :, :, 0:NCMP], gel[:, 1, :, None, :].to_broadcast([P, KH, G, NCMP]),
                  hid[:, 1, :, None, :].to_broadcast([P, KH, G, NCMP]), ALU.mult).then_inc(ev["gelu"], 1)

            def split_merged(i):
                ve.wait_ge(m_hi_done, i + 1)
                tt_op(mT_lo[i][:, :], merge[0][i][:, :], mT_hi[:, i, :].bitcast(F32), ALU.subtract).then_inc(m_lo_done, 1)

            gates = gate_b[:, :, :].rearrange("p t (h b) -> p t h b", b=3)
            cs3 = cmp_sum[:, :].rearrange("p (t h) -> p t h", h=H)

            ve.wait_ge(score_masked, TT - 1)
            for kind, *a in script:
                if kind == "qk":
                    s, = a
                    br, tt, h = units[s]
                    w = (tt + 1) * P
                    ps = wait_full(ve, ("S", s))
                    if s >= 3:
                        wait_full(ve, ("PT", s - 3))
                    if br == DSA and tt:
                        d = score[:, score_at[tt]:score_at[tt] + w]
                    else:
                        d = dist[:, S - w:S]
                    drained(nc.vector.tensor_tensor_reduce(out=prob[:, s % 3, 0:w], in0=ps[:, 0:w], in1=d,
                                                           scale=float(2.0 ** -(h + 1)), scalar=3e38, op0=ALU.add,
                                                           op1=ALU.min, accum_out=neg_max[:, s % 4:s % 4 + 1]),
                            ("S", s))
                elif kind == "topk":
                    tt, k = a
                    w = (tt + 1) * P
                    sc = score[:, score_at[tt]:score_at[tt] + w]
                    link(nc.vector.max(top8[:, :], sc))
                    link(nc.vector.match_replace(sc, top8[:, :], sc, TAKEN))
                    if k == TOPK // 8 - 1:
                        link(nc.vector.tensor_scalar(sc, sc, TAKEN, MASKED, ALU.not_equal, ALU.mult))
                        link(tt_op(sc, sc, dist[:, S - w:S], ALU.add))
                elif kind == "pT" and drains_probT(a[0]) == "vector":
                    u, = a
                    w = (units[u][1] + 1) * P
                    ps = wait_full(ve, ("PT", u))
                    wait_pv(ve, u - 2)
                    drained(nc.vector.tensor_copy(probT[:, u % 2, 0:w], ps[:, 0:w]), ("PT", u))
                elif kind == "kc":
                    ps = wait_full(ve, "kc")
                    drained(nc.vector.tensor_copy(kc[:, :], ps[0:CP * KH, 0:DH]), "kc")
                    ps = wait_full(ve, "vc")
                    for i in range(G):
                        rows = slice(i * CP, (i + 1) * CP)
                        ins = nc.vector.tensor_copy(vc_diag[rows, :, i, :],
                                                    ps[rows, 0:KH * DH].rearrange("p (g d) -> p g d", g=KH))
                        if i == G - 1:
                            drained(ins, "vc")
                        else:
                            link(ins)
                elif kind == "kw":
                    norm_sum("kc", DH, square_late[0:CP * KH, 0:DH])
                    norm_sum("kw", DH, square_late[:, :])
                elif kind == "gate_b":
                    ve.wait_ge(ev["gate_exp"], 1)
                    link(nc.vector.tensor_scalar(gate_b[:, :, :], gate_b[:, :, :], 1.0, None, ALU.add))
                    link(nc.vector.reciprocal(gate_b[:, :, :], gate_b[:, :, :]))
                elif kind == "kw_dup":
                    scale_dup("kw", kw_dup, p_kv2[:, :, KVW:2 * KVW])
                    r = rstd_of("kc")
                    link(nc.vector.tensor_scalar(kc_dup[:, 0, :], kc[:, :], r, None, ALU.mult))
                    nc.vector.tensor_scalar(kc_dup[:, 1, :], kc[:, :], r, None, ALU.mult).then_inc(ev["kc_dup"], 1)
                elif kind == "qa_sum":
                    norm_sum("qa%d%d" % (a[0], a[1]), DH, square_late[:, 0:2 * P])
                elif kind == "qa_scale":
                    hf_, tt = a
                    scale_q(f"qa{hf_}{tt}", p_q[:, tt, hf_ * 2 * P:(hf_ + 1) * 2 * P],
                            slice(hf_ * H // 2, (hf_ + 1) * H // 2)).then_inc(qa_scaled, 1)
                elif kind == "cmpS":
                    tt, = a
                    e = cmp_e[:, tt, :, :]
                    for par in range(2):
                        ps = wait_full(ve, ("cmpS", tt, par))
                        drained(tt_op(e[:, par:H:2, :], ps[:, 0:H // 2 * CP].rearrange("p (h c) -> p h c", c=CP),
                                      cmp_scale[:, :].rearrange("p (h c) -> p h c", c=CP)[:, par:H:2, :], ALU.mult),
                                ("cmpS", tt, par))
                        wait_drained(ve, ("cmpS", tt, par))
                    link(tt_op(e, e, cmp_mask[:, tt, None, :].to_broadcast([P, H, CP]), ALU.add))
                    m = cmp_max[:, tt * H:(tt + 1) * H]
                    link(nc.vector.tensor_reduce(m, e, AX.X, ALU.max))
                    tt_op(e, e, m[:, :, None].to_broadcast([P, H, CP]), ALU.subtract).then_inc(cmp_soft_in, 1)
                elif kind == "cmp_norm":
                    tt, = a
                    e = cmp_e[:, tt, :, :]
                    ve.wait_ge(cmp_exp, tt + 1)
                    cs = cs3[:, tt, :]
                    link(nc.vector.tensor_reduce(cs, e, AX.X, ALU.add))
                    link(nc.vector.reciprocal(cs, cs))
                    link(tt_op(cs, cs, gates[:, tt, :, 0], ALU.mult))
                    tt_op(e, e, cmp_valid[:, tt, None, :].to_broadcast([P, H, CP]), ALU.mult).then_inc(cmp_p, 1)
                elif kind == "cmpO":
                    weigh(ve, link, a[0], wait_full(ve, ("cmpO", a[0])), cs3[:, a[0], :], ("cmpO", a[0]))
                elif kind == "close":
                    ti, = a
                    br, tt, _ = units[ti * H]
                    ps = wait_full(ve, ("O", ti))
                    ve.wait_ge(exp_done, (ti + 1) * H)
                    inv = row_inv[:, ti * H:(ti + 1) * H]
                    link(nc.vector.reciprocal(inv, row_sum[:, ti * H:(ti + 1) * H]))
                    if br != DSA:
                        link(tt_op(inv, inv, gates[:, tt, :, 1 + br], ALU.mult))
                    if br == WIN:
                        weigh(ve, link, tt, ps, inv, ("O", ti))
                    else:
                        o = o_a if br == DSA else o_b
                        drained(tt_op(o[:, tt, :].rearrange("p (h d) -> p h d", d=DH),
                                      ps.rearrange("p (h d) -> p h d", d=DH),
                                      inv[:, :, None].to_broadcast([P, H, DH]), ALU.mult), ("O", ti))
                        wait_drained(ve, ("O", ti))
                elif kind == "oT":
                    split_oT(ve, tt_op, *a)
                elif kind == "split":
                    split_panel(*a)
                elif kind == "tile":
                    t, k = a
                    what, m, i, _, nk, _ = tiles[t]
                    gi = merge[m][i][:, :]
                    if k == nk - 1 and what == "up":
                        ps = wait_full(ve, ("tile", t))
                        ve.wait_ge(sigmoids, i + 1 if m else KT + i + 1)
                        drained(tt_op(gi, gi, ps, ALU.mult), ("tile", t))
                        wait_drained(ve, ("tile", t))
                        if m == 0:
                            tt_op(gi, gi, merge[1][i][:, :], ALU.add).then_inc(mixed, 1)
                            if i:
                                split_merged(i - 1)
            split_merged(KT - 1)
            split_panel(OUT0 + 2)
            split_panel(OUT0 + 3)
            ve.wait_ge(x_reloaded, 16)

            def add_residual(n, tt):
                ps = wait_full(ve, ("out", n, tt))
                dst = xt[:, tt, n * BANK:(n + 1) * BANK]
                drained(tt_op(dst, dst, ps, ALU.add), ("out", n, tt))
                wait_drained(ve, ("out", n, tt))

            for tt in range(TT):
                add_residual(0, tt)
            split_panel(FF1)
            for what, tt in RENORM:
                if what == "square":
                    add_residual(1, tt)
                elif what == "scale":
                    scale_x(TT + tt, tt)
                elif what == "T":
                    drain_h(2 * TT + 2 * tt, tt, "h2T", R_GMLP)
            split_panel(FF1 + 1)
            def up_groups(i):
                for k in range(4):
                    b0 = 4 * (k // 2)
                    ve.wait_ge(hi_done, 4 * PARTS * i + PARTS * (FF1 + 2 + k + 1))
                    tt_op(w_lo[:, k % 2, :], stage[:, k % 2, :], w_hi[:, k % 2, :].bitcast(F32), ALU.subtract)\
                        .then_inc(split_done, PARTS)
                    if k % 2:
                        for j in range(4):
                            a = act[:, bass.ds(8 * i + (b0 + j), 1), :].rearrange("p a t -> p (a t)")
                            ve.wait_ge(bank_drained[b0 + j], i + ff1_first[b0 + j])
                            tt_op(a, a, a, ALU.mult).then_inc(act_done, 1)

            def split_act(q, pair):
                ve.wait_ge(a_hi_done, q + 1)
                tt_op(a_lo[:, q % 2, :], act[:, pair, :].rearrange("p a t -> p (a t)"),
                      a_hi[:, q % 2, :].bitcast(F32), ALU.subtract).then_inc(a_lo_done, 1)

            with ve.Fori(0, NFF1 // 4 - 1) as i:
                up_groups(i)
            for q in range(2):
                split_act(q, slice(2 * q, 2 * q + 2))
            up_groups(NFF1 // 4 - 1)
            with ve.Fori(0, NFF2 // 2 - 1) as i:
                for k in range(2):
                    ve.wait_ge(hi_done, 2 * PARTS * i + PARTS * (FF2 + 2 + k + 1))
                    tt_op(w_lo[:, k, :], stage[:, k, :], w_hi[:, k, :].bitcast(F32), ALU.subtract)\
                        .then_inc(split_done, PARTS)
                    ve.wait_ge(a_hi_done, 2 * i + (k + 3))
                    tt_op(a_lo[:, k, :], act[:, bass.ds(4 * i + (4 + 2 * k), 2), :].rearrange("p a t -> p (a t)"),
                          a_hi[:, k, :].bitcast(F32), ALU.subtract).then_inc(a_lo_done, 1)
            for tt in range(TT):
                for n in range(2):
                    ps = wait_full(ve, ("y", 2 * tt + n))
                    dst = xt[:, tt, n * BANK:(n + 1) * BANK]
                    tt_op(dst, dst, ps, ALU.add).then_inc(y_done, 1)

        @block.tensor
        def _(te):
            mm = nc.tensor.matmul

            def open_bank(key):
                b, n = bank[key]
                if n >= 2:
                    te.wait_ge(bank_drained[b], n - 1)
                return psum[:, b, :]

            def full(ins, key):
                ins.then_inc(bank_full[bank[key][0]], 1)

            def product(dst, a_h, a_l, b_h, b_l, start, stop):
                mm(dst, a_h, b_h, start=start, stop=False)
                mm(dst, a_h, b_l, start=False, stop=False)
                return mm(dst, a_l, b_h, start=False, stop=stop)

            def natural_chunk(p, keys, lhs_hi, lhs_lo, half, tt):
                n = panels[p][2]
                if tt == 0:
                    te.wait_ge(split_done, PARTS * (p + 1))
                dst = (open_bank(keys[tt]) if half == 0 else psum[:, bank[keys[tt]][0], :])[:, 0:n]
                tok = slice(tt * P, (tt + 1) * P)
                for k in range(4):
                    cols = slice(k * n, (k + 1) * n)
                    last = product(dst, lhs_hi[4 * half + k][:, tok], lhs_lo[4 * half + k][:, tok],
                                   w_hi[:, p % 2, cols], w_lo[:, p % 2, cols],
                                   start=half == 0 and k == 0, stop=half == 1 and k == 3)
                if half:
                    full(last, keys[tt])
                elif tt == TT - 1:
                    last.then_inc(half_used, 1)

            def transposes(key, blocks):
                dst = open_bank(key)
                for i, src in enumerate(blocks):
                    rows, cols = src.shape
                    last = nc.tensor.transpose(dst[0:cols, i * rows:(i + 1) * rows], src, ident[0:rows, 0:rows])
                full(last, key)

            te.wait_ge(consts, 2)
            te.wait_ge(gains_loaded, 16 * 2)
            transposes("gains", [gain_rows[:, :]])
            hT_k = ([hT_hi[:, k, :] for k in range(KT)], [hT_lo[:, k, :] for k in range(KT)])

            def h_transposes(key, i, tt):
                te.wait_ge(x_scaled, i + 1)
                for hfl in range(2):
                    transposes((key, tt, hfl), [xs[:, tt, (4 * hfl + k) * P:(4 * hfl + k + 1) * P] for k in range(4)])

            def proj(c, half, tts=range(TT)):
                for tt in tts:
                    natural_chunk(2 * c + half, [("proj", c, i) for i in range(TT)], *hT_k, half, tt)

            for what, tt in START:
                if what == "T":
                    h_transposes("hT", tt, tt)
                elif what == "chunk":
                    te.wait_ge(h_lo_done, 2 * tt + 2)
                    proj(C_IDX, 0, (tt,))
            proj(C_IDX, 1)
            te.wait_ge(more_gains_loaded, 16 * 14)
            transposes("more_gains", [more_rows[:, :]])
            proj(C_KV1, 0)
            te.wait_ge(ev["cn"], 1)
            transposes(("T_idx", 0), [p_idx[:, tt, 0:LAT] for tt in range(TT)])
            for i in range(2):
                transposes(("T_idx", 1 + i), [p_idx[:, tt, LAT + i * P:LAT + (i + 1) * P] for tt in range(TT)])
            te.wait_ge(ev["ki_dup"], 1)
            transposes(("T_idx", 3), [ki_dup[:, tt, :, :].rearrange("p r d -> p (r d)") for tt in range(TT)])
            proj(C_KV1, 1)
            proj(C_QB, 0)
            te.wait_ge(small_loaded, 16 * 4)
            wait_drained(te, ("T_idx", 0))
            dst = open_bank(("kv_a", 0))
            for tt in range(TT):
                last = mm(dst[:, tt * P:(tt + 1) * P], cT[:, tt * P:(tt + 1) * P],
                          w_ukv[:, :, :].rearrange("p a d -> p (a d)"), start=True, stop=True)
            full(last, ("kv_a", 0))
            te.wait_ge(ev["cmp_dup"], 4)
            for i in range(4):
                t, g = divmod(i, KH)
                transposes(("cmpT", i), [cmp_dup[:, t, tt, g, :, :].rearrange("p r d -> p (r d)")
                                         for tt in range(TT)])
            te.wait_ge(ev["ks_dup"], 1)
            for g in range(KH):
                transposes(("ksT", g), [ks_dup[:, tt, g, :, :].rearrange("p r d -> p (r d)") for tt in range(TT)])
            for i in range(1, 4):
                wait_drained(te, ("T_idx", i))
            for u, (tt, h) in enumerate(INDEX_UNITS):
                rows = slice(h % 4 * ID, (h % 4 + 1) * ID)
                dst = open_bank(("index", u))
                full(mm(dst[:, 0:(tt + 1) * P], qiT[rows, h // 4, tt * P:(tt + 1) * P], kiT[rows, 0:(tt + 1) * P],
                        start=True, stop=True), ("index", u))
            proj(C_QB, 1)
            proj(C_KV2, 0)
            te.wait_ge(ev["ka_dup"], 1)
            transposes("kaT", [ka_dup[:, tt, :, :].rearrange("p r d -> p (r d)") for tt in range(TT)])
            te.wait_ge(phi1_loaded, 32)
            te.wait_ge(cmp_in_added, 3 * 2 * KH)
            for t in range(2):
                for g in range(KH):
                    wait_drained(te, ("cmpT", KH * t + g))
                dst = open_bank(("hidden", t))
                for j in range(CMP_LEN // 2):
                    v = j // 8
                    src = cmp_in[:, t, v, :, :].rearrange("p g (c j) -> p g c j", j=8)[:, :, v:v + NCMP, j % 8]
                    last = mm(dst[:, 0:KH * NCMP], phi1[t][:, j, :], src, start=j == 0, stop=j == CMP_LEN // 2 - 1)
                full(last, ("hidden", t))
            for tt in range(TT):
                te.wait_ge(qb_scaled, tt + 1)
                transposes(("qbT", tt), [p_q[:, tt, i * P:(i + 1) * P] for i in range(4)])
            proj(C_KV2, 1)

            wait_drained(te, "kaT")
            keysT = {SLC: ksT, WIN: kwT}
            for i in range(KH):
                wait_drained(te, ("ksT", i))
            for kind, *a in script:
                if kind == "qk":
                    s, = a
                    br, tt, h = units[s]
                    w = (tt + 1) * P
                    if h == 0 and br != WIN:
                        wait_drained(te, ("qaT" if br == DSA else "qbT", tt))
                    if s == TT * H:
                        for i in range(KH):
                            wait_drained(te, ("kwT", i))
                    rows = slice(h % 2 * DH, (h % 2 + 1) * DH)
                    q = qaT if br == DSA else qbT
                    k = kaT[rows, 0:w] if br == DSA else keysT[br][rows, h // G, 0:w]
                    full(mm(open_bank(("S", s))[:, 0:w], q[rows, h // 2, tt * P:(tt + 1) * P], k,
                            start=True, stop=True), ("S", s))
                elif kind == "pT":
                    u, = a
                    te.wait_ge(exp_done, u + 1)
                    transposes(("PT", u), [prob[:, u % 3, j * P:(j + 1) * P] for j in range(units[u][1] + 1)])
                elif kind == "pv":
                    u, = a
                    br, tt, h = units[u]
                    if h == 0:
                        open_bank(("O", u // H))
                        if br == SLC:
                            wait_drained(te, ("proj", C_KV2, tt))
                    wait_drained(te, ("PT", u))
                    dst = psum[:, bank[("O", u // H)][0], h * DH:(h + 1) * DH]
                    for j in range(tt + 1):
                        v = {SLC: p_kv2[:, j, h // G * DH:(h // G + 1) * DH],
                             WIN: p_kv2[:, j, 2 * KVW + h // G * DH:2 * KVW + (h // G + 1) * DH],
                             DSA: kv_a[:, j, DH:2 * DH]}[br]
                        last = mm(dst, probT[:, u % 2, j * P:(j + 1) * P], v, start=j == 0, stop=j == tt)
                    if h == H - 1:
                        full(last, ("O", u // H))
                    else:
                        last.then_inc(pv_done, 1)
                elif kind == "kc":
                    te.wait_ge(ev["gelu"], 1)
                    full(mm(open_bank("kc")[0:CP * KH, 0:DH], gel_k[:, :, :].rearrange("p g c -> p (g c)"),
                            phi2[:, 0, :], start=True, stop=True), "kc")
                    dst = open_bank("vc")
                    for i in range(KH):
                        last = mm(dst[:, i * DH:(i + 1) * DH], gel_v[:, i, :, :].rearrange("p r c -> p (r c)"),
                                  phi2[:, 1, :], start=True, stop=True)
                    full(last, "vc")
                elif kind == "kcT":
                    te.wait_ge(ev["kc_dup"], 1)
                    transposes("kcT", [kc_dup[:, :, :].rearrange("p r d -> p (r d)")])
                elif kind == "kwT":
                    te.wait_ge(ev["kw_dup"], 1)
                    transposes(("kwT", a[0]), [kw_dup[:, tt, a[0], :, :].rearrange("p r d -> p (r d)")
                                               for tt in range(TT)])
                elif kind == "qaT":
                    te.wait_ge(qa_scaled, TT + a[0] + 1)
                    transposes(("qaT", a[0]), [p_q[:, a[0], i * P:(i + 1) * P] for i in range(4)])
                elif kind == "cmpS":
                    tt, = a
                    if tt == 0:
                        wait_drained(te, "kcT")
                    for par in range(2):
                        rows = slice(par * DH, (par + 1) * DH)
                        dst = open_bank(("cmpS", tt, par))
                        for hh in range(H // 2):
                            cols = slice((2 * hh + par) // G * CP, (2 * hh + par) // G * CP + CP)
                            last = mm(dst[:, hh * CP:(hh + 1) * CP], qbT[rows, hh, tt * P:(tt + 1) * P],
                                      kcT[rows, cols], start=True, stop=True)
                        full(last, ("cmpS", tt, par))
                elif kind == "cmpPT":
                    tt, = a
                    te.wait_ge(cmp_p, tt + 1)
                    transposes(("cmpPT", tt), [cmp_e[:, tt, i * G:(i + 1) * G, :].rearrange("p h c -> p (h c)")
                                               for i in range(KH)])
                elif kind == "cmpO":
                    tt, = a
                    wait_drained(te, ("cmpPT", tt))
                    wait_drained(te, "vc")
                    dst = open_bank(("cmpO", tt))
                    for i in range(KH):
                        last = mm(dst[:, i * G * DH:(i + 1) * G * DH], cmp_pT[:, i, tt * P:(tt + 1) * P],
                                  vc_diag[:, i, :, :].rearrange("p i d -> p (i d)"), start=True, stop=True)
                    full(last, ("cmpO", tt))
                elif kind == "oT":
                    m, tt = a
                    wait_drained(te, ("O", 2 * TT + tt if m == 0 else TT + tt))
                    transposes(("oT", m, tt), [(o_b if m else o_a)[:, tt, k * P:(k + 1) * P] for k in range(4)])
                elif kind == "tile":
                    t, k = a
                    what, m, i, p, nk, c0 = tiles[t]
                    if what == "up" and i == 0 and k == 0:
                        for tt in range(TT):
                            wait_drained(te, ("oT", m, tt))
                    te.wait_ge(split_done, PARTS * (p + 1))
                    dst = open_bank(("tile", t)) if k == 0 else psum[:, bank[("tile", t)][0], :]
                    n = panels[p][2]
                    if what == "qa":
                        tok = slice(i * P, (i + 1) * P)
                        for kk in (2 * k, 2 * k + 1):
                            cols = slice(kk * n, (kk + 1) * n)
                            last = product(dst[:, 0:n], hT_hi[:, kk, tok], hT_lo[:, kk, tok], w_hi[:, p % 2, cols],
                                           w_lo[:, p % 2, cols], start=kk == 0, stop=kk == KT - 1)
                    else:
                        cols = slice(k * n + c0, k * n + c0 + P)
                        b_hi, b_lo = (hT_hi, hT_lo) if what == "gate" else (oT_hi[m], oT_lo[m])
                        last = product(dst, w_hi[:, p % 2, cols], w_lo[:, p % 2, cols], b_hi[:, k, :],
                                       b_lo[:, k, :], start=k == 0, stop=k == nk - 1)
                    if k == nk - 1:
                        full(last, ("tile", t))
            def out_chunk(n, half, tt):
                natural_chunk(OUT0 + 2 * n + half, [("out", n, i) for i in range(TT)],
                              [mT_hi[:, k, :] for k in range(KT)], [mT[:, :] for mT in mT_lo], half, tt)

            for n, half in ((0, 0), (0, 1), (1, 0)):
                if n == 0:
                    te.wait_ge(m_lo_done, 4 * half + 4)
                for tt in range(TT):
                    out_chunk(n, half, tt)
            for what, tt in RENORM:
                if what == "chunk":
                    out_chunk(1, 1, tt)
                elif what == "T":
                    h_transposes("h2T", TT + tt, tt)
            te.wait_ge(h_lo_done, 4 * TT)
            with te.Fori(0, NFF1 // 4) as i:
                for k4 in range(4):
                    gg, half = divmod(k4, 2)
                    te.wait_ge(split_done, 4 * PARTS * i + PARTS * (FF1 + k4 + 1))
                    for j in range(4):
                        b = 4 * gg + j
                        if half == 0:
                            te.wait_ge(bank_drained[b], i + (ff1_first[b] - 1))
                        for k in range(4):
                            cols = slice(k * BANK + j * P, k * BANK + (j + 1) * P)
                            last = product(psum[:, b, :], w_hi[:, half, cols], w_lo[:, half, cols],
                                           hT_hi[:, 4 * half + k, :], hT_lo[:, 4 * half + k, :],
                                           start=half == 0 and k == 0, stop=half == 1 and k == 3)
                        if half:
                            last.then_inc(bank_full[b], 1)
                    if not half:
                        last.then_inc(half_used, 1)

            def down_panel(slot, start, stop):
                for b in range(8):
                    tt, n = divmod(b, 2)
                    dst = open_bank(("y", b)) if start else psum[:, b, :]
                    for k in range(2):
                        tok = slice(k * S + tt * P, k * S + (tt + 1) * P)
                        cols = slice(k * D + n * BANK, k * D + (n + 1) * BANK)
                        last = product(dst, a_hi[:, slot, tok], a_lo[:, slot, tok], w_hi[:, slot, cols],
                                       w_lo[:, slot, cols], start=start and k == 0, stop=stop and k == 1)
                    if stop:
                        full(last, ("y", b))
                if not stop:
                    last.then_inc(ff2_used, 1)

            for q in range(2):
                te.wait_ge(split_done, PARTS * (FF2 + q + 1))
                te.wait_ge(a_lo_done, q + 1)
                down_panel(q, q == 0, False)
            with te.Fori(1, NFF2 // 2 - 1) as i:
                for k in range(2):
                    te.wait_ge(split_done, 2 * PARTS * i + PARTS * (FF2 + k + 1))
                    te.wait_ge(a_lo_done, 2 * i + (k + 1))
                    down_panel(k, False, False)
            for k in range(2):
                q = NFF2 - 2 + k
                te.wait_ge(split_done, PARTS * (FF2 + q + 1))
                te.wait_ge(a_lo_done, q + 1)
                down_panel(k, False, k == 1)


_INS = ['x', 'g_mix', 'w_in', 'g_q_a', 'g_k_a', 'g_lat_a', 'w_uk_a', 'w_uv_a', 'g_q_b', 'g_kc_b', 'g_ks_b',
        'g_kw_b', 'pe_cmp_b', 'phi_k1_b', 'phi_k2_b', 'phi_v1_b', 'phi_v2_b', 'w_up_a', 'w_up_b', 'w_out', 'g_mlp',
        'w_ff1', 'w_ff2']


def kernel(**inputs):
    import numpy as np
    import concourse.bacc as bacc
    from concourse.bass_utils import run_bass_kernel_spmd

    nc = bacc.Bacc("TRN2", target_bir_lowering=False, num_devices=1)
    arrays, args = {}, []
    for name in _INS:
        a = np.ascontiguousarray(inputs[name])
        arrays[f"in_{name}"] = a
        args.append(nc.dram_tensor(f"in_{name}", a.shape, mybir.dt.from_np(a.dtype), kind="ExternalInput").ap())
    out = nc.dram_tensor("out_x", inputs["x"].shape, mybir.dt.float32, kind="ExternalOutput").ap()
    hybrid_layer(nc, *args, out)
    r = run_bass_kernel_spmd(nc, [arrays], core_ids=[0])
    return r.results[0]["out_x"]
```
